# Optimizing a Trainium2 kernel written in Bass

```python
import math
import jax, jax.numpy as jnp
from jax import lax
import numpy as np

D_MODEL = 1024
BATCH = 1
SEQ = 256
DEPTH = 1
DEC_BATCH = 8
DEC_SEQ = 1
PAST_LEN = 2048
PAGE_SIZE = 128

HEAD_DIM = 64
N_HEADS = D_MODEL // HEAD_DIM
H_SB = N_HEADS // 2
H_DIL = N_HEADS - H_SB
D_SB = H_SB * HEAD_DIM
D_DIL = H_DIL * HEAD_DIM
ROT_DIM = HEAD_DIM // 4
ROPE_THETA = 500000.0
DILATED_PATTERNS = ((128, 1), (512, 4), (2048, 16))
WIN_MAX = max(w for w, _ in DILATED_PATTERNS)
Q_BLOCK = 128
SB_BIAS_INIT = -6.0
PEER_HEADS = 8
PEER_N_KEYS = 128
PEER_N_EXPERTS = PEER_N_KEYS * PEER_N_KEYS
PEER_D_KEY = 256
PEER_TOPK = 16
TOK_BLOCK = 128
NORM_EPS = 1e-6

kernel_name = "hymba_stickbreak_dilated_peer_step"

def rms_norm(x, g):
    xf = x.astype(jnp.float32)
    y = xf * lax.rsqrt(jnp.mean(xf * xf, axis=-1, keepdims=True) + NORM_EPS)
    return (y * g.astype(jnp.float32)).astype(x.dtype)

def adaln(c, w_ada, b_ada):
    m = jax.nn.silu(c) @ w_ada + b_ada
    return [t[:, None, :] for t in jnp.split(m, 6, axis=-1)]

def rotary_partial(x, positions):
    half = ROT_DIM // 2
    inv_freq = ROPE_THETA ** (-jnp.arange(half, dtype=jnp.float32) / half)
    ang = positions.astype(jnp.float32)[:, None] * inv_freq[None, :]
    cos = jnp.cos(ang)[None, :, None, :]
    sin = jnp.sin(ang)[None, :, None, :]
    xr = x[..., :ROT_DIM].astype(jnp.float32)
    x1, x2 = xr[..., :half], xr[..., half:]
    rot = jnp.concatenate([x1 * cos - x2 * sin, x2 * cos + x1 * sin], axis=-1).astype(x.dtype)
    return jnp.concatenate([rot, x[..., ROT_DIM:]], axis=-1)

def project_qkv(h, w_in, positions):
    b, t, _ = h.shape
    proj = h @ w_in
    qa, ka, va, qb, kb, vb = jnp.split(
        proj, [D_SB, 2 * D_SB, 3 * D_SB, 3 * D_SB + D_DIL, 3 * D_SB + 2 * D_DIL], axis=-1)
    sb = [z.reshape(b, t, H_SB, HEAD_DIM) for z in (qa, ka, va)]
    dl = [z.reshape(b, t, H_DIL, HEAD_DIM) for z in (qb, kb, vb)]
    qb_r = rotary_partial(dl[0], positions)
    kb_r = rotary_partial(dl[1], positions)
    return sb[0], sb[1], sb[2], qb_r, kb_r, dl[2]

def stick_breaking(q, k, v, q_idx, bias):
    z = jnp.einsum('bqhd,bkhd->bhqk', q, k).astype(jnp.float32) / math.sqrt(HEAD_DIM)
    z = z + bias.astype(jnp.float32)[None, :, None, None]
    key_idx = jnp.arange(k.shape[1])
    earlier = key_idx[None, :] < q_idx[:, None]
    log_rest = jnp.where(earlier, jax.nn.log_sigmoid(-z), 0.0)
    log_stick = lax.cumsum(log_rest, axis=3, reverse=True) - log_rest
    a = jnp.where(earlier, jnp.exp(jax.nn.log_sigmoid(z) + log_stick), 0.0)
    return jnp.einsum('bhqk,bkhd->bqhd', a.astype(v.dtype), v)

def dilated_attention(q, k_ext, v_ext, q_idx):
    ms, ls, os_ = [], [], []
    for window, dil in DILATED_PATTERNS:
        taps = jnp.arange(window // dil + 1) * dil
        pos = q_idx[:, None] - taps[None, :]
        valid = pos >= 0
        pos = jnp.maximum(pos, 0)
        kg = jnp.take(k_ext, pos, axis=1)
        vg = jnp.take(v_ext, pos, axis=1)
        z = jnp.einsum('bqhd,bqnhd->bhqn', q, kg).astype(jnp.float32) / math.sqrt(HEAD_DIM)
        z = jnp.where(valid[None, None], z, -jnp.inf)
        m = jnp.max(z, axis=-1, keepdims=True)
        p = jnp.exp(z - m)
        l = jnp.sum(p, axis=-1, keepdims=True)
        o = jnp.einsum('bhqn,bqnhd->bhqd', (p / l).astype(v_ext.dtype), vg)
        ms.append(m); ls.append(l); os_.append(o.astype(jnp.float32))
    m_all = jnp.stack(ms)
    l_all = jnp.stack(ls)
    o_all = jnp.stack(os_)
    wgt = l_all * jnp.exp(m_all - jnp.max(m_all, axis=0, keepdims=True))
    out = jnp.sum(wgt * o_all, axis=0) / jnp.sum(wgt, axis=0)
    return out.transpose(0, 2, 1, 3).astype(v_ext.dtype)

def blockwise_queries(fn, q, k, v):
    b, s, h, d = q.shape
    nblk = s // Q_BLOCK
    qb = q.reshape(b, nblk, Q_BLOCK, h, d).transpose(1, 0, 2, 3, 4)
    starts = jnp.arange(nblk) * Q_BLOCK

    def body(args):
        q_blk, t0 = args
        return fn(q_blk, k, v, t0 + jnp.arange(Q_BLOCK))

    out = lax.map(body, (qb, starts))
    return out.transpose(1, 0, 2, 3, 4).reshape(b, s, h, d)

def merge_out(oa, ob, g_sb, g_dil, w_out):
    b, t = oa.shape[:2]
    oa = rms_norm(oa.reshape(b, t, D_SB), g_sb)
    ob = rms_norm(ob.reshape(b, t, D_DIL), g_dil)
    return jnp.concatenate([oa, ob], axis=-1) @ w_out

def peer_ffn(h, w_pq, sub_keys, expert_u, expert_v):
    t = h.shape[0]
    q = (h @ w_pq).reshape(t, PEER_HEADS, 2, PEER_D_KEY // 2)
    s = jnp.einsum('thcd,hcnd->thcn', q, sub_keys).astype(jnp.float32)
    s_top, i_top = lax.top_k(s, PEER_TOPK)
    cand = (s_top[:, :, 0, :, None] + s_top[:, :, 1, None, :]).reshape(t, PEER_HEADS, PEER_TOPK * PEER_TOPK)
    c_top, c_pos = lax.top_k(cand, PEER_TOPK)
    i1 = jnp.take_along_axis(i_top[:, :, 0], c_pos // PEER_TOPK, axis=-1)
    i2 = jnp.take_along_axis(i_top[:, :, 1], c_pos % PEER_TOPK, axis=-1)
    expert = i1 * PEER_N_KEYS + i2
    g = jax.nn.softmax(c_top, axis=-1)
    u = expert_u[expert]
    act = jax.nn.gelu(jnp.einsum('thkd,td->thk', u, h))
    return jnp.einsum('thk,thkd->td', (g * act).astype(h.dtype), expert_v[expert])

def setup_inputs(seed: int = 0) -> dict:
    key = jax.random.key(seed)
    ks = jax.random.split(key, 24)
    n_pages = PAST_LEN // PAGE_SIZE
    n_used = DEC_BATCH * n_pages
    n_phys = n_used + max(1, n_used // 4)
    buf = min(WIN_MAX, PAST_LEN)
    d_in = 3 * D_SB + 3 * D_DIL

    def nrm(k, shape, scale=1.0):
        return scale * jax.random.normal(k, shape, jnp.float32)

    page_table = jax.random.permutation(ks[0], n_phys)[:n_used].reshape(DEC_BATCH, n_pages).astype(jnp.int32)
    return {
        "x_prompt": nrm(ks[1], (BATCH, SEQ, D_MODEL)),
        "x_sample": nrm(ks[2], (DEC_BATCH, DEC_SEQ, D_MODEL)),
        "cache_sb_k": nrm(ks[3], (DEPTH, n_phys, PAGE_SIZE, H_SB, HEAD_DIM)),
        "cache_sb_v": nrm(ks[4], (DEPTH, n_phys, PAGE_SIZE, H_SB, HEAD_DIM)),
        "cache_dil_k": nrm(ks[5], (DEPTH, DEC_BATCH, buf, H_DIL, HEAD_DIM)),
        "cache_dil_v": nrm(ks[6], (DEPTH, DEC_BATCH, buf, H_DIL, HEAD_DIM)),
        "page_table": page_table,
        "c_prompt": nrm(ks[7], (BATCH, D_MODEL)),
        "c_sample": nrm(ks[8], (DEC_BATCH, D_MODEL)),
        "w_ada": nrm(ks[9], (DEPTH, D_MODEL, 6 * D_MODEL), 0.5 * D_MODEL ** -0.5),
        "b_ada": nrm(ks[10], (DEPTH, 6 * D_MODEL), 0.02),
        "norm_mix": 1.0 + nrm(ks[11], (DEPTH, D_MODEL), 0.02),
        "w_in": nrm(ks[12], (DEPTH, D_MODEL, d_in), D_MODEL ** -0.5),
        "sb_bias": SB_BIAS_INIT + nrm(ks[22], (DEPTH, H_SB), 0.1),
        "norm_out_sb": 1.0 + nrm(ks[13], (DEPTH, D_SB), 0.02),
        "norm_out_dil": 1.0 + nrm(ks[14], (DEPTH, D_DIL), 0.02),
        "w_out": nrm(ks[15], (DEPTH, D_MODEL, D_MODEL), D_MODEL ** -0.5),
        "norm_ffn": 1.0 + nrm(ks[16], (DEPTH, D_MODEL), 0.02),
        "w_peer_q": nrm(ks[17], (DEPTH, D_MODEL, PEER_HEADS * PEER_D_KEY), D_MODEL ** -0.5),
        "peer_sub_keys": nrm(ks[18], (DEPTH, PEER_HEADS, 2, PEER_N_KEYS, PEER_D_KEY // 2), (PEER_D_KEY // 2) ** -0.5),
        "peer_u": nrm(ks[19], (DEPTH, PEER_N_EXPERTS, D_MODEL), D_MODEL ** -0.5),
        "peer_v": nrm(ks[20], (DEPTH, PEER_N_EXPERTS, D_MODEL), PEER_HEADS ** -0.5),
        "norm_final": 1.0 + nrm(ks[21], (D_MODEL,), 0.02),
    }

def reference(x_prompt, x_sample, cache_sb_k, cache_sb_v, cache_dil_k, cache_dil_v, page_table,
              c_prompt, c_sample, w_ada, b_ada, norm_mix, w_in, sb_bias, norm_out_sb, norm_out_dil, w_out,
              norm_ffn, w_peer_q, peer_sub_keys, peer_u, peer_v, norm_final):
    n_pages = PAST_LEN // PAGE_SIZE
    buf = cache_dil_k.shape[2]
    keep_p = min(WIN_MAX, SEQ)
    pos_p = jnp.arange(SEQ, dtype=jnp.int32)
    pos_s = PAST_LEN + jnp.arange(DEC_SEQ, dtype=jnp.int32)
    xp, xs = x_prompt, x_sample
    sbk_p, sbv_p, dk_p, dv_p = [], [], [], []
    sbk_s, sbv_s, dk_s, dv_s = [], [], [], []
    for layer in range(DEPTH):
        sh1_p, sc1_p, g1_p, sh2_p, sc2_p, g2_p = adaln(c_prompt, w_ada[layer], b_ada[layer])
        sh1_s, sc1_s, g1_s, sh2_s, sc2_s, g2_s = adaln(c_sample, w_ada[layer], b_ada[layer])
        bias_l = sb_bias[layer]
        sb_fn = lambda q_, k_, v_, idx_: stick_breaking(q_, k_, v_, idx_, bias_l)

        hp = rms_norm(xp, norm_mix[layer]) * (1.0 + sc1_p) + sh1_p
        qa, ka, va, qb, kb, vb = project_qkv(hp, w_in[layer], pos_p)
        oa = blockwise_queries(sb_fn, qa, ka, va)
        ob = blockwise_queries(dilated_attention, qb, kb, vb)
        xp = xp + g1_p * merge_out(oa, ob, norm_out_sb[layer], norm_out_dil[layer], w_out[layer])
        sbk_p.append(ka); sbv_p.append(va)
        dk_p.append(kb[:, SEQ - keep_p:]); dv_p.append(vb[:, SEQ - keep_p:])

        hs = rms_norm(xs, norm_mix[layer]) * (1.0 + sc1_s) + sh1_s
        qa_s, ka_s, va_s, qb_s, kb_s, vb_s = project_qkv(hs, w_in[layer], pos_s)
        past_k = cache_sb_k[layer][page_table].reshape(DEC_BATCH, n_pages * PAGE_SIZE, H_SB, HEAD_DIM)
        past_v = cache_sb_v[layer][page_table].reshape(DEC_BATCH, n_pages * PAGE_SIZE, H_SB, HEAD_DIM)
        k_all = jnp.concatenate([past_k, ka_s], axis=1)
        v_all = jnp.concatenate([past_v, va_s], axis=1)
        oa_s = stick_breaking(qa_s, k_all, v_all, pos_s, bias_l)
        ext_k = jnp.concatenate([cache_dil_k[layer], kb_s], axis=1)
        ext_v = jnp.concatenate([cache_dil_v[layer], vb_s], axis=1)
        ob_s = dilated_attention(qb_s, ext_k, ext_v, buf + jnp.arange(DEC_SEQ))
        xs = xs + g1_s * merge_out(oa_s, ob_s, norm_out_sb[layer], norm_out_dil[layer], w_out[layer])
        sbk_s.append(ka_s); sbv_s.append(va_s)
        dk_s.append(ext_k[:, DEC_SEQ:]); dv_s.append(ext_v[:, DEC_SEQ:])

        hp2 = rms_norm(xp, norm_ffn[layer]) * (1.0 + sc2_p) + sh2_p
        hp2_blocks = hp2.reshape(BATCH * SEQ // TOK_BLOCK, TOK_BLOCK, D_MODEL)
        fp = lax.map(lambda hb: peer_ffn(hb, w_peer_q[layer], peer_sub_keys[layer], peer_u[layer], peer_v[layer]), hp2_blocks)
        xp = xp + g2_p * fp.reshape(BATCH, SEQ, D_MODEL)
        hs2 = rms_norm(xs, norm_ffn[layer]) * (1.0 + sc2_s) + sh2_s
        fs = peer_ffn(hs2.reshape(DEC_BATCH * DEC_SEQ, D_MODEL), w_peer_q[layer], peer_sub_keys[layer], peer_u[layer], peer_v[layer])
        xs = xs + g2_s * fs.reshape(DEC_BATCH, DEC_SEQ, D_MODEL)

    y_prompt = rms_norm(xp, norm_final)
    y_sample = rms_norm(xs, norm_final)
    return (y_prompt, y_sample,
            jnp.stack(sbk_p), jnp.stack(sbv_p), jnp.stack(dk_p), jnp.stack(dv_p),
            jnp.stack(sbk_s), jnp.stack(sbv_s), jnp.stack(dk_s), jnp.stack(dv_s))


_drawn_inputs = setup_inputs


def setup_inputs(seed=0):
    import zlib

    import numpy as np

    out = dict(_drawn_inputs(seed))
    spreads = {}
    factors = {'norm_mix': 2.949,
     'norm_out_sb': 8.0,
     'norm_out_dil': 8.0,
     'norm_ffn': 7.263,
     'norm_final': 2.753}
    for name, (base, spread) in spreads.items():
        noise = np.random.default_rng([zlib.crc32(name.encode()), seed]).standard_normal(out[name].shape)
        drawn = base * np.exp(spread * noise) if base else spread * noise
        out[name] = __import__('jax').numpy.asarray(drawn.astype(out[name].dtype))
    for name, factor in factors.items():
        out[name] = (out[name] * factor).astype(out[name].dtype)
    return out
```

```python
from contextlib import ExitStack

import numpy as np

import concourse.bass as bass
from concourse import mybir

F32 = mybir.dt.float32
I32 = mybir.dt.int32
U32 = mybir.dt.uint32
ALU = mybir.AluOpType
ACT = mybir.ActivationFunctionType
AX = mybir.AxisListType.X

P = 128
D = 1024
KC = D // P
SEQ = 256
NB = 8
NTOK = SEQ + NB
HD = 64
NH = 8
DG = NH * HD
NPG = 16
PAST = NPG * P
WC = 256
WSLOTS = 4
ADA_CH, QKV_CH, OUT_CH, PQ_CH = 6 * D // WC, 6 * DG // WC, D // WC, 2 * D // WC
QA, KA, VA, QB_, KB_, VB_ = (DG * n for n in range(6))
KVP = 2
KVS = 4
CPB = NPG // KVP
TOPK = 16
NKEY = 128
NSLOT = 8
DIL_ROWS = 96
EPS = 1e-6
SCALE = HD ** -0.5
LOWEST = -3.0e38
MASKED = -1.0e30

_CONST = {}
_at = 0
for _name, _n in (("ident", P), ("tri", P), ("ones", P), ("later", P), ("cnt", 384), ("dbias", 384),
                  ("scnt", 384), ("sbias", 384), ("rope", 48), ("hmask", DG), ("unit8", 64), ("iota", TOPK)):
    _CONST[_name] = (_at, _n)
    _at += _n
NCONST = _at


def constants():
    c = np.zeros((P, NCONST), np.float32)

    def put(name, a):
        at, n = _CONST[name]
        c[:a.shape[0], at:at + n] = a.reshape(a.shape[0], n)

    p, f = np.arange(P)[:, None], np.arange(P)[None, :]
    put("ident", (p == f).astype(np.float32))
    put("tri", (p >= f).astype(np.float32))
    put("ones", np.ones((P, P), np.float32))
    put("later", (p < f).astype(np.float32))

    def count(d):
        d = np.asarray(d)
        return sum(((d >= 0) & (d <= w) & (d % s == 0)).astype(np.float32) for w, s in ((128, 1), (512, 4), (2048, 16)))

    cnt = np.concatenate([count(p - f), count(P + p - f), count(p - f)], 1)
    put("cnt", cnt)
    put("dbias", np.where(cnt > 0, 0.0, MASKED).astype(np.float32))
    far = np.full(P, -1)
    mid, long = far.copy(), far.copy()
    mid[:DIL_ROWS] = 512 - 4 * np.arange(DIL_ROWS)
    mid[DIL_ROWS] = 0
    long[:DIL_ROWS] = 2048 - 16 * np.arange(DIL_ROWS)
    scnt = np.tile(count(np.concatenate([P - np.arange(P), mid, long])), (NB * NH, 1))
    put("scnt", scnt)
    put("sbias", np.where(scnt > 0, 0.0, MASKED).astype(np.float32))
    inv = np.float32(500000.0) ** (-np.arange(8, dtype=np.float32) / np.float32(8))
    pos = np.concatenate([np.arange(SEQ), np.full(P, PAST)]).astype(np.float32)
    ang = (pos[:, None] * inv[None, :]).astype(np.float32)
    rope = np.concatenate([np.cos(ang), np.sin(ang)], 1).reshape(3, P, 16).transpose(1, 0, 2)
    put("rope", np.ascontiguousarray(rope).astype(np.float32))
    put("hmask", (np.arange(NH)[:, None] == (np.arange(DG) // HD)[None, :]).astype(np.float32))
    put("unit8", np.tile(np.eye(8, dtype=np.float32).reshape(1, 64), (P, 1)))
    put("iota", np.tile(np.arange(TOPK, dtype=np.float32), (P, 1)))
    return c


class Count:

    def __init__(self, sem, base=0):
        self.sem, self.base, self.n = sem, base, 0

    def inc(self, instruction):
        instruction.then_inc(self.sem, 1)
        self.n += 1

    def value(self):
        return self.base + self.n

    def wait(self, eng):
        eng.wait_ge(self.sem, self.value())


def build(nc, A):
    ctx = ExitStack()
    with ctx:
        def sb(name, shape, dt=F32):
            return ctx.enter_context(nc.sbuf_tensor(name, shape, dt))

        def sem(name):
            return ctx.enter_context(nc.semaphore(name))

        const = sb("const", [P, NCONST])

        def cst(name):
            at, n = _CONST[name]
            return const[:, at:at + n]

        ident, tri, ones, later = cst("ident"), cst("tri"), cst("ones"), cst("later")
        m_rows = sb("m_rows", [9, 4, D])
        m_all = sb("m_all", [P, 4, D])
        x = sb("x", [P, 3, D])
        H = sb("H", [P, 3, D])
        HT = sb("HT", [P, KC * NTOK])
        QKV = sb("QKV", [P, 3, 6 * DG])
        R = sb("R", [P, NSLOT, 2 * D])
        Z = sb("Z", [P, 3, NPG * NB * NH])
        nffn = sb("nffn", [9, D])
        b24 = sb("b24", [ADA_CH, WC])
        zd = sb("zd", [P, 3, NB * NH])
        zrow = sb("zrow", [NB * NH, 384])
        pd = sb("pd", [P, 3, NB * NH])
        cT = sb("cT", [P, KC, 9])
        bsel = sb("bsel", [ADA_CH, 2, 9])
        sbb = sb("sbb", [P, NH])
        gcol = sb("gcol", [P, KC])
        pages = sb("pages", [1, NB * NPG], I32)
        stat = sb("stat", [P, 32])
        ast = sb("ast", [P, 2, NPG, NH])
        selst = sb("selst", [NH, 2, NB])
        msk = sb("msk", [NH, DG])
        gall = sb("gall", [P, 24, TOPK])
        idxf = sb("idxf", [P, 24, TOPK])
        idx = sb("idx", [P, 24, TOPK], I32)
        idst = sb("idst", [P, 2, TOPK], I32)
        gst = sb("gst", [P, TOPK])
        dots = sb("dots", [P, TOPK])
        gel = sb("gel", [P, TOPK])
        wgt = sb("wgt", [P, TOPK])
        diag = sb("diag", [P, 4, P])

        hT = HT[:, :].rearrange("p (c n) -> p c n", c=KC)
        Rf = R[:, :, :].rearrange("p s n -> p (s n)")
        W = [R[:, s, :].rearrange("p (c n) -> p c n", c=KC) for s in range(WSLOTS)]
        KV = [Rf[:, WSLOTS * 2048 + s * 1024:WSLOTS * 2048 + (s + 1) * 1024].rearrange("p (g n) -> p g n", g=KVP)
              for s in range(KVS)]
        DK = [R[:, WSLOTS + s, 0:3 * DG].rearrange("p (g n) -> p g n", g=3) for s in range(2)]
        subk = R[:, WSLOTS, :].rearrange("p (g n) -> p g n", g=16)
        QB = Rf[:, 6 * 2048:8 * 2048].rearrange("p (b n) -> p b n", b=NB)
        z4 = Z[:, 0, :].rearrange("p (g b h) -> p g b h", g=NPG, b=NB)
        z1, zt, zl = Z[:, 0, :], Z[:, 1, :], Z[:, 2, :]
        cwork = [Z[0:9, n, :] for n in range(3)]
        Hf = H[:, :, :].rearrange("p t n -> p (t n)")
        aw = [Hf[:, n * 768:(n + 1) * 768].rearrange("p (j n) -> p j n", j=2) for n in range(3)]
        stq = Hf[:, 2304:2560].rearrange("p (t n) -> p t n", t=2)
        stk = Hf[:, 2560:2816].rearrange("p (t n) -> p t n", t=2)
        qk = HT[:, 0:512]
        pT = HT[:, 512:1280].rearrange("p (j n) -> p j n", j=2)
        Qf = QKV[:, :, :].rearrange("p t n -> p (t n)")
        S = Qf[:, 0:24 * 2 * NKEY].rearrange("p (i c n) -> p i c n", i=24, c=2)
        tw = Qf[:, 6144:9216]

        eq = Z[:, 0, 0:2 * 512].rearrange("p (j n) -> p j n", j=2)
        sc, rep, cand, crep, oh, oh2 = (tw[:, n * 256:(n + 1) * 256] for n in range(6))
        tsm = tw[:, 1536:2048]
        tv = [tsm[:, 0:16], tsm[:, 16:32]]
        tif = [tsm[:, 32:48], tsm[:, 48:64]]
        cv, ctop_d, ctop_e = tsm[:, 64:80], tsm[:, 80:96], tsm[:, 96:112]
        posf, row_f, col_f, e1f, e2f = (tsm[:, 112 + 16 * n:128 + 16 * n] for n in range(5))
        tst = tsm[:, 200:204]
        tiu = [sb("tiu0", [P, TOPK], U32), sb("tiu1", [P, TOPK], U32)]
        ciu = sb("ciu", [P, TOPK], U32)
        cint = sb("cint", [P, 2, TOPK], U32)

        ps = ctx.enter_context(nc.psum_tensor("ps", [P, 8, 512], F32))

        names = """c_in x_in small_in w_used sel_ready ada_mm ada_ev bc_mm bc_ev cs_ready cT_mm cT_ev m1_ready
          h_ssq h_rt h_ready hT_mm hT_ev qkv_ev qb_mm qb_ev k_used rot_done new_out kv_out z_l z_abs z_suf
          z_s z_e zz_a dk_used qd_mm qd_ev dT_mm dm_ready de_ready dp_ready dU_mm pd_ev st_ready t_mm t_ev
          sc_mm s_l s_t s_L s_mm s_a s_e s_am o_mm o_ev d_zm d_e d_p d_tr d_pT d_o d_oe ast_ready v_used
          msk_ready oA_mm vd_used pdst_ready mskd_ready oB_mm mg_ready mg_mm mg_ev out_ev m2_ready bc2_mm
          bc2_ev pq_mm pq_ev score_mm score_ev top_done id_st g_st dot_done gel_done w_done diag_done
          e_used ff_ready f_rt y_ready y_out sidx_mm sidx_ready hb_mm sdot sgel swd sacc copied dve act
          kst dst sbs dis tks subk_in z_v topsm tope fin_in""".split()
        s = {n: sem(n) for n in names}
        w_ready = [sem(f"w_ready{n}") for n in range(WSLOTS)]
        k_ready = [sem(f"k_ready{n}") for n in range(KVS)]
        v_ready = [sem(f"v_ready{n}") for n in range(KVS)]
        dk_ready = [sem(f"dk_ready{n}") for n in range(2)]
        dv_ready = [sem(f"dv_ready{n}") for n in range(2)]
        e_ready = [sem(f"e_ready{n}") for n in range(NSLOT)]

        TP = [P, P, NB]
        DILS = ((0, P, bass.ds(PAST - P, P)), (1, DIL_ROWS, bass.ds(PAST - 512, DIL_ROWS, step=4)),
                (2, DIL_ROWS, bass.ds(0, DIL_ROWS, step=16)))

        block = ctx.enter_context(nc.Block())

        wait_value = {eng: eng.alloc_register("wait_value") for eng in (nc.vector, nc.tensor, nc.gpsimd)}

        def wait_apart(eng, semaphore, value):
            if not isinstance(value, int):
                eng.reg_mov(wait_value[eng], value)
                value = wait_value[eng]
            eng.wait_ge(s["c_in"], 64)
            eng.wait_ge(semaphore, value)

        @block.sync
        def _(sp):
            sp.dma_start(const[:, :], A["consts"]).then_inc(s["c_in"], 16)
            sp.dma_start(cwork[0], A["c9"]).then_inc(s["c_in"], 16)
            sp.dma_start(cwork[2], A["norm_mix"].to_broadcast([9, D])).then_inc(s["c_in"], 16)
            sp.dma_start(b24[:, :], A["b_ada"]).then_inc(s["c_in"], 16)
            for t in range(3):
                sp.dma_start(x[0:TP[t], t, :], A["x"][t * P:t * P + TP[t], :]).then_inc(s["x_in"], 16)
            sp.dma_start(nffn[:, :], A["norm_ffn"].to_broadcast([9, D])).then_inc(s["small_in"], 16)
            sp.dma_start(sbb[:, :], A["sb_bias"].to_broadcast([P, NH])).then_inc(s["small_in"], 16)
            sp.dma_start(gcol[:, :], A["g_out"]).then_inc(s["small_in"], 16)
            sp.dma_start(pages[:, :], A["pages"]).then_inc(s["small_in"], 16)
            sp.wait_ge(s["small_in"], 64)

            def page_chunk(b, c, cache, ready, waits):
                for sm, v in waits:
                    sp.wait_ge(sm, v)
                for g in range(KVP):
                    page = sp.value_load(pages[0:1, bass.ds(b * NPG + c * KVP + g, 1)], min_val=0, max_val=159)
                    sp.dma_start(KV[c % KVS][:, g, :],
                                 cache[bass.ds(page, 1)].rearrange("a p n -> (a p) n")).then_inc(ready[c % KVS], 16)

            def copy_window(b):
                for src, dst in ((A["dil_k"], A["dil_k_s"]), (A["dil_v"], A["dil_v_s"])):
                    n = (PAST - 1) * DG // 4
                    for q in range(4):
                        sp.dma_start(dst[bass.ds(b, 1), bass.ds(q * n, n)].rearrange("a (r n) -> (a r) n", r=P),
                                     src[bass.ds(b, 1), bass.ds(DG + q * n, n)].rearrange("a (r n) -> (a r) n", r=P)
                                     ).then_inc(s["copied"], 16)

            for c in range(CPB):
                page_chunk(0, c, A["sb_k"], k_ready, [(s["k_used"], c - KVS + 1)] if c >= KVS else [])
            with sp.Fori(1, NB) as b:
                for c in range(CPB):
                    page_chunk(b, c, A["sb_k"], k_ready, [(s["k_used"], b * CPB + (c - KVS + 1))])

            sp.wait_ge(s["rot_done"], 1)
            sp.dma_start(A["dil_k_s"][:, (PAST - 1) * DG:], QKV[0:NB, 2, KB_:KB_ + DG]).then_inc(s["new_out"], 16)
            sp.dma_start(A["dil_v_s"][:, (PAST - 1) * DG:], QKV[0:NB, 2, VB_:VB_ + DG]).then_inc(s["new_out"], 16)
            for name, col in (("sb_k", KA), ("sb_v", VA), ("dil_k", KB_), ("dil_v", VB_)):
                for t in range(2):
                    sp.dma_start(A[name + "_p"][t * P:(t + 1) * P, :], QKV[:, t, col:col + DG]).then_inc(s["kv_out"], 16)
            for name, col in (("sb_k_n", KA), ("sb_v_n", VA)):
                sp.dma_start(A[name], QKV[0:NB, 2, col:col + DG]).then_inc(s["kv_out"], 16)
            sp.wait_ge(s["new_out"], 32)
            sp.wait_ge(s["k_used"], NB * CPB)

            def window_keys(b, slot, src, new, ready, waits):
                for sm, v in waits:
                    sp.wait_ge(sm, v)
                rows = src[bass.ds(b, 1), :].rearrange("a (r n) -> (a r) n", n=DG)
                for g, n, sel in DILS:
                    sp.dma_start(DK[slot][0:n, g, :], rows[sel, :]).then_inc(ready[slot], 16)
                sp.dma_start(DK[slot][DIL_ROWS:DIL_ROWS + 1, 1, :],
                             new[bass.ds(b, 1), (PAST - 1) * DG:]).then_inc(ready[slot], 16)

            for b in range(2):
                window_keys(b, b, A["dil_k"], A["dil_k_s"], dk_ready, [])
            with sp.Fori(1, NB // 2) as i:
                for j in range(2):
                    window_keys(i * 2 + j, j, A["dil_k"], A["dil_k_s"], dk_ready, [(s["dk_used"], i * 2 + (j - 1))])
            with sp.Fori(0, NB // 2) as i:
                copy_window(i)

            sp.wait_ge(s["dk_used"], NB)
            for c in range(CPB):
                page_chunk(0, c, A["sb_v"], v_ready, [(s["v_used"], c - KVS + 1)] if c >= KVS else [])
            with sp.Fori(1, NB) as b:
                for c in range(CPB):
                    page_chunk(b, c, A["sb_v"], v_ready, [(s["v_used"], b * CPB + (c - KVS + 1))])
            sp.wait_ge(s["v_used"], NB * CPB)
            for b in range(2):
                window_keys(b, b, A["dil_v"], A["dil_v_s"], dv_ready, [])
            with sp.Fori(1, NB // 2) as i:
                for j in range(2):
                    window_keys(i * 2 + j, j, A["dil_v"], A["dil_v_s"], dv_ready, [(s["vd_used"], i * 2 + (j - 1))])
            with sp.Fori(NB // 2, NB) as i:
                copy_window(i)
            sp.wait_ge(s["vd_used"], NB)
            sp.dma_start(subk, A["subk"].rearrange("p (g n) -> p g n", g=16)).then_inc(s["subk_in"], 16)
            sp.wait_ge(s["h_ready"], 6)
            sp.dma_start(m_all[:, 3, :], A["norm_final"].to_broadcast([P, D])).then_inc(s["fin_in"], 16)
            for n, (t, dst) in enumerate(((0, A["y_p"][0:P, :]), (1, A["y_p"][P:SEQ, :]), (2, A["y_s"]))):
                sp.wait_ge(s["y_ready"], n + 1)
                sp.dma_start(dst, H[0:TP[t], t, :]).then_inc(s["y_out"], 16)
            sp.wait_ge(s["kv_out"], 16 * 10)
            sp.wait_ge(s["copied"], 16 * 8 * NB)
            sp.wait_ge(s["y_out"], 48)

        @block.gpsimd
        def _(pool):
            rounds = (ADA_CH + QKV_CH + OUT_CH + PQ_CH) // WSLOTS
            for k in range(WSLOTS):
                pool.dma_start(R[:, k, :], A["wts"][k]).then_inc(w_ready[k], 16)
            with pool.Fori(1, rounds) as r:
                for k in range(WSLOTS):
                    pool.wait_ge(s["w_used"], r * WSLOTS + (k - WSLOTS + 1))
                    pool.dma_start(R[:, k, :], A["wts"][bass.ds(r * WSLOTS + k, 1)].rearrange("a p n -> (a p) n")
                                   ).then_inc(w_ready[k], 16)

            def head_rows(i, par, first):
                pool.wait_ge(s["top_done"], i + 1)
                pool.tensor_copy(idst[:, par, :], idx[:, bass.ds(i, 1), :].rearrange("p a n -> p (a n)")
                                 ).then_inc(s["id_st"], 1)
                wait_apart(pool, s["id_st"], i + 1)
                for k in range(TOPK):
                    if not (first and k < NSLOT):
                        wait_apart(pool, s["e_used"], i * TOPK + (k - NSLOT + 1))
                    pool.indirect_dma_start(
                        out=R[:, k % NSLOT, :], out_offset=None, in_=A["uv"],
                        in_offset=bass.IndirectOffsetOnAxis(ap=idst[:, par, k:k + 1], axis=0),
                    ).then_inc(e_ready[k % NSLOT], 16)

            head_rows(0, 0, True)
            head_rows(1, 1, False)
            with pool.Fori(1, NH) as i:
                head_rows(i * 2, 0, False)
                head_rows(i * 2 + 1, 1, False)
            pool.wait_ge(s["sidx_ready"], 1)
            for b in range(NB):
                pool.wait_ge(s["e_used"], 2 * NH * TOPK - NSLOT + b + 1)
                pool.indirect_dma_start(
                    out=R[:, b, :], out_offset=None, in_=A["uv"],
                    in_offset=bass.IndirectOffsetOnAxis(ap=idx[:, 0, b:b + 1], axis=0),
                ).then_inc(e_ready[b], 16)

        @block.tensor
        def _(pe):
            def w_round(r, k):
                pe.wait_ge(w_ready[k], r * 16 + 16)

            pe.wait_ge(s["c_in"], 64)
            pe.wait_ge(s["cs_ready"], 1)
            for c in range(KC):
                last = pe.transpose(ps[:, 7, c * 9:(c + 1) * 9], cwork[0][:, c * P:(c + 1) * P], ident[0:9, 0:9])
            last.then_inc(s["cT_mm"], 1)
            pe.wait_ge(s["cT_ev"], 1)

            def ada(first, sel, n):
                with pe.Fori(0, n) as r:
                    for k in range(WSLOTS):
                        w_round(r + first, k)
                        pe.wait_ge(s["sel_ready"], (r + sel) * WSLOTS + (k + 1))
                        out = ps[0:9, k % 2, 0:WC]
                        for c in range(KC):
                            last = pe.matmul(out, cT[:, c, :], W[k][:, c, :], start=(c == 0), stop=False)
                        last.then_inc(s["w_used"], 1)
                        pe.matmul(out, bsel[:, k % 2, :], b24[:, :], start=False, stop=True).then_inc(s["ada_mm"], 1)

            def spread_rows(order, ready, value, mm, ev):
                pe.wait_ge(ready, value)
                n = 0
                for slot in order:
                    for h in range(2):
                        if n >= 4:
                            pe.wait_ge(ev, n - 3)
                        pe.matmul(ps[:, 4 + n % 4, :], ident[0:9, 8:9].to_broadcast([9, P]),
                                  m_rows[:, slot, h * 512:(h + 1) * 512], start=True, stop=True).then_inc(mm, 1)
                        n += 1

            def turn(n0, ready, mm, ev):
                for t in range(3):
                    pe.wait_ge(ready, n0 + t + 1)
                    if t < 2:
                        for half in range(2):
                            for c in range(4):
                                last = pe.transpose(ps[:, 2 * t + half, c * P:(c + 1) * P],
                                                    H[:, t, (4 * half + c) * P:(4 * half + c + 1) * P], ident)
                            last.then_inc(mm, 1)
                    else:
                        for c in range(KC):
                            last = pe.transpose(ps[:, 4, c * NB:(c + 1) * NB], H[0:NB, t, c * P:(c + 1) * P],
                                                ident[0:NB, 0:NB])
                        last.then_inc(mm, 1)

            def project(base, r, k, ev, wait_ev):
                w_round(base // WSLOTS + r, k)
                if wait_ev is not None:
                    pe.wait_ge(ev, wait_ev)
                for t in range(3):
                    out = ps[0:TP[t], 2 * (k % 2) + t // 2, (t % 2) * WC:(t % 2 + 1) * WC]
                    for c in range(KC):
                        last = pe.matmul(out, hT[:, c, t * P:t * P + TP[t]], W[k][:, c, :],
                                         start=(c == 0), stop=(c == KC - 1))
                    if t == 2:
                        last.then_inc(s["w_used"], 1)

            ada(0, 0, 2)
            spread_rows((0, 1), s["m1_ready"], 1, s["bc_mm"], s["bc_ev"])
            turn(0, s["h_ready"], s["hT_mm"], s["hT_ev"])
            pe.wait_ge(s["hT_ev"], 5)
            base = 8
            for k in range(WSLOTS):
                project(base, 0, k, s["qkv_ev"], k - 1 if k >= 2 else None)
            pe.wait_ge(s["qkv_ev"], 4)
            for b in range(NB):
                if b >= 4:
                    pe.wait_ge(s["qb_ev"], b - 3)
                pe.matmul(ps[:, 4 + b % 4, :], ident[0:NB, b:b + 1].to_broadcast([NB, P]), QKV[0:NB, 2, QA:QA + DG],
                          start=True, stop=True).then_inc(s["qb_mm"], 1)
            with pe.Fori(1, QKV_CH // WSLOTS) as r:
                for k in range(WSLOTS):
                    project(base, r, k, s["qkv_ev"], r * WSLOTS + (k - 1))
            pe.wait_ge(s["qkv_ev"], QKV_CH)
            ada(5, 2, 4)

            pe.wait_ge(s["qb_ev"], NB)
            pe.wait_ge(s["z_suf"], 1)
            for half in range(2):
                c = slice(half * 512, (half + 1) * 512)
                pe.matmul(ps[:, 4 + half, :], tri, zl[:, c], start=True, stop=False)
                last = pe.matmul(ps[:, 4 + half, :], ones, zt[:, c], start=False, stop=True)
            last.then_inc(s["z_s"], 1)

            pe.wait_ge(s["zz_a"], 1)
            pe.wait_ge(s["rot_done"], 1)
            for b in range(NB):
                if b >= 4:
                    pe.wait_ge(s["qd_ev"], b - 3)
                pe.matmul(ps[:, 4 + b % 4, :], ident[0:NB, b:b + 1].to_broadcast([NB, P]), QKV[0:NB, 2, QB_:QB_ + DG],
                          start=True, stop=True).then_inc(s["qd_mm"], 1)
            pe.wait_ge(s["qd_ev"], NB)
            pe.wait_ge(s["dk_used"], NB)
            for g in range(3):
                last = pe.transpose(ps[0:64, 6, g * P:(g + 1) * P], zd[:, g, :], ident)
            last.then_inc(s["dT_mm"], 1)
            pe.wait_ge(s["dp_ready"], 1)
            for g in range(3):
                last = pe.transpose(ps[:, 7, g * 64:(g + 1) * 64], zrow[:, g * P:(g + 1) * P], ident[0:64, 0:64])
            last.then_inc(s["dU_mm"], 1)
            pe.wait_ge(s["pd_ev"], 1)

            def turn_pair(i):
                pe.wait_ge(s["st_ready"], i + 1)
                for n, st in enumerate((stq, stk)):
                    for t in range(2):
                        last = pe.transpose(ps[:, 0, (2 * n + t) * P:(2 * n + t + 1) * P], st[:, t, :], ident)
                last.then_inc(s["t_mm"], 1)
                pe.wait_ge(s["t_ev"], i + 1)

            with pe.Fori(0, NH // 2) as g:
                turn_pair(g)
                for j in range(2):
                    f = slice(64 * j, 64 * j + 64)
                    pe.matmul(ps[:, 1 + j, 0:256], qk[f, 256:384], qk[f, 0:256], start=True, stop=True)
                    last = pe.matmul(ps[:, 1 + j, 256:384], qk[f, 384:512], qk[f, 128:256], start=True, stop=True)
                last.then_inc(s["sc_mm"], 1)
                pe.wait_ge(s["s_L"], g + 1)
                for j in range(2):
                    L = aw[1][:, j, :]
                    pe.matmul(ps[:, 3 + j, 0:128], tri, L[:, 0:128], start=True, stop=True)
                    pe.matmul(ps[:, 3 + j, 128:256], tri, L[:, 128:256], start=True, stop=False)
                    pe.matmul(ps[:, 3 + j, 128:256], ones, L[:, 256:384], start=False, stop=True)
                    last = pe.matmul(ps[:, 3 + j, 256:384], tri, L[:, 256:384], start=True, stop=True)
                last.then_inc(s["s_mm"], 1)
                pe.wait_ge(s["s_am"], g + 1)
                for j in range(2):
                    o0, o1 = ps[:, 5, j * HD:(j + 1) * HD], ps[:, 5, P + j * HD:P + (j + 1) * HD]
                    v = [QKV[:, t, bass.ds(VA + j * HD + g * P, HD)] for t in range(2)]
                    pe.matmul(o0, aw[2][:, j, 0:128], v[0], start=True, stop=True)
                    pe.matmul(o1, aw[2][:, j, 128:256], v[0], start=True, stop=False)
                    last = pe.matmul(o1, aw[2][:, j, 256:384], v[1], start=False, stop=True)
                last.then_inc(s["o_mm"], 1)
                pe.wait_ge(s["o_ev"], g + 1)

            with pe.Fori(0, NH // 2) as g:
                turn_pair(g + 4)
                for j in range(2):
                    f = slice(64 * j, 64 * j + 64)
                    pe.matmul(ps[:, 1 + j, 0:128], qk[f, 0:128], qk[f, 256:384], start=True, stop=True)
                    last = pe.matmul(ps[:, 1 + j, 128:384], qk[f, 128:256], qk[f, 256:512], start=True, stop=True)
                last.then_inc(s["sc_mm"], 1)
                pe.wait_ge(s["d_p"], g + 1)
                for j in range(2):
                    for n in range(3):
                        last = pe.transpose(ps[:, 1 + j, n * P:(n + 1) * P], aw[0][:, j, n * P:(n + 1) * P], ident)
                last.then_inc(s["d_tr"], 1)
                pe.wait_ge(s["d_pT"], g + 1)
                for j in range(2):
                    o0, o1 = ps[:, 5, j * HD:(j + 1) * HD], ps[:, 5, P + j * HD:P + (j + 1) * HD]
                    v = [QKV[:, t, bass.ds(VB_ + j * HD + g * P, HD)] for t in range(2)]
                    pe.matmul(o0, pT[:, j, 0:128], v[0], start=True, stop=True)
                    pe.matmul(o1, pT[:, j, 128:256], v[0], start=True, stop=False)
                    last = pe.matmul(o1, pT[:, j, 256:384], v[1], start=False, stop=True)
                last.then_inc(s["d_o"], 1)
                pe.wait_ge(s["d_oe"], g + 1)

            def add_row(bank, sel, first):
                return pe.matmul(ps[0:NB, bank, :], sel, msk[:, :], start=first, stop=True, skip_group_check=True)

            def pages_pv(i, j, first):
                pe.wait_ge(s["ast_ready"], i + 1)
                for c in range(CPB):
                    pe.wait_ge(v_ready[c % KVS], (i * 2 + (c // KVS + 1)) * 32)
                    for g in range(KVP):
                        last = pe.matmul(ps[0:NH, 6 + j, :], ast[:, j, c * KVP + g, :], KV[c % KVS][:, g, :],
                                         start=(c + g == 0), stop=(c * KVP + g == NPG - 1))
                    last.then_inc(s["v_used"], 1)
                wait_apart(pe, s["msk_ready"], i + 1)
                add_row(3, selst[:, j, :], first).then_inc(s["oA_mm"], 1)

            pages_pv(0, 0, True)
            pages_pv(1, 1, False)
            with pe.Fori(1, NB // 2) as i:
                pages_pv(i * 2, 0, False)
                pages_pv(i * 2 + 1, 1, False)

            def window_pv(i, j, first, value):
                pe.wait_ge(s["pdst_ready"], i + 1)
                pe.wait_ge(dv_ready[j], value)
                for g, n in ((0, P), (1, DIL_ROWS + 1), (2, DIL_ROWS)):
                    last = pe.matmul(ps[0:NH, 6 + j, :], ast[0:n, j, g, :], DK[j][0:n, g, :],
                                     start=(g == 0), stop=(g == 2))
                last.then_inc(s["vd_used"], 1)
                wait_apart(pe, s["mskd_ready"], i + 1)
                add_row(4, selst[:, j, :], first).then_inc(s["oB_mm"], 1)

            window_pv(0, 0, True, 64)
            window_pv(1, 1, False, 64)
            with pe.Fori(1, NB // 2) as i:
                window_pv(i * 2, 0, False, i * 64 + 64)
                window_pv(i * 2 + 1, 1, False, i * 64 + 64)

            spread_rows((2, 3, 0, 1), s["m2_ready"], 1, s["bc2_mm"], s["bc2_ev"])
            pe.wait_ge(s["bc2_ev"], 8)
            turn(0, s["mg_ready"], s["mg_mm"], s["mg_ev"])
            pe.wait_ge(s["mg_ev"], 5)
            for k in range(WSLOTS):
                project(ADA_CH + QKV_CH, 0, k, s["out_ev"], k - 1 if k >= 2 else None)
            pe.wait_ge(s["out_ev"], OUT_CH)
            turn(3, s["h_ready"], s["hT_mm"], s["hT_ev"])
            pe.wait_ge(s["hT_ev"], 10)

            pe.wait_ge(s["subk_in"], 16)
            base = ADA_CH + QKV_CH + OUT_CH

            def query_group(r, k, j, first):
                m = r * 8 + (2 * k + j)
                if j == 0:
                    w_round(base // WSLOTS + r, k)
                if not (first and 2 * k + j < 2):
                    pe.wait_ge(s["pq_ev"], m - 1)
                for c in range(KC):
                    last = pe.matmul(ps[:, j, 0:NTOK], W[k][:, c, j * P:(j + 1) * P], hT[:, c, :],
                                     start=(c == 0), stop=(c == KC - 1))
                last.then_inc(s["w_used"] if j else s["pq_mm"], 1)

            def score_group(r, k, j, first):
                m = r * 8 + (2 * k + j)
                pe.wait_ge(s["pq_ev"], m + 1)
                if not (first and 2 * k + j < 2):
                    pe.wait_ge(s["score_ev"], m - 1)
                for t in range(3):
                    last = pe.matmul(ps[0:TP[t], 2 + j, t * P:(t + 1) * P], eq[:, j, t * P:t * P + TP[t]],
                                     subk[:, bass.ds(m, 1), :].rearrange("p a n -> p (a n)"), start=True, stop=True)
                last.then_inc(s["score_mm"], 1)

            def pq_round(r, first):
                for k in range(WSLOTS):
                    for j in range(2):
                        query_group(r, k, j, first)
                    for j in range(2):
                        score_group(r, k, j, first)

            pq_round(0, True)
            with pe.Fori(1, 2) as r:
                pq_round(r, False)
            pe.wait_ge(s["score_ev"], 16)

            def experts(t, banks):
                for q in range(2):
                    pe.matmul(ps[:, banks + q, :], zeroP, H[:, t, q * 512:(q + 1) * 512], start=True, stop=False,
                              skip_group_check=True)
                with pe.Fori(0, NH) as h:
                    for k in range(TOPK):
                        pe.wait_ge(s["diag_done"], h * TOPK + (t * 128 + k + 1))
                        for q in range(2):
                            last = pe.matmul(ps[:, banks + q, :], diag[:, k % 4, :],
                                             R[:, k % NSLOT, D + q * 512:D + (q + 1) * 512],
                                             start=False, stop=False, skip_group_check=True)
                        last.then_inc(s["e_used"], 1)

            zeroP = tw[:, 2048:2048 + P]
            pe.wait_ge(s["z_v"], 1)
            experts(0, 4)
            experts(1, 6)

            pe.wait_ge(s["top_done"], 24)
            pe.wait_ge(s["score_ev"], 16)
            pe.transpose(ps[:, 0, 0:NB], idxf[0:NB, 16:24, :].rearrange("p a n -> p (a n)"), ident[0:NB, 0:NB])
            pe.transpose(ps[:, 0, NB:2 * NB], gall[0:NB, 16:24, :].rearrange("p a n -> p (a n)"),
                         ident[0:NB, 0:NB]).then_inc(s["sidx_mm"], 1)
            for b in range(NB):
                if b >= 1:
                    pe.wait_ge(s["sdot"], b)
                for q in range(2):
                    last = pe.matmul(ps[:, 2 + q, :], ident[0:NB, b:b + 1].to_broadcast([NB, P]),
                                     H[0:NB, 2, q * 512:(q + 1) * 512], start=True, stop=True)
                last.then_inc(s["hb_mm"], 1)
            pe.wait_ge(s["swd"], 1)
            for b in range(NB):
                for q in range(2):
                    last = pe.matmul(ps[0:NB, q, :], tw[:, b * NB:(b + 1) * NB], R[:, b, D + q * 512:D + (q + 1) * 512],
                                     start=(b == 0), stop=(b == NB - 1))
            last.then_inc(s["sacc"], 1)


        @block.scalar
        def _(act):
            act.wait_ge(s["c_in"], 64)
            act.activation(cwork[1], cwork[0], ACT.Exp, scale=-1.0).then_inc(s["act"], 1)
            act.wait_ge(s["cT_mm"], 1)
            act.activation(cT[:, :, :], ps[:, 7, 0:72].rearrange("p (c n) -> p c n", c=KC), ACT.Copy
                           ).then_inc(s["cT_ev"], 1)

            def stage_sel(a, k):
                act.activation(bsel[:, k % 2, :], ident[0:ADA_CH, bass.ds(a, 1)].to_broadcast([ADA_CH, 9]), ACT.Copy
                               ).then_inc(s["sel_ready"], 1)

            def ada_ev(sel, n, slot0):
                with act.Fori(0, n) as r:
                    for k in range(WSLOTS):
                        a = (r + sel) * WSLOTS + k
                        act.wait_ge(s["ada_mm"], a + 1)
                        act.activation(m_rows[:, bass.ds(r + slot0, 1), k * WC:(k + 1) * WC].rearrange("p a n -> p (a n)"),
                                       ps[0:9, k % 2, 0:WC], ACT.Copy).then_inc(s["ada_ev"], 1)
                        stage_sel(a + 2, k)

            stage_sel(0, 0)
            stage_sel(1, 1)
            ada_ev(0, 2, 0)

            def spread_ev(order, mm, ev):
                for n, slot in enumerate(q for q in order for _ in range(2)):
                    act.wait_ge(mm, n + 1)
                    act.activation(m_all[:, slot, (n % 2) * 512:(n % 2 + 1) * 512], ps[:, 4 + n % 4, :], ACT.Copy
                                   ).then_inc(ev, 1)

            spread_ev((0, 1), s["bc_mm"], s["bc_ev"])

            act.wait_ge(s["h_ssq"], 1)
            act.activation(stat[:, 4:7], stat[:, 0:3], ACT.Sqrt).then_inc(s["h_rt"], 1)

            def turn_ev(n0, mm, ev):
                for n in range(5):
                    act.wait_ge(mm, n0 + n + 1)
                    if n < 4:
                        t, half = divmod(n, 2)
                        act.activation(hT[:, 4 * half:4 * half + 4, t * P:(t + 1) * P],
                                       ps[:, n, :].rearrange("p (c n) -> p c n", c=4), ACT.Copy).then_inc(ev, 1)
                    else:
                        act.activation(hT[:, :, SEQ:NTOK], ps[:, 4, 0:64].rearrange("p (c n) -> p c n", c=KC), ACT.Copy
                                       ).then_inc(ev, 1)

            turn_ev(0, s["hT_mm"], s["hT_ev"])

            def qkv_ev(r, k):
                n = r * WSLOTS + k
                act.wait_ge(s["w_used"], n + (8 + 1))
                act.activation(QKV[:, 0:2, bass.ds(n * WC, WC)],
                               ps[:, 2 * (k % 2), :].rearrange("p (t n) -> p t n", t=2), ACT.Copy)
                act.activation(QKV[0:NB, 2, bass.ds(n * WC, WC)], ps[0:NB, 2 * (k % 2) + 1, 0:WC], ACT.Copy
                               ).then_inc(s["qkv_ev"], 1)

            for k in range(WSLOTS):
                qkv_ev(0, k)

            def queries_ev(mm, ev):
                for b in range(NB):
                    act.wait_ge(mm, b + 1)
                    act.activation(QB[:, b, :], ps[:, 4 + b % 4, :], ACT.Copy).then_inc(ev, 1)

            queries_ev(s["qb_mm"], s["qb_ev"])
            with act.Fori(1, QKV_CH // WSLOTS) as r:
                for k in range(WSLOTS):
                    qkv_ev(r, k)
            ada_ev(2, 2, 2)
            ada_ev(4, 2, 0)

            act.wait_ge(s["z_l"], 1)
            steps = Count(s["z_abs"])
            steps.inc(act.activation(zt, z1, ACT.Abs))
            steps.wait(act)
            steps.inc(act.activation(zt, zt, ACT.Exp, scale=-1.0))
            steps.wait(act)
            steps.inc(act.activation(zt, zt, ACT.Ln, bias=1.0))
            act.wait_ge(s["z_e"], 1)
            act.activation(z1, z1, ACT.Exp).then_inc(s["zz_a"], 1)
            queries_ev(s["qd_mm"], s["qd_ev"])
            act.wait_ge(s["dm_ready"], 1)
            act.activation(zrow[:, :], zrow[:, :], ACT.Exp, bias=stat[0:64, 9:10], scale=SCALE).then_inc(s["de_ready"], 1)
            act.wait_ge(s["dU_mm"], 1)
            act.activation(pd[:, :, :], ps[:, 7, 0:192].rearrange("p (g n) -> p g n", g=3), ACT.Copy).then_inc(s["pd_ev"], 1)

            def stage_pair(i, g, colq, colk):
                act.activation(stq, QKV[:, 0:2, bass.ds(colq + g * P, P)], ACT.Copy)
                act.activation(stk, QKV[:, 0:2, bass.ds(colk + g * P, P)], ACT.Copy).then_inc(s["st_ready"], 1)
                act.wait_ge(s["t_mm"], i + 1)
                act.activation(qk, ps[:, 0, :], ACT.Copy).then_inc(s["t_ev"], 1)

            act.wait_ge(s["rot_done"], 1)
            with act.Fori(0, NH // 2) as g:
                stage_pair(g, g, QA, KA)
                act.wait_ge(s["s_l"], g * 2 + 2)
                st = Count(s["s_t"], g * 3)
                st.inc(act.activation(aw[1], aw[0], ACT.Abs))
                st.wait(act)
                st.inc(act.activation(aw[1], aw[1], ACT.Exp, scale=-1.0))
                st.wait(act)
                st.inc(act.activation(aw[1], aw[1], ACT.Ln, bias=1.0))
                act.wait_ge(s["s_a"], g * 2 + 2)
                act.activation(aw[2], aw[2], ACT.Exp).then_inc(s["s_e"], 1)

            with act.Fori(0, NH // 2) as g:
                stage_pair(g + 4, g, QB_, KB_)
                act.wait_ge(s["d_zm"], g + 1)
                for j in range(2):
                    for n, c in enumerate((slice(0, 128), slice(128, 384))):
                        last = act.activation(aw[0][:, j, c], aw[0][:, j, c], ACT.Exp,
                                              bias=stat[:, 20 + 2 * j + n:21 + 2 * j + n], scale=SCALE)
                last.then_inc(s["d_e"], 1)
                act.wait_ge(s["d_tr"], g + 1)
                act.activation(pT, ps[:, 1:3, 0:384], ACT.Copy).then_inc(s["d_pT"], 1)

            def stage_b(i, j, first, src, ready, used):
                if not first:
                    act.wait_ge(used, i - 1)
                act.activation(ast[:, j, 0:src.shape[1], :], src[:, :, bass.ds(i * NH, NH)], ACT.Copy)
                act.activation(selst[:, j, :], cst("unit8")[0:NH, bass.ds(i * NB, NB)], ACT.Copy).then_inc(ready, 1)

            zsrc = Z[:, 0, :].rearrange("p (g n) -> p g n", g=NPG)
            for src, ready, used, prev in ((zsrc, s["ast_ready"], s["oA_mm"], None),
                                           (pd[:, :, :], s["pdst_ready"], s["oB_mm"], s["oA_mm"])):
                if prev is not None:
                    act.wait_ge(prev, NB)
                stage_b(0, 0, True, src, ready, used)
                stage_b(1, 1, True, src, ready, used)
                with act.Fori(1, NB // 2) as i:
                    stage_b(i * 2, 0, False, src, ready, used)
                    stage_b(i * 2 + 1, 1, False, src, ready, used)

            spread_ev((2, 3, 0, 1), s["bc2_mm"], s["bc2_ev"])
            act.wait_ge(s["ff_ready"], 1)
            act.activation(stat[:, 4:10], stat[:, 10:16], ACT.Sqrt).then_inc(s["f_rt"], 1)
            act.wait_ge(s["h_ssq"], 2)
            act.activation(stat[:, 4:7], stat[:, 0:3], ACT.Sqrt).then_inc(s["h_rt"], 1)
            turn_ev(5, s["hT_mm"], s["hT_ev"])

            def pq_ev(r, k, first):
                for j in range(2):
                    m = r * 8 + (2 * k + j)
                    if j == 0:
                        act.wait_ge(s["pq_mm"], r * 4 + (k + 1))
                    else:
                        act.wait_ge(s["w_used"], r * 4 + (ADA_CH + QKV_CH + OUT_CH + k + 1))
                    if not (first and k == 0):
                        act.wait_ge(s["score_mm"], m - 1)
                    act.activation(eq[:, j, 0:NTOK], ps[:, j, 0:NTOK], ACT.Copy).then_inc(s["pq_ev"], 1)
                for j in range(2):
                    m = r * 8 + (2 * k + j)
                    h = r * 4 + k
                    act.wait_ge(s["score_mm"], m + 1)
                    act.activation(S[:, bass.ds(h, 2, step=NH), j, :],
                                   ps[:, 2 + j, 0:256].rearrange("p (t n) -> p t n", t=2), ACT.Copy)
                    act.activation(S[0:NB, bass.ds(h + 16, 1), j, :].rearrange("p a n -> p (a n)"),
                                   ps[0:NB, 2 + j, 256:384], ACT.Copy).then_inc(s["score_ev"], 1)

            act.wait_ge(s["z_v"], 1)
            for k in range(WSLOTS):
                pq_ev(0, k, True)
            with act.Fori(1, 2) as r:
                for k in range(WSLOTS):
                    pq_ev(r, k, False)

            def top_exp(i):
                act.wait_ge(s["topsm"], i + 1)
                act.activation(ctop_e, ctop_d, ACT.Exp).then_inc(s["tope"], 1)

            def weights(i):
                act.wait_ge(s["top_done"], i + 1)
                act.activation(gst[:, :], gall[:, bass.ds(i, 1), :].rearrange("p a n -> p (a n)"), ACT.Copy
                               ).then_inc(s["g_st"], 1)
                act.wait_ge(s["g_st"], i + 1)
                for k in range(0, TOPK, 2):
                    act.wait_ge(s["dot_done"], i * TOPK + (k + 2))
                    act.activation(gel[:, k:k + 2], dots[:, k:k + 2], ACT.Gelu_apprx_tanh).then_inc(s["gel_done"], 1)
                    act.wait_ge(s["gel_done"], i * (TOPK // 2) + (k // 2 + 1))
                    for q in range(2):
                        last = act.activation(wgt[:, k + q:k + q + 1], gel[:, k + q:k + q + 1], ACT.Copy,
                                              scale=gst[:, k + q:k + q + 1])
                    last.then_inc(s["w_done"], 1)
                    act.wait_ge(s["w_done"], i * (TOPK // 2) + (k // 2 + 1))
                    for q in range(2):
                        yield k + q

            def head_weights(i, first):
                for k in weights(i):
                    if not (first and k < 4):
                        act.wait_ge(s["e_used"], i * TOPK + (k - 3))
                    act.activation(diag[:, k % 4, :], ident, ACT.Copy, scale=wgt[:, k:k + 1]).then_inc(s["diag_done"], 1)

            def final_root(t):
                act.wait_ge(s["ff_ready"], t + 2)
                act.activation(stat[0:TP[t], 17:18], stat[0:TP[t], 16:17], ACT.Sqrt).then_inc(s["f_rt"], 1)

            top_exp(0)
            top_exp(1)
            head_weights(0, True)
            top_exp(2)
            with act.Fori(1, NH) as h:
                head_weights(h, False)
                top_exp(h + 2)
            final_root(0)
            with act.Fori(0, NH - 1) as h:
                head_weights(h + 8, False)
                top_exp(h * 2 + 10)
                top_exp(h * 2 + 11)
            head_weights(2 * NH - 1, False)
            final_root(1)
            act.wait_ge(s["sdot"], NB)
            act.activation(stat[:, 8:16], dots[:, 0:NB], ACT.Gelu_apprx_tanh).then_inc(s["sgel"], 1)
            final_root(2)

        @block.vector
        def _(dve):
            ch = Count(s["dve"])

            def step(ins):
                ch.inc(ins)
                ch.wait(dve)

            dve.wait_ge(s["act"], 1)
            dve.wait_ge(s["c_in"], 64)
            step(dve.tensor_scalar(cwork[1], cwork[1], 1.0, None, ALU.add))
            step(dve.reciprocal(cwork[1], cwork[1]))
            dve.tensor_tensor(cwork[0], cwork[0], cwork[1], ALU.mult).then_inc(s["cs_ready"], 1)
            dve.wait_ge(s["ada_ev"], 8)
            dve.scalar_tensor_tensor(m_rows[:, 1, :], m_rows[:, 1, :], 1.0, cwork[2], ALU.add, ALU.mult
                                     ).then_inc(s["m1_ready"], 1)

            def sums(n):
                for t in range(3):
                    last = dve.tensor_tensor_reduce(H[0:TP[t], t, :], x[0:TP[t], t, :], x[0:TP[t], t, :], 1.0, 0.0,
                                                    ALU.mult, ALU.add, stat[0:TP[t], t:t + 1])
                step(last)
                dve.tensor_scalar(stat[:, 0:3], stat[:, 0:3], 1.0 / D, EPS, ALU.mult, ALU.add).then_inc(s["h_ssq"], 1)
                dve.wait_ge(s["h_rt"], n)
                step(dve.reciprocal(stat[:, 0:3], stat[:, 4:7]))

            def modulate(scale, shift):
                for t in range(3):
                    n = TP[t]
                    a, b = (m_all[:, scale, :], m_all[:, shift, :]) if t < 2 else (m_rows[0:NB, scale, :], m_rows[0:NB, shift, :])
                    step(dve.scalar_tensor_tensor(H[0:n, t, :], x[0:n, t, :], stat[0:n, t:t + 1], a, ALU.mult, ALU.mult))
                    dve.tensor_tensor(H[0:n, t, :], H[0:n, t, :], b, ALU.add).then_inc(s["h_ready"], 1)

            step(dve.memset(stat[:, :], 0.0))
            dve.wait_ge(s["x_in"], 48)
            sums(1)
            dve.wait_ge(s["m1_ready"], 1)
            dve.wait_ge(s["bc_ev"], 4)
            modulate(1, 0)

            dve.wait_ge(s["qb_ev"], NB)
            with dve.Fori(0, NB) as b:
                kc = Count(s["kst"], b * CPB)
                for c in range(CPB):
                    dve.wait_ge(k_ready[c % KVS], b * 64 + 32 * (c // KVS + 1))
                    kv = KV[c % KVS]
                    q = QB[:, bass.ds(b, 1), :].to_broadcast([P, KVP, DG])
                    kc.inc(dve.tensor_tensor(kv, kv, q, ALU.mult))
                    kc.wait(dve)
                    dve.tensor_reduce(z4[:, c * KVP:(c + 1) * KVP, bass.ds(b, 1), :].rearrange("p g a h -> p g (a h)"),
                                      kv.rearrange("p g (h d) -> p g h d", h=NH), AX, ALU.add).then_inc(s["k_used"], 1)

            dve.wait_ge(s["qkv_ev"], QKV_CH)
            for t in range(3):
                n = TP[t]
                qkr = QKV[0:n, t, QB_:QB_ + 2 * DG].rearrange("p (h d) -> p h d", d=HD)
                x1, x2 = qkr[:, :, 0:8], qkr[:, :, 8:16]
                ro = cst("rope")[0:n, t * 16:(t + 1) * 16].rearrange("p (a d) -> p a d", a=2)
                cos, sin = (ro[:, a:a + 1, :].to_broadcast([n, 16, 8]) for a in range(2))
                r = [Hf[0:n, 128 * m:128 * (m + 1)].rearrange("p (h d) -> p h d", d=8) for m in range(4)]
                for out, a, b in ((r[0], x1, cos), (r[1], x2, sin), (r[2], x2, cos), (r[3], x1, sin)):
                    last = dve.tensor_tensor(out, a, b, ALU.mult)
                step(last)
                dve.tensor_tensor(x1, r[0], r[1], ALU.subtract)
                step(dve.tensor_tensor(x2, r[2], r[3], ALU.add))
            dve.tensor_copy(stat[:, 31:32], stat[:, 31:32]).then_inc(s["rot_done"], 1)

            dve.wait_ge(s["k_used"], NB * CPB)
            dve.wait_ge(s["small_in"], 64)
            zv = z1.rearrange("p (n h) -> p n h", h=NH)
            dve.wait_ge(s["dve"], ch.n)
            dve.scalar_tensor_tensor(zv, zv, SCALE, sbb[:, :].rearrange("p (a h) -> p a h", a=1).to_broadcast([P, P, NH]),
                                     ALU.mult, ALU.add).then_inc(s["z_l"], 1)
            dve.wait_ge(s["z_abs"], 3)
            dve.wait_ge(s["z_l"], 1)
            step(dve.scalar_tensor_tensor(zl, z1, 0.0, zt, ALU.max, ALU.add))
            step(dve.memset(zt[:, 960:1024], 0.0))
            for g in range(NPG - 2, -1, -1):
                nxt = slice((g + 1) * 64, (g + 2) * 64)
                ins = dve.tensor_tensor(zt[:, g * 64:(g + 1) * 64], zl[:, nxt], zt[:, nxt], ALU.add)
                if g:
                    step(ins)
            ins.then_inc(s["z_suf"], 1)
            dve.wait_ge(s["z_s"], 1)
            dve.tensor_tensor(Z[:, 0, :].rearrange("p (a n) -> p a n", a=2), Z[:, 0, :].rearrange("p (a n) -> p a n", a=2),
                              ps[:, 4:6, :], ALU.subtract).then_inc(s["z_e"], 1)

            dve.wait_ge(s["qd_ev"], NB)
            with dve.Fori(0, NB // 2) as i:
                for j in range(2):
                    dve.wait_ge(dk_ready[j], i * 64 + 64)
                    kv = DK[j]
                    kc = Count(s["dst"], i * 2 + j)
                    kc.inc(dve.tensor_tensor(kv, kv, QB[:, bass.ds(i * 2 + j, 1), :].to_broadcast([P, 3, DG]), ALU.mult))
                    kc.wait(dve)
                    dve.tensor_reduce(zd[:, :, bass.ds(i * (2 * NH) + j * NH, NH)],
                                      kv.rearrange("p g (h d) -> p g h d", h=NH), AX, ALU.add).then_inc(s["dk_used"], 1)
            dve.wait_ge(s["dT_mm"], 1)
            step(dve.tensor_tensor(zrow[:, :], ps[0:64, 6, 0:384], cst("sbias")[0:64, :], ALU.add))
            step(dve.tensor_reduce(stat[0:64, 8:9], zrow[:, :], AX, ALU.max))
            dve.tensor_scalar(stat[0:64, 9:10], stat[0:64, 8:9], -SCALE, None, ALU.mult).then_inc(s["dm_ready"], 1)
            dve.wait_ge(s["de_ready"], 1)
            step(dve.tensor_tensor_reduce(zrow[:, :], zrow[:, :], cst("scnt")[0:64, :], 1.0, 0.0, ALU.mult, ALU.add,
                                          stat[0:64, 8:9]))
            step(dve.reciprocal(stat[0:64, 8:9], stat[0:64, 8:9]))
            dve.tensor_scalar(zrow[:, :], zrow[:, :], stat[0:64, 8:9], None, ALU.mult).then_inc(s["dp_ready"], 1)

            def both(a):
                return a.rearrange("p j (n k) -> p j n k", n=3)[:, :, bass.ds(0, 2, step=2), :]

            lat = later.rearrange("p (a b k) -> p a b k", a=1, b=1).to_broadcast([P, 2, 2, P])
            with dve.Fori(0, NH // 2) as g:
                dve.wait_ge(s["sc_mm"], g + 1)
                for j in range(2):
                    dve.tensor_scalar(aw[0][:, j, :], ps[:, 1 + j, 0:384], SCALE, sbb[:, bass.ds(g * 2 + j, 1)],
                                      ALU.mult, ALU.add).then_inc(s["s_l"], 1)
                dve.wait_ge(s["s_t"], g * 3 + 3)
                dve.wait_ge(s["s_l"], g * 2 + 2)
                c = Count(s["sbs"], g)
                c.inc(dve.scalar_tensor_tensor(aw[1], aw[0], 0.0, aw[1], ALU.max, ALU.add))
                c.wait(dve)
                dve.tensor_tensor(both(aw[1]), both(aw[1]), lat, ALU.mult).then_inc(s["s_L"], 1)
                dve.wait_ge(s["s_mm"], g + 1)
                for j in range(2):
                    dve.tensor_tensor(aw[2][:, j, :], aw[0][:, j, :], ps[:, 3 + j, 0:384], ALU.subtract
                                      ).then_inc(s["s_a"], 1)
                dve.wait_ge(s["s_e"], g + 1)
                dve.tensor_tensor(both(aw[2]), both(aw[2]), lat, ALU.mult).then_inc(s["s_am"], 1)
                dve.wait_ge(s["o_mm"], g + 1)
                dve.tensor_copy(QKV[:, 0:2, bass.ds(QA + g * P, P)], ps[:, 5, 0:256].rearrange("p (t n) -> p t n", t=2)
                                ).then_inc(s["o_ev"], 1)

            with dve.Fori(0, NH // 2) as g:
                dve.wait_ge(s["sc_mm"], g + 5)
                c = Count(s["dis"], g * 3)
                for j in range(2):
                    last = dve.tensor_tensor(aw[0][:, j, :], ps[:, 1 + j, 0:384], cst("dbias"), ALU.add)
                c.inc(last)
                c.wait(dve)
                for j in range(2):
                    dve.tensor_reduce(stat[:, 24 + 2 * j:25 + 2 * j], aw[0][:, j, 0:128], AX, ALU.max)
                    last = dve.tensor_reduce(stat[:, 25 + 2 * j:26 + 2 * j], aw[0][:, j, 128:384], AX, ALU.max)
                c.inc(last)
                c.wait(dve)
                dve.tensor_scalar(stat[:, 20:24], stat[:, 24:28], -SCALE, None, ALU.mult).then_inc(s["d_zm"], 1)
                dve.wait_ge(s["d_e"], g + 1)
                for j in range(2):
                    for n, cc in enumerate((slice(0, 128), slice(128, 384))):
                        last = dve.tensor_tensor_reduce(aw[0][:, j, cc], aw[0][:, j, cc], cst("cnt")[:, cc], 1.0, 0.0,
                                                        ALU.mult, ALU.add, stat[:, 24 + 2 * j + n:25 + 2 * j + n])
                last.then_inc(s["d_p"], 1)
                dve.wait_ge(s["d_p"], g + 1)
                c.inc(dve.reciprocal(stat[:, 24:28], stat[:, 24:28]))
                c.wait(dve)
                dve.wait_ge(s["d_o"], g + 1)
                for j in range(2):
                    for t in range(2):
                        last = dve.tensor_scalar(QKV[:, t, bass.ds(QB_ + j * HD + g * P, HD)],
                                                 ps[:, 5, t * P + j * HD:t * P + (j + 1) * HD],
                                                 stat[:, 24 + 2 * j + t:25 + 2 * j + t], None, ALU.mult)
                last.then_inc(s["d_oe"], 1)

            for mm, per, ready, used in ((s["v_used"], CPB, s["msk_ready"], s["oA_mm"]), (s["vd_used"], 1, s["mskd_ready"], s["oB_mm"])):
                def block_rows(i, j, first):
                    dve.wait_ge(mm, i * per + per)
                    if not first:
                        dve.wait_ge(used, i)
                    dve.tensor_tensor(msk[:, :], ps[0:NH, 6 + j, :], cst("hmask")[0:NH, :], ALU.mult).then_inc(ready, 1)
                if used is s["oB_mm"]:
                    dve.wait_ge(s["oA_mm"], NB)
                block_rows(0, 0, True)
                block_rows(1, 1, False)
                with dve.Fori(1, NB // 2) as i:
                    block_rows(i * 2, 0, False)
                    block_rows(i * 2 + 1, 1, False)
            dve.wait_ge(s["oB_mm"], NB)
            dve.wait_ge(s["qb_ev"], NB)
            dve.tensor_copy(QKV[0:NB, 2, QA:QA + DG], ps[0:NB, 3, :])
            step(dve.tensor_copy(QKV[0:NB, 2, QB_:QB_ + DG], ps[0:NB, 4, :]))

            dve.wait_ge(s["ada_ev"], ADA_CH)
            dve.wait_ge(s["small_in"], 64)
            dve.scalar_tensor_tensor(m_rows[:, 0, :], m_rows[:, 0, :], 1.0, nffn[:, :], ALU.add, ALU.mult
                                     ).then_inc(s["m2_ready"], 1)

            for t in range(3):
                for q, col in ((0, QA), (1, QB_)):
                    n = TP[t]
                    o = QKV[0:n, t, col:col + DG]
                    last = dve.tensor_tensor_reduce(H[0:n, t, q * DG:(q + 1) * DG], o, o, 1.0, 0.0, ALU.mult, ALU.add,
                                                    stat[0:n, 10 + 2 * t + q:11 + 2 * t + q])
            step(last)
            dve.tensor_scalar(stat[:, 10:16], stat[:, 10:16], 1.0 / DG, EPS, ALU.mult, ALU.add).then_inc(s["ff_ready"], 1)
            dve.wait_ge(s["f_rt"], 1)
            step(dve.reciprocal(stat[:, 10:16], stat[:, 4:10]))
            for t in range(3):
                for q, col in ((0, QA), (1, QB_)):
                    n = TP[t]
                    last = dve.tensor_scalar(H[0:n, t, q * DG:(q + 1) * DG], QKV[0:n, t, col:col + DG],
                                             stat[0:n, 10 + 2 * t + q:11 + 2 * t + q], None, ALU.mult)
                last.then_inc(s["mg_ready"], 1)
            for n in range(5):
                dve.wait_ge(s["mg_mm"], n + 1)
                if n < 4:
                    t, half = divmod(n, 2)
                    dve.tensor_tensor(hT[:, 4 * half:4 * half + 4, t * P:(t + 1) * P],
                                      ps[:, n, :].rearrange("p (c n) -> p c n", c=4),
                                      gcol[:, 4 * half:4 * half + 4].rearrange("p (c a) -> p c a", a=1).to_broadcast([P, 4, P]),
                                      ALU.mult).then_inc(s["mg_ev"], 1)
                else:
                    dve.tensor_tensor(hT[:, :, SEQ:NTOK], ps[:, 4, 0:64].rearrange("p (c n) -> p c n", c=KC),
                                      gcol[:, :].rearrange("p (c a) -> p c a", a=1).to_broadcast([P, KC, NB]),
                                      ALU.mult).then_inc(s["mg_ev"], 1)
            dve.wait_ge(s["kv_out"], 160)
            dve.wait_ge(s["new_out"], 32)
            step(dve.memset(S[:, 16:24, :, :].rearrange("p a b n -> p (a b n)"), 0.0))
            dve.memset(tw[:, 2048:2048 + P], 0.0).then_inc(s["z_v"], 1)
            dve.wait_ge(s["bc2_ev"], 8)
            for k in range(OUT_CH):
                c = slice(k * WC, (k + 1) * WC)
                dve.wait_ge(s["w_used"], ADA_CH + QKV_CH + k + 1)
                if k:
                    dve.wait_ge(s["out_ev"], k)
                g1 = m_all[:, 2:3, c].to_broadcast([P, 2, WC])
                tmp = tw[:, 0:512].rearrange("p (t n) -> p t n", t=2)
                dve.tensor_tensor(tmp, ps[:, 2 * (k % 2), :].rearrange("p (t n) -> p t n", t=2), g1, ALU.mult)
                step(dve.tensor_tensor(tw[0:NB, 512:768], ps[0:NB, 2 * (k % 2) + 1, 0:WC], m_rows[0:NB, 2, c], ALU.mult))
                dve.tensor_tensor(x[:, 0:2, c], x[:, 0:2, c], tmp, ALU.add)
                dve.tensor_tensor(x[0:NB, 2, c], x[0:NB, 2, c], tw[0:NB, 512:768], ALU.add).then_inc(s["out_ev"], 1)
            dve.wait_ge(s["out_ev"], OUT_CH)
            sums(2)
            modulate(0, 3)

            def top16(tk, vals, where, row, spare):
                wait_apart(dve, tk.sem, tk.value())
                tk.inc(dve.max(vals[:, 0:8], row))
                wait_apart(dve, tk.sem, tk.value())
                dve.max_index(where[:, 0:8], vals[:, 0:8], row)
                tk.inc(dve.match_replace(spare, vals[:, 0:8], row, LOWEST))
                wait_apart(dve, tk.sem, tk.value())
                tk.inc(dve.max(vals[:, 8:16], spare))
                wait_apart(dve, tk.sem, tk.value())
                tk.inc(dve.max_index(where[:, 8:16], vals[:, 8:16], spare))

            def grid(a):
                return a.rearrange("p (k j) -> p k j", k=TOPK)

            def along(a, dim):
                if dim == 1:
                    return a.rearrange("p (k j) -> p k j", j=1).to_broadcast([P, TOPK, TOPK])
                return a.rearrange("p (k j) -> p k j", k=1).to_broadcast([P, TOPK, TOPK])

            TOPSTEPS = 22

            def choose(i):
                tk = Count(s["tks"], i * TOPSTEPS)
                tk.inc(dve.tensor_copy(sc, S[:, bass.ds(i, 1), :, :].rearrange("p a c n -> p (a c n)")))
                for c in range(2):
                    top16(tk, tv[c], tiu[c], sc[:, c * NKEY:(c + 1) * NKEY], rep[:, c * NKEY:(c + 1) * NKEY])
                tk.wait(dve)
                for c in range(2):
                    last = dve.tensor_copy(tif[c], tiu[c][:, :])
                tk.inc(dve.tensor_tensor(grid(cand), along(tv[0], 1), along(tv[1], 2), ALU.add))
                top16(tk, cv, ciu, cand, crep)
                tk.wait(dve)
                dve.tensor_scalar(ctop_d, cv, cv[:, 0:1], None, ALU.subtract).then_inc(s["topsm"], 1)
                dve.tensor_scalar(cint[:, 0, :], ciu[:, :], 4, None, ALU.logical_shift_right)
                tk.inc(dve.tensor_scalar(cint[:, 1, :], ciu[:, :], 15, None, ALU.bitwise_and))
                tk.wait(dve)
                dve.tensor_copy(row_f, cint[:, 0, :])
                tk.inc(dve.tensor_copy(col_f, cint[:, 1, :]))
                tk.wait(dve)
                for want, o in ((row_f, oh), (col_f, oh2)):
                    last = dve.tensor_tensor(grid(o), along(want, 1), along(cst("iota"), 2), ALU.is_equal)
                tk.inc(last)
                tk.wait(dve)
                for c, o in ((0, oh), (1, oh2)):
                    last = dve.tensor_tensor(grid(o), grid(o), along(tif[c], 2), ALU.mult)
                tk.inc(last)
                tk.wait(dve)
                dve.tensor_reduce(e1f, grid(oh), AX, ALU.add)
                tk.inc(dve.tensor_reduce(e2f, grid(oh2), AX, ALU.add))
                tk.wait(dve)
                ef = idxf[:, bass.ds(i, 1), :].rearrange("p a n -> p (a n)")
                tk.inc(dve.scalar_tensor_tensor(ef, e1f, float(NKEY), e2f, ALU.mult, ALU.add))
                tk.wait(dve)
                dve.tensor_copy(idx[:, bass.ds(i, 1), :].rearrange("p a n -> p (a n)"), ef)
                dve.wait_ge(s["tope"], i + 1)
                tk.inc(dve.tensor_reduce(tst[:, 0:1], ctop_e, AX, ALU.add))
                tk.wait(dve)
                tk.inc(dve.reciprocal(tst[:, 1:2], tst[:, 0:1]))
                tk.wait(dve)
                dve.tensor_scalar(gall[:, bass.ds(i, 1), :].rearrange("p a n -> p (a n)"), ctop_e, tst[:, 1:2], None,
                                  ALU.mult).then_inc(s["top_done"], 1)
                assert tk.n == TOPSTEPS, tk.n

            def dot_rows(i, t):
                for k in range(TOPK):
                    dve.wait_ge(e_ready[k % NSLOT], i * 32 + 16 * (k // NSLOT + 1))
                    u = R[:, k % NSLOT, 0:D]
                    dve.tensor_tensor_reduce(u, u, H[:, t, :], 1.0, 0.0, ALU.mult, ALU.add, dots[:, k:k + 1]
                                             ).then_inc(s["dot_done"], 1)

            def finish(t, bank, acc, value, gate):
                n = TP[t]
                dve.wait_ge(acc, value)
                dve.wait_ge(s["fin_in"], 16)
                a = ps[0:n, bank:bank + 2, :]
                Ht = H[0:n, t, :].rearrange("p (a n) -> p a n", a=2)
                step(dve.tensor_tensor(Ht, a, gate.rearrange("p (a n) -> p a n", a=2), ALU.mult))
                step(dve.tensor_tensor(x[0:n, t, :], x[0:n, t, :], H[0:n, t, :], ALU.add))
                step(dve.tensor_tensor_reduce(H[0:n, t, :], x[0:n, t, :], x[0:n, t, :], 1.0, 0.0, ALU.mult, ALU.add,
                                              stat[0:n, 18:19]))
                dve.tensor_scalar(stat[0:n, 16:17], stat[0:n, 18:19], 1.0 / D, EPS, ALU.mult, ALU.add
                                  ).then_inc(s["ff_ready"], 1)
                dve.wait_ge(s["f_rt"], t + 2)
                step(dve.reciprocal(stat[0:n, 19:20], stat[0:n, 17:18]))
                dve.scalar_tensor_tensor(H[0:n, t, :], x[0:n, t, :], stat[0:n, 19:20], m_all[0:n, 3, :], ALU.mult, ALU.mult
                                         ).then_inc(s["y_ready"], 1)

            dve.wait_ge(s["score_ev"], 16)
            choose(0)
            choose(1)
            with dve.Fori(0, NH) as h:
                dot_rows(h, 0)
                choose(h + 2)
            finish(0, 4, s["e_used"], NH * TOPK, m_all[:, 1, :])
            with dve.Fori(0, NH - 1) as h:
                dot_rows(h + 8, 1)
                choose(h * 2 + 10)
                choose(h * 2 + 11)
            dot_rows(2 * NH - 1, 1)

            dve.wait_ge(s["sidx_mm"], 1)
            dve.tensor_copy(idx[:, 0, 0:NB], ps[:, 0, 0:NB]).then_inc(s["sidx_ready"], 1)
            gT = stat[:, 20:28]
            step(dve.tensor_copy(gT, ps[:, 0, NB:2 * NB]))
            finish(1, 6, s["e_used"], 2 * NH * TOPK, m_all[:, 1, :])
            for b in range(NB):
                dve.wait_ge(e_ready[b], 16 * (2 * NH * 2 + 1))
                dve.wait_ge(s["hb_mm"], b + 1)
                u = R[:, b, 0:D]
                dve.tensor_tensor_reduce(u.rearrange("p (a n) -> p a n", a=2), u.rearrange("p (a n) -> p a n", a=2),
                                         ps[:, 2:4, :], 1.0, 0.0, ALU.mult, ALU.add, dots[:, b:b + 1]
                                         ).then_inc(s["sdot"], 1)
            dve.wait_ge(s["sgel"], 1)
            step(dve.tensor_tensor(stat[:, 8:16], stat[:, 8:16], gT, ALU.mult))
            dve.tensor_tensor(tw[:, 0:64].rearrange("p (b c) -> p b c", b=NB), cst("unit8").rearrange("p (b c) -> p b c", b=NB),
                              stat[:, 8:16].rearrange("p (b c) -> p b c", c=1).to_broadcast([P, NB, NB]), ALU.mult
                              ).then_inc(s["swd"], 1)
            finish(2, 0, s["sacc"], 1, m_rows[0:NB, 1, :])


_OUTS = [("y_p", (SEQ, D), (1, SEQ, D)), ("y_s", (NB, D), (NB, 1, D)),
         ("sb_k_p", (SEQ, DG), (1, 1, SEQ, NH, HD)), ("sb_v_p", (SEQ, DG), (1, 1, SEQ, NH, HD)),
         ("dil_k_p", (SEQ, DG), (1, 1, SEQ, NH, HD)), ("dil_v_p", (SEQ, DG), (1, 1, SEQ, NH, HD)),
         ("sb_k_n", (NB, DG), (1, NB, 1, NH, HD)), ("sb_v_n", (NB, DG), (1, NB, 1, NH, HD)),
         ("dil_k_s", (NB, PAST * DG), (1, NB, PAST, NH, HD)), ("dil_v_s", (NB, PAST * DG), (1, NB, PAST, NH, HD))]


def kernel(**inputs):
    import concourse.bacc as _bacc
    from concourse.bass_utils import run_bass_kernel_spmd as _run

    a = {k: np.asarray(v) for k, v in inputs.items()}

    def chunks(w):
        return w.reshape(KC, P, -1, WC).transpose(2, 1, 0, 3).reshape(-1, P, KC * WC)

    arrays = {
        "consts": constants(),
        "c9": np.concatenate([a["c_sample"], a["c_prompt"]], 0),
        "x": np.concatenate([a["x_prompt"].reshape(SEQ, D), a["x_sample"].reshape(NB, D)], 0),
        "b_ada": a["b_ada"].reshape(ADA_CH, WC),
        "norm_mix": a["norm_mix"].reshape(1, D),
        "norm_ffn": a["norm_ffn"].reshape(1, D),
        "norm_final": a["norm_final"].reshape(1, D),
        "sb_bias": a["sb_bias"].reshape(1, NH),
        "g_out": np.concatenate([a["norm_out_sb"], a["norm_out_dil"]], -1).reshape(KC, P).T,
        "pages": a["page_table"].reshape(1, NB * NPG),
        "wts": np.concatenate([chunks(w) for w in (a["w_ada"][0][:, :2 * D], a["w_in"][0], a["w_ada"][0][:, 2 * D:],
                                                   a["w_out"][0], a["w_peer_q"][0])], 0),
        "subk": a["peer_sub_keys"].reshape(16, NKEY, P).transpose(2, 0, 1).reshape(P, 16 * NKEY),
        "sb_k": a["cache_sb_k"].reshape(-1, P, DG),
        "sb_v": a["cache_sb_v"].reshape(-1, P, DG),
        "dil_k": a["cache_dil_k"].reshape(NB, PAST * DG),
        "dil_v": a["cache_dil_v"].reshape(NB, PAST * DG),
        "uv": np.concatenate([a["peer_u"][0], a["peer_v"][0]], -1),
    }
    arrays = {k: np.ascontiguousarray(v) for k, v in arrays.items()}
    nc = _bacc.Bacc("TRN2", target_bir_lowering=False, num_devices=1)
    A = {k: nc.dram_tensor("in_" + k, v.shape, mybir.dt.from_np(v.dtype), kind="ExternalInput").ap()
         for k, v in arrays.items()}
    for name, shape, _ in _OUTS:
        A[name] = nc.dram_tensor("out_" + name, shape, F32, kind="ExternalOutput").ap()
    build(nc, A)
    r = _run(nc, [{"in_" + k: v for k, v in arrays.items()}], core_ids=[0])
    return tuple(r.results[0]["out_" + name].reshape(final) for name, _, final in _OUTS)
```

```python
from contextlib import ExitStack

import numpy as np

import concourse.bass as bass
from concourse import mybir

F32 = mybir.dt.float32
I32 = mybir.dt.int32
U32 = mybir.dt.uint32
ALU = mybir.AluOpType
ACT = mybir.ActivationFunctionType
AX = mybir.AxisListType.X

P = 128
D = 1024
KC = D // P
SEQ = 256
NB = 8
NTOK = SEQ + NB
HD = 64
NH = 8
DG = NH * HD
NPG = 16
PAST = NPG * P
WC = 256
WSLOTS = 4
ADA_CH, QKV_CH, OUT_CH, PQ_CH = 6 * D // WC, 6 * DG // WC, D // WC, 2 * D // WC
QA, KA, VA, QB_, KB_, VB_ = (DG * n for n in range(6))
KVP = 2
KVS = 4
CPB = NPG // KVP
TOPK = 16
NKEY = 128
NSLOT = 8
DIL_ROWS = 96
UNITS = 2 * NH + 1
PAIRS = NB * NH
SHIFT1, SCALE1 = 2, 3
GATE1, SHIFT2, SCALE2, GATE2 = range(4)
EARLY_COPIES = 2
EPS = 1e-6
SCALE = HD ** -0.5
LOWEST = -3.0e38
MASKED = -1.0e30

_CONST = {}
_at = 0
for _name, _n in (("ident", P), ("tri", P), ("ones", P), ("later", P), ("cnt", 384), ("dbias", 384),
                  ("scnt", 384), ("sbias", 384), ("rope", 48), ("hmask", DG), ("unit8", 64), ("rep8", 64), ("fold8", NB), ("iota", TOPK)):
    _CONST[_name] = (_at, _n)
    _at += _n
NCONST = _at


def constants():
    c = np.zeros((P, NCONST), np.float32)

    def put(name, a):
        at, n = _CONST[name]
        c[:a.shape[0], at:at + n] = a.reshape(a.shape[0], n)

    p, f = np.arange(P)[:, None], np.arange(P)[None, :]
    put("ident", (p == f).astype(np.float32))
    put("tri", (p >= f).astype(np.float32))
    put("ones", np.ones((P, P), np.float32))
    put("later", (p < f).astype(np.float32))

    def count(d):
        d = np.asarray(d)
        return sum(((d >= 0) & (d <= w) & (d % s == 0)).astype(np.float32) for w, s in ((128, 1), (512, 4), (2048, 16)))

    cnt = np.concatenate([count(p - f), count(P + p - f), count(p - f)], 1)
    put("cnt", cnt)
    put("dbias", np.where(cnt > 0, 0.0, MASKED).astype(np.float32))
    far = np.full(P, -1)
    mid, long = far.copy(), far.copy()
    mid[:DIL_ROWS] = 512 - 4 * np.arange(DIL_ROWS)
    mid[DIL_ROWS] = 0
    long[:DIL_ROWS] = 2048 - 16 * np.arange(DIL_ROWS)
    scnt = np.tile(count(np.concatenate([P - np.arange(P), mid, long])), (NB * NH, 1))
    put("scnt", scnt)
    put("sbias", np.where(scnt > 0, 0.0, MASKED).astype(np.float32))
    inv = np.float32(500000.0) ** (-np.arange(8, dtype=np.float32) / np.float32(8))
    pos = np.concatenate([np.arange(SEQ), np.full(P, PAST)]).astype(np.float32)
    ang = (pos[:, None] * inv[None, :]).astype(np.float32)
    rope = np.concatenate([np.cos(ang), np.sin(ang)], 1).reshape(3, P, 16).transpose(1, 0, 2)
    put("rope", np.ascontiguousarray(rope).astype(np.float32))
    put("hmask", (np.arange(NH)[:, None] == (np.arange(DG) // HD)[None, :]).astype(np.float32))
    put("unit8", np.tile(np.eye(8, dtype=np.float32).reshape(1, 64), (P, 1)))
    put("rep8", np.tile(np.eye(NB, dtype=np.float32), (1, NH)))
    put("fold8", np.tile(np.eye(NB, dtype=np.float32), (NH, 1)))
    put("iota", np.tile(np.arange(TOPK, dtype=np.float32), (P, 1)))
    return c


class Count:

    def __init__(self, sem, base=0):
        self.sem, self.base, self.n = sem, base, 0

    def inc(self, instruction):
        instruction.then_inc(self.sem, 1)
        self.n += 1

    def value(self):
        return self.base + self.n

    def wait(self, eng):
        eng.wait_ge(self.sem, self.value())


def build(nc, A):
    ctx = ExitStack()
    with ctx:
        def sb(name, shape, dt=F32):
            return ctx.enter_context(nc.sbuf_tensor(name, shape, dt))

        def sem(name):
            return ctx.enter_context(nc.semaphore(name))

        const = sb("const", [P, NCONST])

        def cst(name):
            at, n = _CONST[name]
            return const[:, at:at + n]

        ident, tri, ones, later = cst("ident"), cst("tri"), cst("ones"), cst("later")
        m_rows = sb("m_rows", [9, 4, D])
        m_all = sb("m_all", [P, 4, D])
        x = sb("x", [P, 3, D])
        H = sb("H", [P, 3, D])
        HT = sb("HT", [P, KC * NTOK])
        QKV = sb("QKV", [P, 3, 6 * DG])
        R = sb("R", [P, NSLOT, 2 * D])
        Z = sb("Z", [P, 3, NPG * NB * NH])
        nffn = sb("nffn", [9, D])
        b24 = sb("b24", [ADA_CH, WC])
        zd = sb("zd", [P, 3, NB * NH])
        zrow = sb("zrow", [NB * NH, 384])
        pd = sb("pd", [P, 3, NB * NH])
        cT = sb("cT", [P, KC, 9])
        bsel = sb("bsel", [ADA_CH, 2, 9])
        sbb = sb("sbb", [P, NH])
        gcol = sb("gcol", [P, KC])
        pages = sb("pages", [1, NB * NPG], I32)
        stat = sb("stat", [P, 32])
        ast = sb("ast", [P, 2, NPG, NH])
        selst = sb("selst", [NH, 2, NB])
        msk = sb("msk", [NH, DG])
        gall = sb("gall", [P, UNITS, TOPK])
        
        idx = sb("idx", [P, UNITS, TOPK], I32)
        idst = sb("idst", [P, 2, TOPK], I32)
        gst = sb("gst", [P, TOPK])
        dots = sb("dots", [P, TOPK])
        gel = sb("gel", [P, TOPK])
        wgt = sb("wgt", [P, TOPK])
        diag = sb("diag", [P, 4, P])

        hT = HT[:, :].rearrange("p (c n) -> p c n", c=KC)
        Rf = R[:, :, :].rearrange("p s n -> p (s n)")
        W = [R[:, s, :].rearrange("p (c n) -> p c n", c=KC) for s in range(WSLOTS)]
        KV = [Rf[:, WSLOTS * 2048 + s * 1024:WSLOTS * 2048 + (s + 1) * 1024].rearrange("p (g n) -> p g n", g=KVP)
              for s in range(KVS)]
        m_flat = m_all[:, :, :].rearrange("p s n -> p (s n)")
        DK = [m_flat[:, s * 3 * DG:(s + 1) * 3 * DG].rearrange("p (g n) -> p g n", g=3) for s in range(2)]
        subk = R[:, WSLOTS, :].rearrange("p (g n) -> p g n", g=16)
        QB = Rf[:, 6 * 2048:8 * 2048].rearrange("p (b n) -> p b n", b=NB)
        z4 = Z[:, 0, :].rearrange("p (g b h) -> p g b h", g=NPG, b=NB)
        z1, zt, zl = Z[:, 0, :], Z[:, 1, :], Z[:, 2, :]
        cwork = [Z[0:9, n, :] for n in range(3)]
        Hf = H[:, :, :].rearrange("p t n -> p (t n)")
        aw = [Hf[:, n * 768:(n + 1) * 768].rearrange("p (j n) -> p j n", j=2) for n in range(3)]
        stq = Hf[:, 2304:2560].rearrange("p (t n) -> p t n", t=2)
        stk = Hf[:, 2560:2816].rearrange("p (t n) -> p t n", t=2)
        qk = HT[:, 0:512]
        pT = HT[:, 512:1280].rearrange("p (j n) -> p j n", j=2)
        Qf = QKV[:, :, :].rearrange("p t n -> p (t n)")
        S = Qf[:, 0:UNITS * 2 * NKEY].rearrange("p (i c n) -> p i c n", i=UNITS, c=2)
        tw = Qf[:, 6144:9216]

        eq = Z[:, 0, 0:2 * 512].rearrange("p (j n) -> p j n", j=2)
        eqz = Z[:, 1, :]
        sc, rep, cand, crep, oh, oh2 = (tw[:, n * 256:(n + 1) * 256] for n in range(6))
        tsm = tw[:, 1536:2048]
        tv = [tsm[:, 0:16], tsm[:, 16:32]]
        tif = [tsm[:, 32:48], tsm[:, 48:64]]
        cv, ctop_d, ctop_e = tsm[:, 64:80], tsm[:, 80:96], tsm[:, 96:112]
        eidf, row_f, col_f, e1f, e2f = (tsm[:, 112 + 16 * n:128 + 16 * n] for n in range(5))
        tst = tsm[:, 200:204]
        tiu = [sb("tiu0", [P, TOPK], U32), sb("tiu1", [P, TOPK], U32)]
        ciu = sb("ciu", [P, TOPK], U32)
        cint = sb("cint", [P, 2, TOPK], U32)

        ps = ctx.enter_context(nc.psum_tensor("ps", [P, 8, 512], F32))

        names = """c_in x_in small_in w_used sel_ready ada_mm ada_ev bc_mm bc_ev cs_ready cT_mm cT_ev m1_ready
          h_ssq h_rt h_ready hT_mm hT_ev qkv_ev qb_mm qb_ev k_used rot_done new_out kv_out z_l z_abs z_suf
          z_s z_e zz_a dk_used qd_mm qd_ev dT_mm dm_ready de_ready dp_ready dU_mm pd_ev st_ready t_mm t_ev
          sc_mm s_l s_t s_L s_mm s_a s_e s_am o_mm o_ev d_zm d_e d_p d_tr d_pT d_o d_oe ast_ready v_used
          msk_ready oA_mm vd_used pdst_ready mskd_ready oB_mm mg_ready mg_mm mg_ev out_ev m2_ready bc2_mm
          bc2_ev pq_mm pq_ev score_mm score_ev top_done id_st g_st dot_done gel_done w_done diag_done
          e_used ff_ready f_rt y_ready y_out hr_mm hr_ev dve act
          kst dst sbs dis tks subk_in z_v topsm tope fin_in""".split()
        s = {n: sem(n) for n in names}
        w_ready = [sem(f"w_ready{n}") for n in range(WSLOTS)]
        k_ready = [sem(f"k_ready{n}") for n in range(KVS)]
        v_ready = [sem(f"v_ready{n}") for n in range(KVS)]
        dk_ready = [sem(f"dk_ready{n}") for n in range(2)]
        dv_ready = [sem(f"dv_ready{n}") for n in range(2)]
        copied = [sem(f"copied{n}") for n in range(2)]
        e_ready = [sem(f"e_ready{n}") for n in range(NSLOT)]

        TP = [P, P, NB]
        DILS = ((0, P, bass.ds(PAST - P, P)), (1, DIL_ROWS, bass.ds(PAST - 512, DIL_ROWS, step=4)),
                (2, DIL_ROWS, bass.ds(0, DIL_ROWS, step=16)))

        block = ctx.enter_context(nc.Block())

        wait_value = {eng: eng.alloc_register("wait_value") for eng in (nc.vector, nc.tensor, nc.gpsimd)}

        def wait_apart(eng, semaphore, value):
            if not isinstance(value, int):
                eng.reg_mov(wait_value[eng], value)
                value = wait_value[eng]
            eng.wait_ge(s["c_in"], 64)
            eng.wait_ge(semaphore, value)

        @block.sync
        def _(sp):
            sp.dma_start(const[:, :], A["consts"]).then_inc(s["c_in"], 16)
            sp.dma_start(cwork[0], A["c9"]).then_inc(s["c_in"], 16)
            sp.dma_start(cwork[2], A["norm_mix"].to_broadcast([9, D])).then_inc(s["c_in"], 16)
            sp.dma_start(b24[:, :], A["b_ada"]).then_inc(s["c_in"], 16)
            for t in range(3):
                sp.dma_start(x[0:TP[t], t, :], A["x"][t * P:t * P + TP[t], :]).then_inc(s["x_in"], 16)
            sp.dma_start(nffn[:, :], A["norm_ffn"].to_broadcast([9, D])).then_inc(s["small_in"], 16)
            sp.dma_start(sbb[:, :], A["sb_bias"].to_broadcast([P, NH])).then_inc(s["small_in"], 16)
            sp.dma_start(gcol[:, :], A["g_out"]).then_inc(s["small_in"], 16)
            sp.dma_start(pages[:, :], A["pages"]).then_inc(s["small_in"], 16)
            sp.wait_ge(s["small_in"], 64)

            def page_chunk(b, c, cache, ready, waits):
                for sm, v in waits:
                    sp.wait_ge(sm, v)
                for g in range(KVP):
                    page = sp.value_load(pages[0:1, bass.ds(b * NPG + c * KVP + g, 1)], min_val=0, max_val=159)
                    sp.dma_start(KV[c % KVS][:, g, :],
                                 cache[bass.ds(page, 1)].rearrange("a p n -> (a p) n")).then_inc(ready[c % KVS], 16)

            def copy_window(b):
                for m, (src, dst) in enumerate(((A["dil_k"], A["dil_k_s"]), (A["dil_v"], A["dil_v_s"]))):
                    n = (PAST - 1) * DG // 4
                    for q in range(4):
                        if not (isinstance(b, int) and b * 8 + m * 4 + q < 2):
                            sp.wait_ge(copied[q % 2], b * 64 + 16 * (m * 2 + q // 2))
                        sp.dma_start(dst[bass.ds(b, 1), bass.ds(q * n, n)].rearrange("a (r n) -> (a r) n", r=P),
                                     src[bass.ds(b, 1), bass.ds(DG + q * n, n)].rearrange("a (r n) -> (a r) n", r=P)
                                     ).then_inc(copied[q % 2], 16)

            for c in range(CPB):
                page_chunk(0, c, A["sb_k"], k_ready, [(s["k_used"], c - KVS + 1)] if c >= KVS else [])
                if c == KVS - 1:
                    for i in range(EARLY_COPIES):
                        copy_window(i)
            with sp.Fori(1, NB) as b:
                for c in range(CPB):
                    page_chunk(b, c, A["sb_k"], k_ready, [(s["k_used"], b * CPB + (c - KVS + 1))])

            sp.wait_ge(s["rot_done"], 1)
            sp.dma_start(A["dil_k_s"][:, (PAST - 1) * DG:], QKV[0:NB, 2, KB_:KB_ + DG]).then_inc(s["new_out"], 16)
            sp.dma_start(A["dil_v_s"][:, (PAST - 1) * DG:], QKV[0:NB, 2, VB_:VB_ + DG]).then_inc(s["new_out"], 16)
            for name, col in (("sb_k", KA), ("sb_v", VA), ("dil_k", KB_), ("dil_v", VB_)):
                for t in range(2):
                    sp.dma_start(A[name + "_p"][t * P:(t + 1) * P, :], QKV[:, t, col:col + DG]).then_inc(s["kv_out"], 16)
            for name, col in (("sb_k_n", KA), ("sb_v_n", VA)):
                sp.dma_start(A[name], QKV[0:NB, 2, col:col + DG]).then_inc(s["kv_out"], 16)
            sp.wait_ge(s["new_out"], 32)
            sp.wait_ge(s["h_ready"], 3)

            def window_keys(b, slot, src, new, ready, waits):
                for sm, v in waits:
                    sp.wait_ge(sm, v)
                rows = src[bass.ds(b, 1), :].rearrange("a (r n) -> (a r) n", n=DG)
                for g, n, sel in DILS:
                    sp.dma_start(DK[slot][0:n, g, :], rows[sel, :]).then_inc(ready[slot], 16)
                sp.dma_start(DK[slot][DIL_ROWS:DIL_ROWS + 1, 1, :],
                             new[bass.ds(b, 1), (PAST - 1) * DG:]).then_inc(ready[slot], 16)

            def value_pages(b, first=False):
                for c in range(CPB):
                    page_chunk(b, c, A["sb_v"], v_ready,
                               [] if first and c < KVS else [(s["v_used"], b * CPB + (c - KVS + 1))])

            for b in range(2):
                window_keys(b, b, A["dil_k"], A["dil_k_s"], dk_ready, [])
            sp.wait_ge(s["k_used"], NB * CPB)
            value_pages(0, first=True)
            with sp.Fori(1, NB // 2) as i:
                for j in range(2):
                    window_keys(i * 2 + j, j, A["dil_k"], A["dil_k_s"], dk_ready, [(s["dk_used"], i * 2 + (j - 1))])
                    value_pages(i * 2 + (j - 1))
            value_pages(NB - 1)
            for b in range(2):
                window_keys(b, b, A["dil_v"], A["dil_v_s"], dv_ready, [(s["dk_used"], NB)])
            with sp.Fori(1, NB // 2) as i:
                for j in range(2):
                    window_keys(i * 2 + j, j, A["dil_v"], A["dil_v_s"], dv_ready, [(s["vd_used"], i * 2 + (j - 1))])
            sp.wait_ge(s["v_used"], NB * CPB)
            sp.dma_start(subk, A["subk"].rearrange("p (g n) -> p g n", g=16)).then_inc(s["subk_in"], 16)
            with sp.Fori(EARLY_COPIES, NB) as i:
                copy_window(i)
            sp.wait_ge(s["h_ready"], 6)
            sp.dma_start(m_all[:, SHIFT2, :], A["norm_final"].to_broadcast([P, D])).then_inc(s["fin_in"], 16)
            for n, (t, dst) in enumerate(((0, A["y_p"][0:P, :]), (1, A["y_p"][P:SEQ, :]), (2, A["y_s"]))):
                sp.wait_ge(s["y_ready"], n + 1)
                sp.dma_start(dst, H[0:TP[t], t, :]).then_inc(s["y_out"], 16)
            sp.wait_ge(s["kv_out"], 16 * 10)
            for n in range(2):
                sp.wait_ge(copied[n], 16 * 4 * NB)
            sp.wait_ge(s["y_out"], 48)

        @block.gpsimd
        def _(pool):
            rounds = (ADA_CH + QKV_CH + OUT_CH + PQ_CH) // WSLOTS
            for k in range(WSLOTS):
                pool.dma_start(R[:, k, :], A["wts"][k]).then_inc(w_ready[k], 16)
            with pool.Fori(1, rounds) as r:
                for k in range(WSLOTS):
                    pool.wait_ge(s["w_used"], r * WSLOTS + (k - WSLOTS + 1))
                    pool.dma_start(R[:, k, :], A["wts"][bass.ds(r * WSLOTS + k, 1)].rearrange("a p n -> (a p) n")
                                   ).then_inc(w_ready[k], 16)

            def head_rows(i, par, first):
                pool.wait_ge(s["top_done"], i + 1)
                pool.tensor_copy(idst[:, par, :], idx[:, bass.ds(i, 1), :].rearrange("p a n -> p (a n)")
                                 ).then_inc(s["id_st"], 1)
                wait_apart(pool, s["id_st"], i + 1)
                for k in range(TOPK):
                    if not (first and k < NSLOT):
                        wait_apart(pool, s["e_used"], i * TOPK + (k - NSLOT + 1))
                    pool.indirect_dma_start(
                        out=R[:, k % NSLOT, :], out_offset=None, in_=A["uv"],
                        in_offset=bass.IndirectOffsetOnAxis(ap=idst[:, par, k:k + 1], axis=0),
                    ).then_inc(e_ready[k % NSLOT], 16)

            head_rows(0, 0, True)
            head_rows(1, 1, False)
            with pool.Fori(1, NH) as i:
                head_rows(i * 2, 0, False)
                head_rows(i * 2 + 1, 1, False)
            pool.wait_ge(s["top_done"], UNITS)
            pool.tensor_copy(idst[:, 0, :], idx[:, UNITS - 1, :]).then_inc(s["id_st"], 1)
            pool.wait_ge(s["id_st"], UNITS)
            for k in range(TOPK):
                pool.wait_ge(s["e_used"], (UNITS - 1) * TOPK + (k - NSLOT + 1))
                pool.indirect_dma_start(
                    out=R[0:PAIRS, k % NSLOT, :], out_offset=None, in_=A["uv"],
                    in_offset=bass.IndirectOffsetOnAxis(ap=idst[0:PAIRS, 0, k:k + 1], axis=0),
                ).then_inc(e_ready[k % NSLOT], 16)

        @block.tensor
        def _(pe):
            def w_round(r, k):
                pe.wait_ge(w_ready[k], r * 16 + 16)

            pe.wait_ge(s["c_in"], 64)
            pe.wait_ge(s["cs_ready"], 1)
            for c in range(KC):
                last = pe.transpose(ps[:, 7, c * 9:(c + 1) * 9], cwork[0][:, c * P:(c + 1) * P], ident[0:9, 0:9])
            last.then_inc(s["cT_mm"], 1)
            pe.wait_ge(s["cT_ev"], 1)

            def ada_chunk(r, first, sel, k, bank):
                w_round(r + first, k)
                pe.wait_ge(s["sel_ready"], (r + sel) * WSLOTS + (k + 1))
                out = ps[0:9, bank + k % 2, 0:WC]
                for c in range(KC):
                    last = pe.matmul(out, cT[:, c, :], W[k][:, c, :], start=(c == 0), stop=False)
                last.then_inc(s["w_used"], 1)
                pe.matmul(out, bsel[:, k % 2, :], b24[:, :], start=False, stop=True).then_inc(s["ada_mm"], 1)

            def spread_rows(order, ready, value, mm, ev):
                pe.wait_ge(ready, value)
                n = 0
                for slot in order:
                    for h in range(2):
                        if n >= 4:
                            pe.wait_ge(ev, n - 3)
                        pe.matmul(ps[:, 4 + n % 4, :], ident[0:9, 8:9].to_broadcast([9, P]),
                                  m_rows[:, slot, h * 512:(h + 1) * 512], start=True, stop=True).then_inc(mm, 1)
                        n += 1

            def turn(n0, ready, mm, ev):
                for t in range(3):
                    pe.wait_ge(ready, n0 + t + 1)
                    if t < 2:
                        for half in range(2):
                            for c in range(4):
                                last = pe.transpose(ps[:, 2 * t + half, c * P:(c + 1) * P],
                                                    H[:, t, (4 * half + c) * P:(4 * half + c + 1) * P], ident)
                            last.then_inc(mm, 1)
                    else:
                        for c in range(KC):
                            last = pe.transpose(ps[:, 4, c * NB:(c + 1) * NB], H[0:NB, t, c * P:(c + 1) * P],
                                                ident[0:NB, 0:NB])
                        last.then_inc(mm, 1)

            def project(base, r, k, ev, wait_ev):
                w_round(base // WSLOTS + r, k)
                if wait_ev is not None:
                    pe.wait_ge(ev, wait_ev)
                for t in range(3):
                    out = ps[0:TP[t], 2 * (k % 2) + t // 2, (t % 2) * WC:(t % 2 + 1) * WC]
                    for c in range(KC):
                        last = pe.matmul(out, hT[:, c, t * P:t * P + TP[t]], W[k][:, c, :],
                                         start=(c == 0), stop=(c == KC - 1))
                    if t == 2:
                        last.then_inc(s["w_used"], 1)

            with pe.Fori(0, 2) as r:
                for k in range(WSLOTS):
                    ada_chunk(r, 0, 0, k, 0)
            spread_rows((SHIFT1, SCALE1), s["m1_ready"], 1, s["bc_mm"], s["bc_ev"])
            turn(0, s["h_ready"], s["hT_mm"], s["hT_ev"])
            pe.wait_ge(s["hT_ev"], 5)
            base = 8
            for k in range(WSLOTS):
                project(base, 0, k, s["qkv_ev"], k - 1 if k >= 2 else None)
            pe.wait_ge(s["qkv_ev"], 4)
            for b in range(NB):
                if b >= 4:
                    pe.wait_ge(s["qb_ev"], b - 3)
                pe.matmul(ps[:, 4 + b % 4, :], ident[0:NB, b:b + 1].to_broadcast([NB, P]), QKV[0:NB, 2, QA:QA + DG],
                          start=True, stop=True).then_inc(s["qb_mm"], 1)
            with pe.Fori(1, QKV_CH // WSLOTS) as r:
                for k in range(WSLOTS):
                    project(base, r, k, s["qkv_ev"], r * WSLOTS + (k - 1))
            pe.wait_ge(s["qkv_ev"], QKV_CH)
            def turn_pair(i):
                pe.wait_ge(s["st_ready"], i + 1)
                for n, st in enumerate((stq, stk)):
                    for t in range(2):
                        last = pe.transpose(ps[:, 0, (2 * n + t) * P:(2 * n + t + 1) * P], st[:, t, :], ident)
                last.then_inc(s["t_mm"], 1)
                pe.wait_ge(s["t_ev"], i + 1)

            with pe.Fori(0, NH // 2) as g:
                turn_pair(g)
                for j in range(2):
                    f = slice(64 * j, 64 * j + 64)
                    pe.matmul(ps[:, 1 + j, 0:256], qk[f, 256:384], qk[f, 0:256], start=True, stop=True)
                    last = pe.matmul(ps[:, 1 + j, 256:384], qk[f, 384:512], qk[f, 128:256], start=True, stop=True)
                last.then_inc(s["sc_mm"], 1)
                for k in range(2):
                    ada_chunk(g, 5, 2, k, 6)
                pe.wait_ge(s["s_L"], g + 1)
                for j in range(2):
                    L = aw[1][:, j, :]
                    pe.matmul(ps[:, 3 + j, 0:128], tri, L[:, 0:128], start=True, stop=True)
                    pe.matmul(ps[:, 3 + j, 128:256], tri, L[:, 128:256], start=True, stop=False)
                    pe.matmul(ps[:, 3 + j, 128:256], ones, L[:, 256:384], start=False, stop=True)
                    last = pe.matmul(ps[:, 3 + j, 256:384], tri, L[:, 256:384], start=True, stop=True)
                last.then_inc(s["s_mm"], 1)
                for k in range(2, 4):
                    ada_chunk(g, 5, 2, k, 6)
                pe.wait_ge(s["s_am"], g + 1)
                for j in range(2):
                    o0, o1 = ps[:, 5, j * HD:(j + 1) * HD], ps[:, 5, P + j * HD:P + (j + 1) * HD]
                    v = [QKV[:, t, bass.ds(VA + j * HD + g * P, HD)] for t in range(2)]
                    pe.matmul(o0, aw[2][:, j, 0:128], v[0], start=True, stop=True)
                    pe.matmul(o1, aw[2][:, j, 128:256], v[0], start=True, stop=False)
                    last = pe.matmul(o1, aw[2][:, j, 256:384], v[1], start=False, stop=True)
                last.then_inc(s["o_mm"], 1)
                pe.wait_ge(s["o_ev"], g + 1)

            pe.wait_ge(s["k_used"], NB * CPB)
            pe.wait_ge(s["ada_ev"], ADA_CH)
            for b in range(NB):
                if b >= 4:
                    pe.wait_ge(s["qd_ev"], b - 3)
                pe.matmul(ps[:, 4 + b % 4, :], ident[0:NB, b:b + 1].to_broadcast([NB, P]), QKV[0:NB, 2, QB_:QB_ + DG],
                          start=True, stop=True).then_inc(s["qd_mm"], 1)
            pe.wait_ge(s["z_suf"], 1)
            for half in range(2):
                c = slice(half * 512, (half + 1) * 512)
                pe.matmul(ps[:, 1 + half, :], tri, zl[:, c], start=True, stop=False)
                last = pe.matmul(ps[:, 1 + half, :], ones, zt[:, c], start=False, stop=True)
            last.then_inc(s["z_s"], 1)
            pe.wait_ge(s["z_e"], 1)
            pe.wait_ge(s["qd_ev"], NB)

            def add_row(bank, j, first):
                return pe.matmul(ps[0:NB, bank, :], selst[:, j, :], msk[:, :], start=first, stop=True,
                                 skip_group_check=True)

            def pages_pv(i, j):
                pe.wait_ge(s["ast_ready"], i + 1)
                for c in range(CPB):
                    pe.wait_ge(v_ready[c % KVS], (i * 2 + (c // KVS + 1)) * 32)
                    for g in range(KVP):
                        last = pe.matmul(ps[0:NH, 6 + j, :], ast[:, j, c * KVP + g, :], KV[c % KVS][:, g, :],
                                         start=(c + g == 0), stop=(c * KVP + g == NPG - 1))
                    last.then_inc(s["v_used"], 1)

            def pages_row(i, j, first=False):
                wait_apart(pe, s["msk_ready"], i + 1)
                add_row(3, j, first).then_inc(s["oA_mm"], 1)

            def dilated_pair(g, first=False):
                turn_pair(g + 4)
                for j in range(2):
                    f = slice(64 * j, 64 * j + 64)
                    pe.matmul(ps[:, 1 + j, 0:128], qk[f, 0:128], qk[f, 256:384], start=True, stop=True)
                    last = pe.matmul(ps[:, 1 + j, 128:384], qk[f, 128:256], qk[f, 256:512], start=True, stop=True)
                last.then_inc(s["sc_mm"], 1)
                pages_pv(g * 2, 0)
                pe.wait_ge(s["d_p"], g + 1)
                for j in range(2):
                    for n in range(3):
                        last = pe.transpose(ps[:, 1 + j, n * P:(n + 1) * P], aw[0][:, j, n * P:(n + 1) * P], ident)
                last.then_inc(s["d_tr"], 1)
                pages_row(g * 2, 0, first)
                pages_pv(g * 2 + 1, 1)
                pe.wait_ge(s["d_pT"], g + 1)
                for j in range(2):
                    o0, o1 = ps[:, 5, j * HD:(j + 1) * HD], ps[:, 5, P + j * HD:P + (j + 1) * HD]
                    v = [QKV[:, t, bass.ds(VB_ + j * HD + g * P, HD)] for t in range(2)]
                    pe.matmul(o0, pT[:, j, 0:128], v[0], start=True, stop=True)
                    pe.matmul(o1, pT[:, j, 128:256], v[0], start=True, stop=False)
                    last = pe.matmul(o1, pT[:, j, 256:384], v[1], start=False, stop=True)
                last.then_inc(s["d_o"], 1)
                pages_row(g * 2 + 1, 1)
                pe.wait_ge(s["d_oe"], g + 1)

            dilated_pair(0, first=True)
            with pe.Fori(1, NH // 2) as g:
                dilated_pair(g)

            pe.wait_ge(s["dk_used"], NB)
            for g in range(3):
                last = pe.transpose(ps[0:64, 6, g * P:(g + 1) * P], zd[:, g, :], ident)
            last.then_inc(s["dT_mm"], 1)
            pe.wait_ge(s["dp_ready"], 1)
            for g in range(3):
                last = pe.transpose(ps[:, 7, g * 64:(g + 1) * 64], zrow[:, g * P:(g + 1) * P], ident[0:64, 0:64])
            last.then_inc(s["dU_mm"], 1)
            pe.wait_ge(s["pd_ev"], 1)

            def window_pv(i, j, value):
                pe.wait_ge(s["pdst_ready"], i + 1)
                pe.wait_ge(dv_ready[j], value)
                for g, n in ((0, P), (1, DIL_ROWS + 1), (2, DIL_ROWS)):
                    last = pe.matmul(ps[0:NH, 6 + j, :], ast[0:n, j, g, :], DK[j][0:n, g, :],
                                     start=(g == 0), stop=(g == 2))
                last.then_inc(s["vd_used"], 1)

            def window_row(i, j, first=False):
                wait_apart(pe, s["mskd_ready"], i + 1)
                add_row(4, j, first).then_inc(s["oB_mm"], 1)

            window_pv(0, 0, 64)
            window_pv(1, 1, 64)
            window_row(0, 0, first=True)
            with pe.Fori(1, NB // 2) as i:
                window_pv(i * 2, 0, i * 64 + 64)
                window_row(i * 2 - 1, 1)
                window_pv(i * 2 + 1, 1, i * 64 + 64)
                window_row(i * 2, 0)
            window_row(NB - 1, 1)

            spread_rows((GATE1, SHIFT2, SCALE2, GATE2), s["m2_ready"], 1, s["bc2_mm"], s["bc2_ev"])
            pe.wait_ge(s["bc2_ev"], 8)
            turn(0, s["mg_ready"], s["mg_mm"], s["mg_ev"])
            pe.wait_ge(s["mg_ev"], 5)
            for k in range(WSLOTS):
                project(ADA_CH + QKV_CH, 0, k, s["out_ev"], k - 1 if k >= 2 else None)
            pe.wait_ge(s["out_ev"], OUT_CH)
            turn(3, s["h_ready"], s["hT_mm"], s["hT_ev"])
            pe.wait_ge(s["hT_ev"], 10)

            pe.wait_ge(s["subk_in"], 16)
            base = ADA_CH + QKV_CH + OUT_CH

            def query_group(r, k, j, first):
                m = r * 8 + (2 * k + j)
                if j == 0:
                    w_round(base // WSLOTS + r, k)
                if not (first and 2 * k + j < 2):
                    pe.wait_ge(s["pq_ev"], m - 1)
                for c in range(KC):
                    last = pe.matmul(ps[:, j, 0:NTOK], W[k][:, c, j * P:(j + 1) * P], hT[:, c, :],
                                     start=(c == 0), stop=(c == KC - 1))
                last.then_inc(s["w_used"] if j else s["pq_mm"], 1)

            def score_group(r, k, j, first):
                m = r * 8 + (2 * k + j)
                pe.wait_ge(s["pq_ev"], m + 1)
                if not (first and 2 * k + j < 2):
                    pe.wait_ge(s["score_ev"], m - 1)
                for t in range(2):
                    last = pe.matmul(ps[:, 2 + j, t * P:(t + 1) * P], eq[:, j, t * P:(t + 1) * P],
                                     subk[:, bass.ds(m, 1), :].rearrange("p a n -> p (a n)"), start=True, stop=True)
                last.then_inc(s["score_mm"], 1)

            def pq_round(r, first):
                for k in range(WSLOTS):
                    for j in range(2):
                        query_group(r, k, j, first)
                    for j in range(2):
                        score_group(r, k, j, first)

            pq_round(0, True)
            with pe.Fori(1, 2) as r:
                pq_round(r, False)
            pe.wait_ge(s["pq_ev"], 16)
            for j in range(2):
                for h in range(NH):
                    m = 2 * h + j
                    last = pe.matmul(ps[0:PAIRS, 0, j * NKEY:(j + 1) * NKEY], eqz[:, m * PAIRS:(m + 1) * PAIRS],
                                     subk[:, m, :], start=(h == 0), stop=(h == NH - 1))
            last.then_inc(s["score_mm"], 1)
            for q in range(2):
                last = pe.matmul(ps[0:PAIRS, 6 + q, :], cst("rep8")[0:NB, :], H[0:NB, 2, q * 512:(q + 1) * 512],
                                 start=True, stop=True)
            last.then_inc(s["hr_mm"], 1)
            pe.wait_ge(s["hr_ev"], 1)
            pe.wait_ge(s["score_ev"], 17)

            def experts(t, banks):
                for q in range(2):
                    pe.matmul(ps[:, banks + q, :], zeroP, H[:, t, q * 512:(q + 1) * 512], start=True, stop=False,
                              skip_group_check=True)
                with pe.Fori(0, NH) as h:
                    for k in range(TOPK):
                        pe.wait_ge(s["diag_done"], h * TOPK + (t * 128 + k + 1))
                        for q in range(2):
                            last = pe.matmul(ps[:, banks + q, :], diag[:, k % 4, :],
                                             R[:, k % NSLOT, D + q * 512:D + (q + 1) * 512],
                                             start=False, stop=False, skip_group_check=True)
                        last.then_inc(s["e_used"], 1)

            zeroP = tw[:, 2048:2048 + P]
            pe.wait_ge(s["z_v"], 1)
            experts(0, 4)
            experts(1, 6)

            for k in range(TOPK):
                pe.wait_ge(s["diag_done"], (UNITS - 1) * TOPK + k + 1)
                for q in range(2):
                    last = pe.matmul(ps[0:NB, q, :], diag[0:PAIRS, k % 4, 0:NB],
                                     R[0:PAIRS, k % NSLOT, D + q * 512:D + (q + 1) * 512],
                                     start=(k == 0), stop=(k == TOPK - 1))
                last.then_inc(s["e_used"], 1)

        @block.scalar
        def _(act):
            act.wait_ge(s["c_in"], 64)
            act.activation(cwork[1], cwork[0], ACT.Exp, scale=-1.0).then_inc(s["act"], 1)
            act.wait_ge(s["cT_mm"], 1)
            act.activation(cT[:, :, :], ps[:, 7, 0:72].rearrange("p (c n) -> p c n", c=KC), ACT.Copy
                           ).then_inc(s["cT_ev"], 1)

            def stage_sel(a, k):
                act.activation(bsel[:, k % 2, :], ident[0:ADA_CH, bass.ds(a, 1)].to_broadcast([ADA_CH, 9]), ACT.Copy
                               ).then_inc(s["sel_ready"], 1)

            def ada_ev(r, sel, k, slot, bank):
                a = (r + sel) * WSLOTS + k
                act.wait_ge(s["ada_mm"], a + 1)
                act.activation(m_rows[:, bass.ds(slot, 1), k * WC:(k + 1) * WC].rearrange("p a n -> p (a n)"),
                               ps[0:9, bank + k % 2, 0:WC], ACT.Copy).then_inc(s["ada_ev"], 1)
                stage_sel(a + 2, k)

            stage_sel(0, 0)
            stage_sel(1, 1)
            with act.Fori(0, 2) as r:
                for k in range(WSLOTS):
                    ada_ev(r, 0, k, r + SHIFT1, 0)

            def spread_ev(order, mm, ev):
                for n, slot in enumerate(q for q in order for _ in range(2)):
                    act.wait_ge(mm, n + 1)
                    act.activation(m_all[:, slot, (n % 2) * 512:(n % 2 + 1) * 512], ps[:, 4 + n % 4, :], ACT.Copy
                                   ).then_inc(ev, 1)

            spread_ev((SHIFT1, SCALE1), s["bc_mm"], s["bc_ev"])

            act.wait_ge(s["h_ssq"], 1)
            act.activation(stat[:, 4:7], stat[:, 0:3], ACT.Sqrt).then_inc(s["h_rt"], 1)

            def turn_ev(n0, mm, ev):
                for n in range(5):
                    act.wait_ge(mm, n0 + n + 1)
                    if n < 4:
                        t, half = divmod(n, 2)
                        act.activation(hT[:, 4 * half:4 * half + 4, t * P:(t + 1) * P],
                                       ps[:, n, :].rearrange("p (c n) -> p c n", c=4), ACT.Copy).then_inc(ev, 1)
                    else:
                        act.activation(hT[:, :, SEQ:NTOK], ps[:, 4, 0:64].rearrange("p (c n) -> p c n", c=KC), ACT.Copy
                                       ).then_inc(ev, 1)

            turn_ev(0, s["hT_mm"], s["hT_ev"])

            def qkv_ev(r, k):
                n = r * WSLOTS + k
                act.wait_ge(s["w_used"], n + (8 + 1))
                act.activation(QKV[:, 0:2, bass.ds(n * WC, WC)],
                               ps[:, 2 * (k % 2), :].rearrange("p (t n) -> p t n", t=2), ACT.Copy)
                act.activation(QKV[0:NB, 2, bass.ds(n * WC, WC)], ps[0:NB, 2 * (k % 2) + 1, 0:WC], ACT.Copy
                               ).then_inc(s["qkv_ev"], 1)

            for k in range(WSLOTS):
                qkv_ev(0, k)

            def queries_ev(mm, ev):
                for b in range(NB):
                    act.wait_ge(mm, b + 1)
                    act.activation(QB[:, b, :], ps[:, 4 + b % 4, :], ACT.Copy).then_inc(ev, 1)

            queries_ev(s["qb_mm"], s["qb_ev"])
            with act.Fori(1, QKV_CH // WSLOTS) as r:
                for k in range(WSLOTS):
                    qkv_ev(r, k)
            def stage_pair(i, g, colq, colk):
                act.activation(stq, QKV[:, 0:2, bass.ds(colq + g * P, P)], ACT.Copy)
                act.activation(stk, QKV[:, 0:2, bass.ds(colk + g * P, P)], ACT.Copy).then_inc(s["st_ready"], 1)
                act.wait_ge(s["t_mm"], i + 1)
                act.activation(qk, ps[:, 0, :], ACT.Copy).then_inc(s["t_ev"], 1)

            act.wait_ge(s["rot_done"], 1)
            with act.Fori(0, NH // 2) as g:
                stage_pair(g, g, QA, KA)
                act.wait_ge(s["s_l"], g * 2 + 2)
                st = Count(s["s_t"], g * 3)
                st.inc(act.activation(aw[1], aw[0], ACT.Abs))
                st.wait(act)
                st.inc(act.activation(aw[1], aw[1], ACT.Exp, scale=-1.0))
                st.wait(act)
                st.inc(act.activation(aw[1], aw[1], ACT.Ln, bias=1.0))
                for k in range(2):
                    ada_ev(g, 2, k, g, 6)
                act.wait_ge(s["s_a"], g * 2 + 2)
                act.activation(aw[2], aw[2], ACT.Exp).then_inc(s["s_e"], 1)
                for k in range(2, 4):
                    ada_ev(g, 2, k, g, 6)

            act.wait_ge(s["z_l"], 1)
            steps = Count(s["z_abs"])
            steps.inc(act.activation(zt, z1, ACT.Abs))
            steps.wait(act)
            steps.inc(act.activation(zt, zt, ACT.Exp, scale=-1.0))
            steps.wait(act)
            steps.inc(act.activation(zt, zt, ACT.Ln, bias=1.0))
            queries_ev(s["qd_mm"], s["qd_ev"])
            act.wait_ge(s["z_e"], 1)
            act.activation(z1, z1, ACT.Exp).then_inc(s["zz_a"], 1)

            def stage_b(i, j, first, src, ready, used):
                if not first:
                    act.wait_ge(used, i - 1)
                act.activation(ast[:, j, 0:src.shape[1], :], src[:, :, bass.ds(i * NH, NH)], ACT.Copy)
                act.activation(selst[:, j, :], cst("unit8")[0:NH, bass.ds(i * NB, NB)], ACT.Copy).then_inc(ready, 1)

            zsrc = Z[:, 0, :].rearrange("p (g n) -> p g n", g=NPG)
            act.wait_ge(s["zz_a"], 1)

            def dilated_pair(g, first=False):
                stage_pair(g + 4, g, QB_, KB_)
                for j in range(2):
                    stage_b(g * 2 + j, j, first, zsrc, s["ast_ready"], s["oA_mm"])
                act.wait_ge(s["d_zm"], g + 1)
                for j in range(2):
                    for n, c in enumerate((slice(0, 128), slice(128, 384))):
                        last = act.activation(aw[0][:, j, c], aw[0][:, j, c], ACT.Exp,
                                              bias=stat[:, 20 + 2 * j + n:21 + 2 * j + n], scale=SCALE)
                last.then_inc(s["d_e"], 1)
                act.wait_ge(s["d_tr"], g + 1)
                act.activation(pT, ps[:, 1:3, 0:384], ACT.Copy).then_inc(s["d_pT"], 1)

            dilated_pair(0, first=True)
            with act.Fori(1, NH // 2) as g:
                dilated_pair(g)

            act.wait_ge(s["dm_ready"], 1)
            act.activation(zrow[:, :], zrow[:, :], ACT.Exp, bias=stat[0:64, 9:10], scale=SCALE).then_inc(s["de_ready"], 1)
            act.wait_ge(s["dU_mm"], 1)
            act.activation(pd[:, :, :], ps[:, 7, 0:192].rearrange("p (g n) -> p g n", g=3), ACT.Copy).then_inc(s["pd_ev"], 1)
            act.wait_ge(s["pd_ev"], 1)
            act.wait_ge(s["oA_mm"], NB)
            stage_b(0, 0, True, pd[:, :, :], s["pdst_ready"], s["oB_mm"])
            stage_b(1, 1, True, pd[:, :, :], s["pdst_ready"], s["oB_mm"])
            with act.Fori(1, NB // 2) as i:
                for j in range(2):
                    stage_b(i * 2 + j, j, False, pd[:, :, :], s["pdst_ready"], s["oB_mm"])

            spread_ev((GATE1, SHIFT2, SCALE2, GATE2), s["bc2_mm"], s["bc2_ev"])
            act.wait_ge(s["ff_ready"], 1)
            act.activation(stat[:, 4:10], stat[:, 10:16], ACT.Sqrt).then_inc(s["f_rt"], 1)
            act.wait_ge(s["h_ssq"], 2)
            act.activation(stat[:, 4:7], stat[:, 0:3], ACT.Sqrt).then_inc(s["h_rt"], 1)
            turn_ev(5, s["hT_mm"], s["hT_ev"])

            def pq_ev(r, k, first):
                for j in range(2):
                    m = r * 8 + (2 * k + j)
                    if j == 0:
                        act.wait_ge(s["pq_mm"], r * 4 + (k + 1))
                    else:
                        act.wait_ge(s["w_used"], r * 4 + (ADA_CH + QKV_CH + OUT_CH + k + 1))
                    if not (first and k == 0):
                        act.wait_ge(s["score_mm"], m - 1)
                    act.activation(eqz[:, bass.ds(r * (4 * (2 * PAIRS + NB)) + (k * (2 * PAIRS + NB) + j * PAIRS), NB)],
                                   ps[:, j, SEQ:NTOK], ACT.Copy)
                    act.activation(eq[:, j, 0:SEQ], ps[:, j, 0:SEQ], ACT.Copy).then_inc(s["pq_ev"], 1)
                for j in range(2):
                    m = r * 8 + (2 * k + j)
                    h = r * 4 + k
                    act.wait_ge(s["score_mm"], m + 1)
                    act.activation(S[:, bass.ds(h, 2, step=NH), j, :],
                                   ps[:, 2 + j, 0:256].rearrange("p (t n) -> p t n", t=2), ACT.Copy
                                   ).then_inc(s["score_ev"], 1)

            act.wait_ge(s["z_v"], 1)
            for k in range(WSLOTS):
                pq_ev(0, k, True)
            with act.Fori(1, 2) as r:
                for k in range(WSLOTS):
                    pq_ev(r, k, False)
            act.wait_ge(s["score_mm"], 17)
            act.activation(S[0:PAIRS, UNITS - 1, :, :], ps[0:PAIRS, 0, 0:2 * NKEY].rearrange("p (c n) -> p c n", c=2),
                           ACT.Copy).then_inc(s["score_ev"], 1)
            act.wait_ge(s["hr_mm"], 1)
            act.activation(H[0:PAIRS, 2, :].rearrange("p (a n) -> p a n", a=2), ps[0:PAIRS, 6:8, :], ACT.Copy
                           ).then_inc(s["hr_ev"], 1)

            def top_exp(i):
                act.wait_ge(s["topsm"], i + 1)
                act.activation(ctop_e, ctop_d, ACT.Exp).then_inc(s["tope"], 1)

            def weights(i):
                act.wait_ge(s["top_done"], i + 1)
                act.activation(gst[:, :], gall[:, bass.ds(i, 1), :].rearrange("p a n -> p (a n)"), ACT.Copy
                               ).then_inc(s["g_st"], 1)
                act.wait_ge(s["g_st"], i + 1)
                for k in range(0, TOPK, 2):
                    act.wait_ge(s["dot_done"], i * TOPK + (k + 2))
                    act.activation(gel[:, k:k + 2], dots[:, k:k + 2], ACT.Gelu_apprx_tanh).then_inc(s["gel_done"], 1)
                    act.wait_ge(s["gel_done"], i * (TOPK // 2) + (k // 2 + 1))
                    for q in range(2):
                        last = act.activation(wgt[:, k + q:k + q + 1], gel[:, k + q:k + q + 1], ACT.Copy,
                                              scale=gst[:, k + q:k + q + 1])
                    last.then_inc(s["w_done"], 1)
                    act.wait_ge(s["w_done"], i * (TOPK // 2) + (k // 2 + 1))
                    for q in range(2):
                        yield k + q

            def head_weights(i, first=False, top=None, decode=False):
                for k in weights(i):
                    if not (first and k < 4):
                        act.wait_ge(s["e_used"], i * TOPK + (k - 3))
                    if decode:
                        act.activation(diag[0:PAIRS, k % 4, 0:NB], cst("fold8")[0:PAIRS, :], ACT.Copy,
                                       scale=wgt[0:PAIRS, k:k + 1]).then_inc(s["diag_done"], 1)
                    else:
                        act.activation(diag[:, k % 4, :], ident, ACT.Copy, scale=wgt[:, k:k + 1]
                                       ).then_inc(s["diag_done"], 1)
                    if top is not None and k == 13:
                        top_exp(top)

            def final_root(t):
                act.wait_ge(s["ff_ready"], t + 2)
                act.activation(stat[0:TP[t], 17:18], stat[0:TP[t], 16:17], ACT.Sqrt).then_inc(s["f_rt"], 1)

            top_exp(0)
            top_exp(1)
            head_weights(0, first=True, top=2)
            with act.Fori(1, NH) as h:
                head_weights(h, top=h + 2)
            final_root(0)
            with act.Fori(0, NH - 1) as h:
                head_weights(h + 8, top=h + 10)
            head_weights(2 * NH - 1)
            head_weights(2 * NH, decode=True)
            final_root(1)
            final_root(2)

        @block.vector
        def _(dve):
            ch = Count(s["dve"])

            def step(ins):
                ch.inc(ins)
                ch.wait(dve)

            dve.wait_ge(s["act"], 1)
            dve.wait_ge(s["c_in"], 64)
            step(dve.tensor_scalar(cwork[1], cwork[1], 1.0, None, ALU.add))
            step(dve.reciprocal(cwork[1], cwork[1]))
            dve.tensor_tensor(cwork[0], cwork[0], cwork[1], ALU.mult).then_inc(s["cs_ready"], 1)
            dve.wait_ge(s["ada_ev"], 8)
            dve.scalar_tensor_tensor(m_rows[:, SCALE1, :], m_rows[:, SCALE1, :], 1.0, cwork[2], ALU.add, ALU.mult
                                     ).then_inc(s["m1_ready"], 1)

            def sums(n):
                for t in range(3):
                    last = dve.tensor_tensor_reduce(H[0:TP[t], t, :], x[0:TP[t], t, :], x[0:TP[t], t, :], 1.0, 0.0,
                                                    ALU.mult, ALU.add, stat[0:TP[t], t:t + 1])
                step(last)
                dve.tensor_scalar(stat[:, 0:3], stat[:, 0:3], 1.0 / D, EPS, ALU.mult, ALU.add).then_inc(s["h_ssq"], 1)
                dve.wait_ge(s["h_rt"], n)
                step(dve.reciprocal(stat[:, 0:3], stat[:, 4:7]))

            def modulate(scale, shift):
                for t in range(3):
                    n = TP[t]
                    a, b = (m_all[:, scale, :], m_all[:, shift, :]) if t < 2 else (m_rows[0:NB, scale, :], m_rows[0:NB, shift, :])
                    step(dve.scalar_tensor_tensor(H[0:n, t, :], x[0:n, t, :], stat[0:n, t:t + 1], a, ALU.mult, ALU.mult))
                    dve.tensor_tensor(H[0:n, t, :], H[0:n, t, :], b, ALU.add).then_inc(s["h_ready"], 1)

            dve.memset(m_all[:, 0:2, :], 0.0)
            step(dve.memset(stat[:, :], 0.0))
            dve.wait_ge(s["x_in"], 48)
            sums(1)
            dve.wait_ge(s["m1_ready"], 1)
            dve.wait_ge(s["bc_ev"], 4)
            modulate(SCALE1, SHIFT1)

            dve.wait_ge(s["qb_ev"], NB)
            def page_scores(b, chunks):
                kc = Count(s["kst"], b * CPB + chunks[0])
                for c in chunks:
                    dve.wait_ge(k_ready[c % KVS], b * 64 + 32 * (c // KVS + 1))
                    kv = KV[c % KVS]
                    q = QB[:, bass.ds(b, 1), :].to_broadcast([P, KVP, DG])
                    kc.inc(dve.tensor_tensor(kv, kv, q, ALU.mult))
                    kc.wait(dve)
                    dve.tensor_reduce(z4[:, c * KVP:(c + 1) * KVP, bass.ds(b, 1), :].rearrange("p g a h -> p g (a h)"),
                                      kv.rearrange("p g (h d) -> p g h d", h=NH), AX, ALU.add).then_inc(s["k_used"], 1)

            with dve.Fori(0, NB // 2) as b:
                page_scores(b, range(CPB))

            dve.wait_ge(s["qkv_ev"], QKV_CH)
            for t in range(3):
                n = TP[t]
                qkr = QKV[0:n, t, QB_:QB_ + 2 * DG].rearrange("p (h d) -> p h d", d=HD)
                x1, x2 = qkr[:, :, 0:8], qkr[:, :, 8:16]
                ro = cst("rope")[0:n, t * 16:(t + 1) * 16].rearrange("p (a d) -> p a d", a=2)
                cos, sin = (ro[:, a:a + 1, :].to_broadcast([n, 16, 8]) for a in range(2))
                r = [Hf[0:n, 128 * m:128 * (m + 1)].rearrange("p (h d) -> p h d", d=8) for m in range(4)]
                for out, a, b in ((r[0], x1, cos), (r[1], x2, sin), (r[2], x2, cos), (r[3], x1, sin)):
                    last = dve.tensor_tensor(out, a, b, ALU.mult)
                step(last)
                dve.tensor_tensor(x1, r[0], r[1], ALU.subtract)
                step(dve.tensor_tensor(x2, r[2], r[3], ALU.add))
            dve.tensor_copy(stat[:, 31:32], stat[:, 31:32]).then_inc(s["rot_done"], 1)

            def both(a):
                return a.rearrange("p j (n k) -> p j n k", n=3)[:, :, bass.ds(0, 2, step=2), :]

            lat = later.rearrange("p (a b k) -> p a b k", a=1, b=1).to_broadcast([P, 2, 2, P])
            with dve.Fori(0, NH // 2) as g:
                dve.wait_ge(s["sc_mm"], g + 1)
                for j in range(2):
                    dve.tensor_scalar(aw[0][:, j, :], ps[:, 1 + j, 0:384], SCALE, sbb[:, bass.ds(g * 2 + j, 1)],
                                      ALU.mult, ALU.add).then_inc(s["s_l"], 1)
                page_scores(g + 4, (0, 1))
                dve.wait_ge(s["s_t"], g * 3 + 3)
                dve.wait_ge(s["s_l"], g * 2 + 2)
                c = Count(s["sbs"], g)
                c.inc(dve.scalar_tensor_tensor(aw[1], aw[0], 0.0, aw[1], ALU.max, ALU.add))
                c.wait(dve)
                dve.tensor_tensor(both(aw[1]), both(aw[1]), lat, ALU.mult).then_inc(s["s_L"], 1)
                page_scores(g + 4, (2, 3))
                dve.wait_ge(s["s_mm"], g + 1)
                for j in range(2):
                    dve.tensor_tensor(aw[2][:, j, :], aw[0][:, j, :], ps[:, 3 + j, 0:384], ALU.subtract
                                      ).then_inc(s["s_a"], 1)
                page_scores(g + 4, (4, 5))
                dve.wait_ge(s["s_e"], g + 1)
                dve.tensor_tensor(both(aw[2]), both(aw[2]), lat, ALU.mult).then_inc(s["s_am"], 1)
                page_scores(g + 4, (6, 7))
                dve.wait_ge(s["o_mm"], g + 1)
                dve.tensor_copy(QKV[:, 0:2, bass.ds(QA + g * P, P)], ps[:, 5, 0:256].rearrange("p (t n) -> p t n", t=2)
                                ).then_inc(s["o_ev"], 1)

            dve.wait_ge(s["k_used"], NB * CPB)
            dve.wait_ge(s["small_in"], 64)
            zv = z1.rearrange("p (n h) -> p n h", h=NH)
            dve.wait_ge(s["dve"], ch.n)
            dve.scalar_tensor_tensor(zv, zv, SCALE, sbb[:, :].rearrange("p (a h) -> p a h", a=1).to_broadcast([P, P, NH]),
                                     ALU.mult, ALU.add).then_inc(s["z_l"], 1)
            dve.wait_ge(s["z_abs"], 3)
            dve.wait_ge(s["z_l"], 1)
            step(dve.scalar_tensor_tensor(zl, z1, 0.0, zt, ALU.max, ALU.add))
            step(dve.memset(zt[:, 960:1024], 0.0))
            for g in range(NPG - 2, -1, -1):
                nxt = slice((g + 1) * 64, (g + 2) * 64)
                ins = dve.tensor_tensor(zt[:, g * 64:(g + 1) * 64], zl[:, nxt], zt[:, nxt], ALU.add)
                if g:
                    step(ins)
            ins.then_inc(s["z_suf"], 1)
            dve.wait_ge(s["z_s"], 1)
            dve.tensor_tensor(Z[:, 0, :].rearrange("p (a n) -> p a n", a=2), Z[:, 0, :].rearrange("p (a n) -> p a n", a=2),
                              ps[:, 1:3, :], ALU.subtract).then_inc(s["z_e"], 1)

            def window_scores(g, j):
                dve.wait_ge(dk_ready[j], g * 64 + 64)
                kv = DK[j]
                kc = Count(s["dst"], g * 2 + j)
                kc.inc(dve.tensor_tensor(kv, kv, QB[:, bass.ds(g * 2 + j, 1), :].to_broadcast([P, 3, DG]), ALU.mult))
                kc.wait(dve)
                dve.tensor_reduce(zd[:, :, bass.ds(g * (2 * NH) + j * NH, NH)],
                                  kv.rearrange("p g (h d) -> p g h d", h=NH), AX, ALU.add).then_inc(s["dk_used"], 1)

            def block_rows(i, j, first, mm, per, ready, used):
                dve.wait_ge(mm, i * per + per)
                if not first:
                    dve.wait_ge(used, i)
                dve.tensor_tensor(msk[:, :], ps[0:NH, 6 + j, :], cst("hmask")[0:NH, :], ALU.mult).then_inc(ready, 1)

            def page_rows(i, j, first=False):
                block_rows(i, j, first, s["v_used"], CPB, s["msk_ready"], s["oA_mm"])

            def dilated_pair(g, first=False):
                window_scores(g, 0)
                dve.wait_ge(s["sc_mm"], g + 5)
                c = Count(s["dis"], g * 3)
                for j in range(2):
                    last = dve.tensor_tensor(aw[0][:, j, :], ps[:, 1 + j, 0:384], cst("dbias"), ALU.add)
                c.inc(last)
                c.wait(dve)
                for j in range(2):
                    dve.tensor_reduce(stat[:, 24 + 2 * j:25 + 2 * j], aw[0][:, j, 0:128], AX, ALU.max)
                    last = dve.tensor_reduce(stat[:, 25 + 2 * j:26 + 2 * j], aw[0][:, j, 128:384], AX, ALU.max)
                c.inc(last)
                c.wait(dve)
                dve.tensor_scalar(stat[:, 20:24], stat[:, 24:28], -SCALE, None, ALU.mult).then_inc(s["d_zm"], 1)
                dve.wait_ge(s["d_e"], g + 1)
                for j in range(2):
                    for n, cc in enumerate((slice(0, 128), slice(128, 384))):
                        last = dve.tensor_tensor_reduce(aw[0][:, j, cc], aw[0][:, j, cc], cst("cnt")[:, cc], 1.0, 0.0,
                                                        ALU.mult, ALU.add, stat[:, 24 + 2 * j + n:25 + 2 * j + n])
                last.then_inc(s["d_p"], 1)
                dve.wait_ge(s["d_p"], g + 1)
                c.inc(dve.reciprocal(stat[:, 24:28], stat[:, 24:28]))
                page_rows(g * 2, 0, first)
                window_scores(g, 1)
                page_rows(g * 2 + 1, 1)
                dve.wait_ge(s["dis"], g * 3 + 3)
                dve.wait_ge(s["d_o"], g + 1)
                for j in range(2):
                    for t in range(2):
                        last = dve.tensor_scalar(QKV[:, t, bass.ds(QB_ + j * HD + g * P, HD)],
                                                 ps[:, 5, t * P + j * HD:t * P + (j + 1) * HD],
                                                 stat[:, 24 + 2 * j + t:25 + 2 * j + t], None, ALU.mult)
                last.then_inc(s["d_oe"], 1)

            dve.wait_ge(s["qd_ev"], NB)
            dilated_pair(0, first=True)
            with dve.Fori(1, NH // 2) as g:
                dilated_pair(g)

            dve.wait_ge(s["dT_mm"], 1)
            step(dve.tensor_tensor(zrow[:, :], ps[0:64, 6, 0:384], cst("sbias")[0:64, :], ALU.add))
            step(dve.tensor_reduce(stat[0:64, 8:9], zrow[:, :], AX, ALU.max))
            dve.tensor_scalar(stat[0:64, 9:10], stat[0:64, 8:9], -SCALE, None, ALU.mult).then_inc(s["dm_ready"], 1)
            dve.wait_ge(s["de_ready"], 1)
            step(dve.tensor_tensor_reduce(zrow[:, :], zrow[:, :], cst("scnt")[0:64, :], 1.0, 0.0, ALU.mult, ALU.add,
                                          stat[0:64, 8:9]))
            step(dve.reciprocal(stat[0:64, 8:9], stat[0:64, 8:9]))
            dve.tensor_scalar(zrow[:, :], zrow[:, :], stat[0:64, 8:9], None, ALU.mult).then_inc(s["dp_ready"], 1)

            dve.wait_ge(s["oA_mm"], NB)
            window_args = (s["vd_used"], 1, s["mskd_ready"], s["oB_mm"])
            block_rows(0, 0, True, *window_args)
            block_rows(1, 1, False, *window_args)
            with dve.Fori(1, NB // 2) as i:
                for j in range(2):
                    block_rows(i * 2 + j, j, False, *window_args)
            dve.wait_ge(s["oB_mm"], NB)
            dve.wait_ge(s["qb_ev"], NB)
            dve.tensor_copy(QKV[0:NB, 2, QA:QA + DG], ps[0:NB, 3, :])
            step(dve.tensor_copy(QKV[0:NB, 2, QB_:QB_ + DG], ps[0:NB, 4, :]))

            dve.wait_ge(s["ada_ev"], ADA_CH)
            dve.wait_ge(s["small_in"], 64)
            dve.scalar_tensor_tensor(m_rows[:, SCALE2, :], m_rows[:, SCALE2, :], 1.0, nffn[:, :], ALU.add, ALU.mult
                                     ).then_inc(s["m2_ready"], 1)

            for t in range(3):
                for q, col in ((0, QA), (1, QB_)):
                    n = TP[t]
                    o = QKV[0:n, t, col:col + DG]
                    last = dve.tensor_tensor_reduce(H[0:n, t, q * DG:(q + 1) * DG], o, o, 1.0, 0.0, ALU.mult, ALU.add,
                                                    stat[0:n, 10 + 2 * t + q:11 + 2 * t + q])
            step(last)
            dve.tensor_scalar(stat[:, 10:16], stat[:, 10:16], 1.0 / DG, EPS, ALU.mult, ALU.add).then_inc(s["ff_ready"], 1)
            dve.wait_ge(s["f_rt"], 1)
            step(dve.reciprocal(stat[:, 10:16], stat[:, 4:10]))
            for t in range(3):
                for q, col in ((0, QA), (1, QB_)):
                    n = TP[t]
                    last = dve.tensor_scalar(H[0:n, t, q * DG:(q + 1) * DG], QKV[0:n, t, col:col + DG],
                                             stat[0:n, 10 + 2 * t + q:11 + 2 * t + q], None, ALU.mult)
                last.then_inc(s["mg_ready"], 1)
            for n in range(5):
                dve.wait_ge(s["mg_mm"], n + 1)
                if n < 4:
                    t, half = divmod(n, 2)
                    dve.tensor_tensor(hT[:, 4 * half:4 * half + 4, t * P:(t + 1) * P],
                                      ps[:, n, :].rearrange("p (c n) -> p c n", c=4),
                                      gcol[:, 4 * half:4 * half + 4].rearrange("p (c a) -> p c a", a=1).to_broadcast([P, 4, P]),
                                      ALU.mult).then_inc(s["mg_ev"], 1)
                else:
                    dve.tensor_tensor(hT[:, :, SEQ:NTOK], ps[:, 4, 0:64].rearrange("p (c n) -> p c n", c=KC),
                                      gcol[:, :].rearrange("p (c a) -> p c a", a=1).to_broadcast([P, KC, NB]),
                                      ALU.mult).then_inc(s["mg_ev"], 1)
            dve.wait_ge(s["kv_out"], 160)
            dve.wait_ge(s["new_out"], 32)
            dve.memset(eqz, 0.0)
            step(dve.memset(S[:, UNITS - 1, :, :].rearrange("p b n -> p (b n)"), 0.0))
            dve.memset(tw[:, 2048:2048 + P], 0.0).then_inc(s["z_v"], 1)
            dve.wait_ge(s["bc2_ev"], 8)
            for k in range(OUT_CH):
                c = slice(k * WC, (k + 1) * WC)
                dve.wait_ge(s["w_used"], ADA_CH + QKV_CH + k + 1)
                if k:
                    dve.wait_ge(s["out_ev"], k)
                g1 = m_all[:, GATE1:GATE1 + 1, c].to_broadcast([P, 2, WC])
                tmp = tw[:, 0:512].rearrange("p (t n) -> p t n", t=2)
                dve.tensor_tensor(tmp, ps[:, 2 * (k % 2), :].rearrange("p (t n) -> p t n", t=2), g1, ALU.mult)
                step(dve.tensor_tensor(tw[0:NB, 512:768], ps[0:NB, 2 * (k % 2) + 1, 0:WC], m_rows[0:NB, GATE1, c], ALU.mult))
                dve.tensor_tensor(x[:, 0:2, c], x[:, 0:2, c], tmp, ALU.add)
                dve.tensor_tensor(x[0:NB, 2, c], x[0:NB, 2, c], tw[0:NB, 512:768], ALU.add).then_inc(s["out_ev"], 1)
            dve.wait_ge(s["out_ev"], OUT_CH)
            sums(2)
            modulate(SCALE2, SHIFT2)

            def top16(tk, vals, where, row, spare):
                wait_apart(dve, tk.sem, tk.value())
                tk.inc(dve.max(vals[:, 0:8], row))
                wait_apart(dve, tk.sem, tk.value())
                dve.max_index(where[:, 0:8], vals[:, 0:8], row)
                tk.inc(dve.match_replace(spare, vals[:, 0:8], row, LOWEST))
                wait_apart(dve, tk.sem, tk.value())
                tk.inc(dve.max(vals[:, 8:16], spare))
                wait_apart(dve, tk.sem, tk.value())
                tk.inc(dve.max_index(where[:, 8:16], vals[:, 8:16], spare))

            def grid(a):
                return a.rearrange("p (k j) -> p k j", k=TOPK)

            def along(a, dim):
                if dim == 1:
                    return a.rearrange("p (k j) -> p k j", j=1).to_broadcast([P, TOPK, TOPK])
                return a.rearrange("p (k j) -> p k j", k=1).to_broadcast([P, TOPK, TOPK])

            TOPSTEPS = 22

            def choose(i):
                tk = Count(s["tks"], i * TOPSTEPS)
                tk.inc(dve.tensor_copy(sc, S[:, bass.ds(i, 1), :, :].rearrange("p a c n -> p (a c n)")))
                for c in range(2):
                    top16(tk, tv[c], tiu[c], sc[:, c * NKEY:(c + 1) * NKEY], rep[:, c * NKEY:(c + 1) * NKEY])
                    if c == 0:
                        yield
                tk.wait(dve)
                for c in range(2):
                    last = dve.tensor_copy(tif[c], tiu[c][:, :])
                tk.inc(dve.tensor_tensor(grid(cand), along(tv[0], 1), along(tv[1], 2), ALU.add))
                yield
                top16(tk, cv, ciu, cand, crep)
                tk.wait(dve)
                dve.tensor_scalar(ctop_d, cv, cv[:, 0:1], None, ALU.subtract).then_inc(s["topsm"], 1)
                yield
                dve.tensor_scalar(cint[:, 0, :], ciu[:, :], 4, None, ALU.logical_shift_right)
                tk.inc(dve.tensor_scalar(cint[:, 1, :], ciu[:, :], 15, None, ALU.bitwise_and))
                tk.wait(dve)
                dve.tensor_copy(row_f, cint[:, 0, :])
                tk.inc(dve.tensor_copy(col_f, cint[:, 1, :]))
                tk.wait(dve)
                for want, o in ((row_f, oh), (col_f, oh2)):
                    last = dve.tensor_tensor(grid(o), along(want, 1), along(cst("iota"), 2), ALU.is_equal)
                tk.inc(last)
                tk.wait(dve)
                for c, o in ((0, oh), (1, oh2)):
                    last = dve.tensor_tensor(grid(o), grid(o), along(tif[c], 2), ALU.mult)
                tk.inc(last)
                tk.wait(dve)
                dve.tensor_reduce(e1f, grid(oh), AX, ALU.add)
                tk.inc(dve.tensor_reduce(e2f, grid(oh2), AX, ALU.add))
                tk.wait(dve)
                tk.inc(dve.scalar_tensor_tensor(eidf, e1f, float(NKEY), e2f, ALU.mult, ALU.add))
                tk.wait(dve)
                dve.tensor_copy(idx[:, bass.ds(i, 1), :].rearrange("p a n -> p (a n)"), eidf)
                dve.wait_ge(s["tope"], i + 1)
                tk.inc(dve.tensor_reduce(tst[:, 0:1], ctop_e, AX, ALU.add))
                tk.wait(dve)
                tk.inc(dve.reciprocal(tst[:, 1:2], tst[:, 0:1]))
                tk.wait(dve)
                dve.tensor_scalar(gall[:, bass.ds(i, 1), :].rearrange("p a n -> p (a n)"), ctop_e, tst[:, 1:2], None,
                                  ALU.mult).then_inc(s["top_done"], 1)
                assert tk.n == TOPSTEPS, tk.n

            def dot_rows(i, t, n=P, choosing=()):
                parts = iter(choosing)
                for k in range(TOPK):
                    dve.wait_ge(e_ready[k % NSLOT], i * 32 + 16 * (k // NSLOT + 1))
                    u = R[0:n, k % NSLOT, 0:D]
                    dve.tensor_tensor_reduce(u, u, H[0:n, t, :], 1.0, 0.0, ALU.mult, ALU.add, dots[0:n, k:k + 1]
                                             ).then_inc(s["dot_done"], 1)
                    if k % 4 == 3:
                        next(parts, None)

            def finish(t, bank, acc, value, gate):
                n = TP[t]
                dve.wait_ge(acc, value)
                dve.wait_ge(s["fin_in"], 16)
                a = ps[0:n, bank:bank + 2, :]
                Ht = H[0:n, t, :].rearrange("p (a n) -> p a n", a=2)
                step(dve.tensor_tensor(Ht, a, gate.rearrange("p (a n) -> p a n", a=2), ALU.mult))
                step(dve.tensor_tensor(x[0:n, t, :], x[0:n, t, :], H[0:n, t, :], ALU.add))
                step(dve.tensor_tensor_reduce(H[0:n, t, :], x[0:n, t, :], x[0:n, t, :], 1.0, 0.0, ALU.mult, ALU.add,
                                              stat[0:n, 18:19]))
                dve.tensor_scalar(stat[0:n, 16:17], stat[0:n, 18:19], 1.0 / D, EPS, ALU.mult, ALU.add
                                  ).then_inc(s["ff_ready"], 1)
                dve.wait_ge(s["f_rt"], t + 2)
                step(dve.reciprocal(stat[0:n, 19:20], stat[0:n, 17:18]))
                dve.scalar_tensor_tensor(H[0:n, t, :], x[0:n, t, :], stat[0:n, 19:20], m_all[0:n, SHIFT2, :], ALU.mult, ALU.mult
                                         ).then_inc(s["y_ready"], 1)

            dve.wait_ge(s["score_ev"], 17)
            for i in range(2):
                for _ in choose(i):
                    pass
            with dve.Fori(0, NH) as h:
                dot_rows(h, 0, choosing=choose(h + 2))
            finish(0, 4, s["e_used"], NH * TOPK, m_all[:, GATE2, :])
            with dve.Fori(0, NH - 1) as h:
                dot_rows(h + 8, 1, choosing=choose(h + 10))
            dot_rows(2 * NH - 1, 1)
            dve.wait_ge(s["hr_ev"], 1)
            dot_rows(2 * NH, 2, n=PAIRS)
            finish(1, 6, s["e_used"], 2 * NH * TOPK, m_all[:, GATE2, :])
            finish(2, 0, s["e_used"], UNITS * TOPK, m_rows[0:NB, GATE2, :])


_OUTS = [("y_p", (SEQ, D), (1, SEQ, D)), ("y_s", (NB, D), (NB, 1, D)),
         ("sb_k_p", (SEQ, DG), (1, 1, SEQ, NH, HD)), ("sb_v_p", (SEQ, DG), (1, 1, SEQ, NH, HD)),
         ("dil_k_p", (SEQ, DG), (1, 1, SEQ, NH, HD)), ("dil_v_p", (SEQ, DG), (1, 1, SEQ, NH, HD)),
         ("sb_k_n", (NB, DG), (1, NB, 1, NH, HD)), ("sb_v_n", (NB, DG), (1, NB, 1, NH, HD)),
         ("dil_k_s", (NB, PAST * DG), (1, NB, PAST, NH, HD)), ("dil_v_s", (NB, PAST * DG), (1, NB, PAST, NH, HD))]


def kernel(**inputs):
    import concourse.bacc as _bacc
    from concourse.bass_utils import run_bass_kernel_spmd as _run

    a = {k: np.asarray(v) for k, v in inputs.items()}

    def chunks(w):
        return w.reshape(KC, P, -1, WC).transpose(2, 1, 0, 3).reshape(-1, P, KC * WC)

    arrays = {
        "consts": constants(),
        "c9": np.concatenate([a["c_sample"], a["c_prompt"]], 0),
        "x": np.concatenate([a["x_prompt"].reshape(SEQ, D), a["x_sample"].reshape(NB, D)], 0),
        "b_ada": a["b_ada"].reshape(ADA_CH, WC),
        "norm_mix": a["norm_mix"].reshape(1, D),
        "norm_ffn": a["norm_ffn"].reshape(1, D),
        "norm_final": a["norm_final"].reshape(1, D),
        "sb_bias": a["sb_bias"].reshape(1, NH),
        "g_out": np.concatenate([a["norm_out_sb"], a["norm_out_dil"]], -1).reshape(KC, P).T,
        "pages": a["page_table"].reshape(1, NB * NPG),
        "wts": np.concatenate([chunks(w) for w in (a["w_ada"][0][:, :2 * D], a["w_in"][0], a["w_ada"][0][:, 2 * D:],
                                                   a["w_out"][0], a["w_peer_q"][0])], 0),
        "subk": a["peer_sub_keys"].reshape(16, NKEY, P).transpose(2, 0, 1).reshape(P, 16 * NKEY),
        "sb_k": a["cache_sb_k"].reshape(-1, P, DG),
        "sb_v": a["cache_sb_v"].reshape(-1, P, DG),
        "dil_k": a["cache_dil_k"].reshape(NB, PAST * DG),
        "dil_v": a["cache_dil_v"].reshape(NB, PAST * DG),
        "uv": np.concatenate([a["peer_u"][0], a["peer_v"][0]], -1),
    }
    arrays = {k: np.ascontiguousarray(v) for k, v in arrays.items()}
    nc = _bacc.Bacc("TRN2", target_bir_lowering=False, num_devices=1)
    A = {k: nc.dram_tensor("in_" + k, v.shape, mybir.dt.from_np(v.dtype), kind="ExternalInput").ap()
         for k, v in arrays.items()}
    for name, shape, _ in _OUTS:
        A[name] = nc.dram_tensor("out_" + name, shape, F32, kind="ExternalOutput").ap()
    build(nc, A)
    r = _run(nc, [{"in_" + k: v for k, v in arrays.items()}], core_ids=[0])
    return tuple(r.results[0]["out_" + name].reshape(final) for name, _, final in _OUTS)
```

```python
from contextlib import ExitStack

import numpy as np

import concourse.bass as bass
from concourse import mybir

F32 = mybir.dt.float32
I32 = mybir.dt.int32
U32 = mybir.dt.uint32
ALU = mybir.AluOpType
ACT = mybir.ActivationFunctionType
AX = mybir.AxisListType.X

P = 128
D = 1024
KC = D // P
SEQ = 256
NB = 8
NTOK = SEQ + NB
HD = 64
NH = 8
DG = NH * HD
NPG = 16
PAST = NPG * P
WC = 256
WSLOTS = 4
ADA_CH, QKV_CH, OUT_CH, PQ_CH = 6 * D // WC, 6 * DG // WC, D // WC, 2 * D // WC
QA, KA, VA, QB_, KB_, VB_ = (DG * n for n in range(6))
CHUNKS = ADA_CH + QKV_CH + OUT_CH + PQ_CH
KVP = 2
KVS = 4
CPB = NPG // KVP
TOPK = 16
NKEY = 128
NSLOT = 8
DIL_ROWS = 96
UNITS = 2 * NH + 1
PAIRS = NB * NH
HALF = 8
SHIFT1, SCALE1 = 2, 3
GATE1, SHIFT2, SCALE2, GATE2 = range(4)
EPS = 1e-6
SCALE = HD ** -0.5
LOWEST = -3.0e38
MASKED = -1.0e30

_CONST = {}
_at = 0
for _name, _n in (("ident", P), ("tri", P), ("ones", P), ("later", P), ("cnt", 384), ("dbias", 384),
                  ("scnt", 384), ("sbias", 384), ("rope", 48), ("hmask", DG), ("unit8", 64), ("rep8", P), ("fold8", NB), ("iota", TOPK)):
    _CONST[_name] = (_at, _n)
    _at += _n
NCONST = _at


def constants():
    c = np.zeros((P, NCONST), np.float32)

    def put(name, a):
        at, n = _CONST[name]
        c[:a.shape[0], at:at + n] = a.reshape(a.shape[0], n)

    p, f = np.arange(P)[:, None], np.arange(P)[None, :]
    put("ident", (p == f).astype(np.float32))
    put("tri", (p >= f).astype(np.float32))
    put("ones", np.ones((P, P), np.float32))
    put("later", (p < f).astype(np.float32))

    def count(d):
        d = np.asarray(d)
        return sum(((d >= 0) & (d <= w) & (d % s == 0)).astype(np.float32) for w, s in ((128, 1), (512, 4), (2048, 16)))

    cnt = np.concatenate([count(p - f), count(P + p - f), count(p - f)], 1)
    put("cnt", cnt)
    put("dbias", np.where(cnt > 0, 0.0, MASKED).astype(np.float32))
    far = np.full(P, -1)
    mid, long = far.copy(), far.copy()
    mid[:DIL_ROWS] = 512 - 4 * np.arange(DIL_ROWS)
    mid[DIL_ROWS] = 0
    long[:DIL_ROWS] = 2048 - 16 * np.arange(DIL_ROWS)
    scnt = np.tile(count(np.concatenate([P - np.arange(P), mid, long])), (NB * NH, 1))
    put("scnt", scnt)
    put("sbias", np.where(scnt > 0, 0.0, MASKED).astype(np.float32))
    inv = np.float32(500000.0) ** (-np.arange(8, dtype=np.float32) / np.float32(8))
    pos = np.concatenate([np.arange(SEQ), np.full(P, PAST)]).astype(np.float32)
    ang = (pos[:, None] * inv[None, :]).astype(np.float32)
    rope = np.concatenate([np.cos(ang), np.sin(ang)], 1).reshape(3, P, 16).transpose(1, 0, 2)
    put("rope", np.ascontiguousarray(rope).astype(np.float32))
    put("hmask", (np.arange(NH)[:, None] == (np.arange(DG) // HD)[None, :]).astype(np.float32))
    put("unit8", np.tile(np.eye(8, dtype=np.float32).reshape(1, 64), (P, 1)))
    put("rep8", np.tile(np.eye(NB, dtype=np.float32), (1, 2 * NH)))
    put("fold8", np.tile(np.eye(NB, dtype=np.float32), (2 * NH, 1)))
    put("iota", np.tile(np.arange(TOPK, dtype=np.float32), (P, 1)))
    return c


class Count:

    def __init__(self, sem, base=0):
        self.sem, self.base, self.n = sem, base, 0

    def inc(self, instruction):
        instruction.then_inc(self.sem, 1)
        self.n += 1

    def value(self):
        return self.base + self.n

    def wait(self, eng):
        eng.wait_ge(self.sem, self.value())


def build(nc, A):
    ctx = ExitStack()
    with ctx:
        def sb(name, shape, dt=F32):
            return ctx.enter_context(nc.sbuf_tensor(name, shape, dt))

        def sem(name):
            return ctx.enter_context(nc.semaphore(name))

        const = sb("const", [P, NCONST])

        def cst(name):
            at, n = _CONST[name]
            return const[:, at:at + n]

        ident, tri, ones, later = cst("ident"), cst("tri"), cst("ones"), cst("later")
        m_rows = sb("m_rows", [9, 4, D])
        m_all = sb("m_all", [P, 4, D])
        x = sb("x", [P, 3, D])
        H = sb("H", [P, 3, D])
        HT = sb("HT", [P, KC * NTOK])
        QKV = sb("QKV", [P, 3, 6 * DG])
        R = sb("R", [P, NSLOT, 2 * D])
        Z = sb("Z", [P, 3, NPG * NB * NH])
        nffn = sb("nffn", [9, D])
        b24 = sb("b24", [ADA_CH, WC])
        zd = sb("zd", [P, 3, NB * NH])
        zrow = sb("zrow", [NB * NH, 384])
        pd = sb("pd", [P, 3, NB * NH])
        cT = sb("cT", [P, KC, 9])
        bsel = sb("bsel", [ADA_CH, 2, 9])
        sbb = sb("sbb", [P, NH])
        gcol = sb("gcol", [P, KC])
        pages = sb("pages", [1, NB * NPG], I32)
        stat = sb("stat", [P, 32])
        ast = sb("ast", [P, 2, NPG, NH])
        selst = sb("selst", [NH, 2, NB])
        msk = sb("msk", [NH, DG])
        gall = sb("gall", [P, UNITS, TOPK])
        idx = sb("idx", [P, UNITS, TOPK], I32)
        idst = sb("idst", [P, 2, TOPK], I32)
        idec = sb("idec", [P, HALF], I32)
        gst = sb("gst", [P, TOPK])
        dots = sb("dots", [P, TOPK])
        gel = sb("gel", [P, TOPK])
        wgt = sb("wgt", [P, TOPK])
        diag = sb("diag", [P, 4, P])

        hT = HT[:, :].rearrange("p (c n) -> p c n", c=KC)
        Rf = R[:, :, :].rearrange("p s n -> p (s n)")
        W = [R[:, s, :].rearrange("p (c n) -> p c n", c=KC) for s in range(WSLOTS)]
        KV = [Rf[:, WSLOTS * 2048 + s * 1024:WSLOTS * 2048 + (s + 1) * 1024].rearrange("p (g n) -> p g n", g=KVP)
              for s in range(KVS)]
        m_flat = m_all[:, :, :].rearrange("p s n -> p (s n)")
        DK = [m_flat[:, s * 3 * DG:(s + 1) * 3 * DG].rearrange("p (g n) -> p g n", g=3) for s in range(2)]
        DV = [R[:, 6 + s, 0:3 * DG].rearrange("p (g n) -> p g n", g=3) for s in range(2)]
        subk = R[:, WSLOTS, :].rearrange("p (g n) -> p g n", g=16)
        QB = Rf[:, 6 * 2048:8 * 2048].rearrange("p (b n) -> p b n", b=NB)
        z4 = Z[:, 0, :].rearrange("p (g b h) -> p g b h", g=NPG, b=NB)
        z1, zt, zl = Z[:, 0, :], Z[:, 1, :], Z[:, 2, :]
        cwork = [Z[0:9, n, :] for n in range(3)]
        Hf = H[:, :, :].rearrange("p t n -> p (t n)")
        aw = [Hf[:, n * 768:(n + 1) * 768].rearrange("p (j n) -> p j n", j=2) for n in range(3)]
        stq = Hf[:, 2304:2560].rearrange("p (t n) -> p t n", t=2)
        stk = Hf[:, 2560:2816].rearrange("p (t n) -> p t n", t=2)
        qk = HT[:, 0:512]
        pT = HT[:, 512:1280].rearrange("p (j n) -> p j n", j=2)
        Qf = QKV[:, :, :].rearrange("p t n -> p (t n)")
        S = Qf[:, 0:UNITS * 2 * NKEY].rearrange("p (i c n) -> p i c n", i=UNITS, c=2)
        tw = Qf[:, 6144:9216]

        eq = Z[:, 0, 0:2 * 512].rearrange("p (j n) -> p j n", j=2)
        eqz = Z[:, 1:3, :].rearrange("p a n -> p (a n)")
        eqz4 = eqz.rearrange("p (m g n) -> p g m n", g=2, n=PAIRS)

        def row_slot(k):
            return (5, 6, 7, 0, 1, 2, 3, 4)[k % NSLOT]

        sc, rep, cand, crep, oh, oh2 = (tw[:, n * 256:(n + 1) * 256] for n in range(6))
        tsm = tw[:, 1536:2048]
        tv = [tsm[:, 0:16], tsm[:, 16:32]]
        tif = [tsm[:, 32:48], tsm[:, 48:64]]
        cv, ctop_d, ctop_e = tsm[:, 64:80], tsm[:, 80:96], tsm[:, 96:112]
        eidf, row_f, col_f, e1f, e2f = (tsm[:, 112 + 16 * n:128 + 16 * n] for n in range(5))
        tst = tsm[:, 200:204]
        tiu = [sb("tiu0", [P, TOPK], U32), sb("tiu1", [P, TOPK], U32)]
        ciu = sb("ciu", [P, TOPK], U32)
        cint = sb("cint", [P, 2, TOPK], U32)

        ps = ctx.enter_context(nc.psum_tensor("ps", [P, 8, 512], F32))

        names = """c9_in c_in x_in small_in w_used sel_ready ada_mm ada_ev bc_mm bc_ev cs_ready cT_mm cT_ev m1_ready
          h_ssq h_rt h_ready hT_mm hT_ev qkv_ev qb_mm qb_ev k_used rot_done new_out kv_out z_l z_abs z_suf
          z_s z_e zz_a dk_used qd_mm qd_ev dT_mm dm_ready de_ready dp_ready dU_mm pd_ev rots st_ready t_mm t_ev
          sc_mm s_l s_t s_L s_mm s_a s_e s_am o_mm o_ev d_zm d_e d_p d_tr d_pT d_o d_oe ast_ready v_used
          msk_ready oA_mm vd_used pdst_ready mskd_ready oB_mm mg_ready mg_mm mg_ev out_ev m2_ready bc2_mm
          bc2_ev pq_mm pq_ev score_mm score_ev top_done id_st g_st dot_done gel_done w_done diag_done
          e_used ff_ready f_rt y_ready y_out hr_mm hr_ev idec_ready dve act
          kst dst sbs dis tks subk_in z_v topsm tope fin_in""".split()
        s = {n: sem(n) for n in names}
        w_ready = [sem(f"w_ready{n}") for n in range(WSLOTS)]
        k_ready = [sem(f"k_ready{n}") for n in range(KVS)]
        v_ready = [sem(f"v_ready{n}") for n in range(KVS)]
        dk_ready = [sem(f"dk_ready{n}") for n in range(2)]
        dv_ready = [sem(f"dv_ready{n}") for n in range(2)]
        copied = [sem(f"copied{n}") for n in range(4)]
        e_ready = [sem(f"e_ready{n}") for n in range(NSLOT)]

        TP = [P, P, NB]
        DILS = ((0, P, bass.ds(PAST - P, P)), (1, DIL_ROWS, bass.ds(PAST - 512, DIL_ROWS, step=4)),
                (2, DIL_ROWS, bass.ds(0, DIL_ROWS, step=16)))

        block = ctx.enter_context(nc.Block())

        wait_value = {eng: eng.alloc_register("wait_value") for eng in (nc.vector, nc.tensor, nc.gpsimd)}

        def wait_apart(eng, semaphore, value):
            if not isinstance(value, int):
                eng.reg_mov(wait_value[eng], value)
                value = wait_value[eng]
            eng.wait_ge(s["c_in"], 48)
            eng.wait_ge(semaphore, value)

        def window_rows(eng, to, b, slot, src, new, ready):
            rows = src[bass.ds(b, 1), :].rearrange("a (r n) -> (a r) n", n=DG)
            for g, n, sel in DILS:
                eng.dma_start(to[slot][0:n, g, :], rows[sel, :]).then_inc(ready[slot], 16)
            eng.dma_start(to[slot][DIL_ROWS:DIL_ROWS + 1, 1, :],
                          new[bass.ds(b, 1), (PAST - 1) * DG:]).then_inc(ready[slot], 16)

        @block.sync
        def _(sp):
            sp.dma_start(cwork[0], A["c9"]).then_inc(s["c9_in"], 16)
            sp.dma_start(const[:, :], A["consts"]).then_inc(s["c_in"], 16)
            sp.dma_start(cwork[2], A["norm_mix"].to_broadcast([9, D])).then_inc(s["c_in"], 16)
            sp.dma_start(b24[:, :], A["b_ada"]).then_inc(s["c_in"], 16)
            for t in range(3):
                sp.dma_start(x[0:TP[t], t, :], A["x"][t * P:t * P + TP[t], :]).then_inc(s["x_in"], 16)
            sp.dma_start(nffn[:, :], A["norm_ffn"].to_broadcast([9, D])).then_inc(s["small_in"], 16)
            sp.dma_start(sbb[:, :], A["sb_bias"].to_broadcast([P, NH])).then_inc(s["small_in"], 16)
            sp.dma_start(gcol[:, :], A["g_out"]).then_inc(s["small_in"], 16)
            sp.dma_start(pages[:, :], A["pages"]).then_inc(s["small_in"], 16)
            sp.wait_ge(s["small_in"], 64)

            def page_chunk(b, c, cache, ready, waits):
                for sm, v in waits:
                    sp.wait_ge(sm, v)
                for g in range(KVP):
                    page = sp.value_load(pages[0:1, bass.ds(b * NPG + c * KVP + g, 1)], min_val=0, max_val=cache.shape[0] - 1)
                    sp.dma_start(KV[c % KVS][:, g, :],
                                 cache[bass.ds(page, 1)].rearrange("a p n -> (a p) n")).then_inc(ready[c % KVS], 16)

            def copy_piece(pair, odd, m, q):
                src, dst = ((A["dil_k"], A["dil_k_s"]), (A["dil_v"], A["dil_v_s"]))[m]
                n = (PAST - 1) * DG // 4
                landed = copied[2 * odd + m]
                if not (isinstance(pair, int) and isinstance(q, int) and pair + q == 0):
                    sp.wait_ge(landed, pair * 64 + q * 16)
                sp.dma_start(dst[bass.ds(pair * 2 + odd, 1), bass.ds(q * n, n)].rearrange("a (r n) -> (a r) n", r=P),
                             src[bass.ds(pair * 2 + odd, 1), bass.ds(q * n + DG, n)].rearrange("a (r n) -> (a r) n", r=P)
                             ).then_inc(landed, 16)

            def copy_windows(pair, odd):
                for q in range(4):
                    for m in range(2):
                        copy_piece(pair, odd, m, q)

            for c in range(CPB):
                page_chunk(0, c, A["sb_k"], k_ready, [(s["k_used"], c - KVS + 1)] if c >= KVS else [])
                if c == KVS - 1:
                    copy_windows(0, 0)
                    copy_windows(0, 1)
                    copy_windows(1, 0)

            with sp.Fori(1, NB) as b:
                for c in range(CPB):
                    page_chunk(b, c, A["sb_k"], k_ready, [(s["k_used"], b * CPB + (c - KVS + 1))])

            sp.wait_ge(s["rot_done"], 6)
            for name, col in (("sb_k", KA), ("sb_v", VA), ("dil_k", KB_), ("dil_v", VB_)):
                for t in range(2):
                    sp.dma_start(A[name + "_p"][t * P:(t + 1) * P, :], QKV[:, t, col:col + DG]).then_inc(s["kv_out"], 16)
            for name, col in (("sb_k_n", KA), ("sb_v_n", VA)):
                sp.dma_start(A[name], QKV[0:NB, 2, col:col + DG]).then_inc(s["kv_out"], 16)

            def value_pages(b, first=False, q=None):
                for c in range(CPB):
                    page_chunk(b, c, A["sb_v"], v_ready,
                               [] if first and c < KVS else [(s["v_used"], b * CPB + (c - KVS + 1))])
                    if q is not None and c % 4 == 1:
                        copy_piece(2, 0, c // 4, q)

            for m in range(2):
                copy_piece(1, 1, m, 0)
            sp.wait_ge(s["k_used"], NB * CPB)
            value_pages(0, first=True, q=0)
            with sp.Fori(1, NB // 2) as i:
                value_pages(i * 2 - 1)
                value_pages(i * 2, q=i)
            value_pages(NB - 1)
            sp.wait_ge(s["new_out"], 32)
            sp.wait_ge(s["dk_used"], NB)
            for b in range(2):
                window_rows(sp, DV, b, b, A["dil_v"], A["dil_v_s"], dv_ready)
            with sp.Fori(1, NB // 2) as i:
                for j in range(2):
                    sp.wait_ge(s["vd_used"], i * 2 + (j - 1))
                    window_rows(sp, DV, i * 2 + j, j, A["dil_v"], A["dil_v_s"], dv_ready)
                    copy_piece(1, 1, j, i)
            sp.wait_ge(s["v_used"], NB * CPB)
            sp.dma_start(subk, A["subk"].rearrange("p (g n) -> p g n", g=16)).then_inc(s["subk_in"], 16)
            for pair, odd in ((2, 1), (3, 0), (3, 1)):
                copy_windows(pair, odd)
            sp.wait_ge(s["h_ready"], 6)
            sp.dma_start(m_all[:, SHIFT2, :], A["norm_final"].to_broadcast([P, D])).then_inc(s["fin_in"], 16)
            for n, (t, dst) in enumerate(((0, A["y_p"][0:P, :]), (1, A["y_p"][P:SEQ, :]), (2, A["y_s"]))):
                sp.wait_ge(s["y_ready"], n + 1)
                sp.dma_start(dst, H[0:TP[t], t, :]).then_inc(s["y_out"], 16)
            sp.wait_ge(s["kv_out"], 16 * 10)
            for n in range(4):
                sp.wait_ge(copied[n], 16 * 4 * NB // 2)
            sp.wait_ge(s["y_out"], 48)

        @block.gpsimd
        def _(pool):
            for k in range(WSLOTS):
                pool.dma_start(R[:, k, :], A["wts"][k]).then_inc(w_ready[k], 16)

            def weight_rounds(first, end):
                with pool.Fori(first, end) as r:
                    for k in range(WSLOTS):
                        pool.wait_ge(s["w_used"], r * WSLOTS + (k - WSLOTS + 1))
                        pool.dma_start(R[:, k, :], A["wts"][bass.ds(r * WSLOTS + k, 1)].rearrange("a p n -> (a p) n")
                                       ).then_inc(w_ready[k], 16)

            weight_rounds(1, 6)
            pool.wait_ge(s["qkv_ev"], QKV_CH)
            rs = Count(s["rots"])
            for t in range(3):
                n = TP[t]
                qkr = QKV[0:n, t, QB_:QB_ + 2 * DG].rearrange("p (h d) -> p h d", d=HD)
                x1, x2 = qkr[:, :, 0:8], qkr[:, :, 8:16]
                ro = cst("rope")[0:n, t * 16:(t + 1) * 16].rearrange("p (a d) -> p a d", a=2)
                cos, sin = (ro[:, a:a + 1, :].to_broadcast([n, 16, 8]) for a in range(2))
                rot = [zt[0:n, 128 * m:128 * (m + 1)].rearrange("p (h d) -> p h d", d=8) for m in range(4)]
                if t:
                    pool.wait_ge(s["rot_done"], 2 * t)
                for out, a, b in ((rot[0], x1, cos), (rot[1], x2, sin), (rot[2], x2, cos), (rot[3], x1, sin)):
                    last = pool.tensor_tensor(out, a, b, ALU.mult)
                rs.inc(last)
                rs.wait(pool)
                pool.tensor_tensor(x1, rot[0], rot[1], ALU.subtract).then_inc(s["rot_done"], 1)
                pool.tensor_tensor(x2, rot[2], rot[3], ALU.add).then_inc(s["rot_done"], 1)
            pool.wait_ge(s["rot_done"], 6)
            pool.dma_start(A["dil_k_s"][:, (PAST - 1) * DG:], QKV[0:NB, 2, KB_:KB_ + DG]).then_inc(s["new_out"], 16)
            pool.dma_start(A["dil_v_s"][:, (PAST - 1) * DG:], QKV[0:NB, 2, VB_:VB_ + DG]).then_inc(s["new_out"], 16)
            weight_rounds(6, 9)

            pool.wait_ge(s["new_out"], 32)
            pool.wait_ge(s["h_ready"], 3)
            for b in range(2):
                window_rows(pool, DK, b, b, A["dil_k"], A["dil_k_s"], dk_ready)
            weight_rounds(9, 10)
            with pool.Fori(1, NB // 2) as i:
                for j in range(2):
                    pool.wait_ge(s["dk_used"], i * 2 + (j - 1))
                    window_rows(pool, DK, i * 2 + j, j, A["dil_k"], A["dil_k_s"], dk_ready)
            weight_rounds(10, CHUNKS // WSLOTS)

            def head_rows(i, par, first):
                pool.wait_ge(s["top_done"], i + 1)
                pool.tensor_copy(idst[:, par, :], idx[:, bass.ds(i, 1), :].rearrange("p a n -> p (a n)")
                                 ).then_inc(s["id_st"], 1)
                wait_apart(pool, s["id_st"], i + 1)
                for k in range(TOPK):
                    if first and row_slot(k) < WSLOTS:
                        pool.wait_ge(s["w_used"], CHUNKS - WSLOTS + row_slot(k) + 1)
                    elif first and row_slot(k) == WSLOTS:
                        pool.wait_ge(s["score_mm"], UNITS)
                    if not (first and k < NSLOT):
                        wait_apart(pool, s["e_used"], i * TOPK + (k - NSLOT + 1))
                    pool.indirect_dma_start(
                        out=R[:, row_slot(k), :], out_offset=None, in_=A["uv"],
                        in_offset=bass.IndirectOffsetOnAxis(ap=idst[:, par, k:k + 1], axis=0),
                    ).then_inc(e_ready[k % NSLOT], 16)

            head_rows(0, 0, True)
            head_rows(1, 1, False)
            with pool.Fori(1, NH) as i:
                head_rows(i * 2, 0, False)
                head_rows(i * 2 + 1, 1, False)
            pool.wait_ge(s["idec_ready"], 1)
            for k in range(HALF):
                pool.wait_ge(s["e_used"], (UNITS - 1) * TOPK + (k - NSLOT + 1))
                pool.indirect_dma_start(
                    out=R[:, row_slot(k), :], out_offset=None, in_=A["uv"],
                    in_offset=bass.IndirectOffsetOnAxis(ap=idec[:, k:k + 1], axis=0),
                ).then_inc(e_ready[k % NSLOT], 16)

        @block.tensor
        def _(pe):
            def w_round(r, k):
                pe.wait_ge(w_ready[k], r * 16 + 16)

            pe.wait_ge(s["c_in"], 48)
            pe.wait_ge(s["cs_ready"], 1)
            for c in range(KC):
                last = pe.transpose(ps[:, 7, c * 9:(c + 1) * 9], cwork[0][:, c * P:(c + 1) * P], ident[0:9, 0:9])
            last.then_inc(s["cT_mm"], 1)
            pe.wait_ge(s["cT_ev"], 1)

            def ada_chunk(r, first, sel, k, bank):
                w_round(r + first, k)
                pe.wait_ge(s["sel_ready"], (r + sel) * WSLOTS + (k + 1))
                out = ps[0:9, bank + k % 2, 0:WC]
                for c in range(KC):
                    last = pe.matmul(out, cT[:, c, :], W[k][:, c, :], start=(c == 0), stop=False)
                last.then_inc(s["w_used"], 1)
                pe.matmul(out, bsel[:, k % 2, :], b24[:, :], start=False, stop=True).then_inc(s["ada_mm"], 1)

            def spread_rows(order, n, banks, mm, ev):
                for m, slot in enumerate(q for q in order for _ in range(2)):
                    if m >= len(banks):
                        pe.wait_ge(ev, n + m - len(banks) + 1)
                    pe.matmul(ps[:, banks[m % len(banks)], :], ident[0:9, 8:9].to_broadcast([9, P]),
                              m_rows[:, slot, (m % 2) * 512:(m % 2 + 1) * 512], start=True, stop=True).then_inc(mm, 1)

            def turn_tile(n0, t, banks, ready, mm):
                pe.wait_ge(ready, n0 + t + 1)
                if t < 2:
                    for half, bank in enumerate(banks):
                        for c in range(4):
                            last = pe.transpose(ps[:, bank, c * P:(c + 1) * P],
                                                H[:, t, (4 * half + c) * P:(4 * half + c + 1) * P], ident)
                        last.then_inc(mm, 1)
                else:
                    for c in range(KC):
                        last = pe.transpose(ps[:, banks[0], c * NB:(c + 1) * NB], H[0:NB, t, c * P:(c + 1) * P],
                                            ident[0:NB, 0:NB])
                    last.then_inc(mm, 1)

            def project(base, r, k, ev, wait_ev, late=False):
                w_round(base // WSLOTS + r, k)
                if wait_ev is not None:
                    pe.wait_ge(ev, wait_ev)
                for t in range(3):
                    if late and t == 2:
                        turn_tile(0, t, (6,), s["mg_ready"], s["mg_mm"])
                        pe.wait_ge(s["mg_ev"], 5)
                    out = ps[0:TP[t], 2 * (k % 2) + t // 2, (t % 2) * WC:(t % 2 + 1) * WC]
                    for c in range(KC):
                        last = pe.matmul(out, hT[:, c, t * P:t * P + TP[t]], W[k][:, c, :],
                                         start=(c == 0), stop=(c == KC - 1))
                    if t == 2:
                        last.then_inc(s["w_used"], 1)

            with pe.Fori(0, 2) as r:
                for k in range(WSLOTS):
                    ada_chunk(r, 0, 0, k, 0)
            pe.wait_ge(s["m1_ready"], 1)
            spread_rows((SHIFT1, SCALE1), 0, (4, 5, 6, 7), s["bc_mm"], s["bc_ev"])
            pe.wait_ge(s["bc_ev"], 4)
            for t in range(3):
                turn_tile(0, t, (0, 1, 2, 3, 4)[2 * t:2 * t + 2], s["h_ready"], s["hT_mm"])
            pe.wait_ge(s["hT_ev"], 5)
            base = 8
            for k in range(WSLOTS):
                project(base, 0, k, s["qkv_ev"], k - 1 if k >= 2 else None)
            pe.wait_ge(s["qkv_ev"], 4)
            for b in range(NB):
                if b >= 4:
                    pe.wait_ge(s["qb_ev"], b - 3)
                pe.matmul(ps[:, 4 + b % 4, :], ident[0:NB, b:b + 1].to_broadcast([NB, P]), QKV[0:NB, 2, QA:QA + DG],
                          start=True, stop=True).then_inc(s["qb_mm"], 1)
            with pe.Fori(1, QKV_CH // WSLOTS) as r:
                for k in range(WSLOTS):
                    project(base, r, k, s["qkv_ev"], r * WSLOTS + (k - 1))
            pe.wait_ge(s["qkv_ev"], QKV_CH)
            def turn_pair(i):
                pe.wait_ge(s["st_ready"], i + 1)
                for n, st in enumerate((stq, stk)):
                    for t in range(2):
                        last = pe.transpose(ps[:, 0, (2 * n + t) * P:(2 * n + t + 1) * P], st[:, t, :], ident)
                last.then_inc(s["t_mm"], 1)
                pe.wait_ge(s["t_ev"], i + 1)

            def sticks_pair(g, first=False):
                turn_pair(g)
                for j in range(2):
                    f = slice(64 * j, 64 * j + 64)
                    pe.matmul(ps[:, 1 + j, 0:256], qk[f, 256:384], qk[f, 0:256], start=True, stop=True)
                    last = pe.matmul(ps[:, 1 + j, 256:384], qk[f, 384:512], qk[f, 128:256], start=True, stop=True)
                last.then_inc(s["sc_mm"], 1)
                for k in range(2):
                    ada_chunk(g, 5, 2, k, 6)
                pe.wait_ge(s["s_L"], g + 1)
                for j in range(2):
                    L = aw[1][:, j, :]
                    pe.matmul(ps[:, 3 + j, 0:128], tri, L[:, 0:128], start=True, stop=True)
                    pe.matmul(ps[:, 3 + j, 128:256], tri, L[:, 128:256], start=True, stop=False)
                    pe.matmul(ps[:, 3 + j, 128:256], ones, L[:, 256:384], start=False, stop=True)
                    last = pe.matmul(ps[:, 3 + j, 256:384], tri, L[:, 256:384], start=True, stop=True)
                last.then_inc(s["s_mm"], 1)
                for k in range(2, 4):
                    ada_chunk(g, 5, 2, k, 6)
                pe.wait_ge(s["s_am"], g + 1)
                if not first:
                    pe.wait_ge(s["o_ev"], g)
                for j in range(2):
                    o0, o1 = ps[:, 5, j * HD:(j + 1) * HD], ps[:, 5, P + j * HD:P + (j + 1) * HD]
                    v = [QKV[:, t, bass.ds(VA + j * HD + g * P, HD)] for t in range(2)]
                    pe.matmul(o0, aw[2][:, j, 0:128], v[0], start=True, stop=True)
                    pe.matmul(o1, aw[2][:, j, 128:256], v[0], start=True, stop=False)
                    last = pe.matmul(o1, aw[2][:, j, 256:384], v[1], start=False, stop=True)
                last.then_inc(s["o_mm"], 1)

            sticks_pair(0, first=True)
            with pe.Fori(1, NH // 2) as g:
                sticks_pair(g)

            def add_row(bank, j, first):
                return pe.matmul(ps[0:NB, bank, :], selst[:, j, :], msk[:, :], start=first, stop=True,
                                 skip_group_check=True)

            def pages_pv(i, j, half):
                if half == 0:
                    pe.wait_ge(s["ast_ready"], i + 1)
                for c in range(half * 4, half * 4 + 4):
                    pe.wait_ge(v_ready[c % KVS], (i * 2 + (c // KVS + 1)) * 32)
                    for g in range(KVP):
                        last = pe.matmul(ps[0:NH, 6 + j, :], ast[:, j, c * KVP + g, :], KV[c % KVS][:, g, :],
                                         start=(c + g == 0), stop=(c * KVP + g == NPG - 1))
                    last.then_inc(s["v_used"], 1)

            def pages_row(i, j, first=False):
                wait_apart(pe, s["msk_ready"], i + 1)
                add_row(3, j, first).then_inc(s["oA_mm"], 1)

            def dilated_scores(g):
                pe.wait_ge(s["t_ev"], g + 5)
                for j in range(2):
                    f = slice(64 * j, 64 * j + 64)
                    pe.matmul(ps[:, 1 + j, 0:128], qk[f, 0:128], qk[f, 256:384], start=True, stop=True)
                    last = pe.matmul(ps[:, 1 + j, 128:384], qk[f, 128:256], qk[f, 256:512], start=True, stop=True)
                last.then_inc(s["sc_mm"], 1)

            def dilated_turn(g):
                pe.wait_ge(s["d_p"], g + 1)
                for j in range(2):
                    for n in range(3):
                        last = pe.transpose(ps[:, 1 + j, n * P:(n + 1) * P], aw[0][:, j, n * P:(n + 1) * P], ident)
                last.then_inc(s["d_tr"], 1)

            def dilated_values(g, first=False):
                pe.wait_ge(s["d_pT"], g + 1)
                if not first:
                    pe.wait_ge(s["d_oe"], g)
                for j in range(2):
                    o0, o1 = ps[:, 5, j * HD:(j + 1) * HD], ps[:, 5, P + j * HD:P + (j + 1) * HD]
                    v = [QKV[:, t, bass.ds(VB_ + j * HD + g * P, HD)] for t in range(2)]
                    pe.matmul(o0, pT[:, j, 0:128], v[0], start=True, stop=True)
                    pe.matmul(o1, pT[:, j, 128:256], v[0], start=True, stop=False)
                    last = pe.matmul(o1, pT[:, j, 256:384], v[1], start=False, stop=True)
                last.then_inc(s["d_o"], 1)

            turn_pair(4)
            dilated_scores(0)
            pe.wait_ge(s["k_used"], NB * CPB)
            pe.wait_ge(s["ada_ev"], ADA_CH)
            pe.wait_ge(s["o_ev"], NH // 2)
            pe.wait_ge(s["rot_done"], 6)
            for b in range(NB):
                if b >= 4:
                    pe.wait_ge(s["qd_ev"], b - 3)
                pe.matmul(ps[:, 4 + b % 4, :], ident[0:NB, b:b + 1].to_broadcast([NB, P]), QKV[0:NB, 2, QB_:QB_ + DG],
                          start=True, stop=True).then_inc(s["qd_mm"], 1)
            dilated_turn(0)
            pe.wait_ge(s["z_suf"], 1)
            pe.wait_ge(s["qd_ev"], NB)
            for half in range(2):
                c = slice(half * 512, (half + 1) * 512)
                pe.matmul(ps[:, 3 + half, :], tri, zl[:, c], start=True, stop=False)
                last = pe.matmul(ps[:, 3 + half, :], ones, zt[:, c], start=False, stop=True)
            last.then_inc(s["z_s"], 1)
            dilated_values(0, first=True)

            def dilated_pair(g, first=False):
                a, b = g * 2 - 2, g * 2 - 1
                turn_pair(g + 4)
                pages_pv(a, 0, 0)
                if not first:
                    pages_row(a - 1, 1)
                dilated_scores(g)
                pages_pv(a, 0, 1)
                dilated_turn(g)
                pages_pv(b, 1, 0)
                pages_row(a, 0, first)
                dilated_values(g)
                pages_pv(b, 1, 1)

            dilated_pair(1, first=True)
            with pe.Fori(2, NH // 2) as g:
                dilated_pair(g)

            pages_pv(NB - 2, 0, 0)
            pages_row(NB - 3, 1)
            pe.wait_ge(s["dk_used"], NB)
            for g in range(3):
                last = pe.transpose(ps[0:64, 1, g * P:(g + 1) * P], zd[:, g, :], ident)
            last.then_inc(s["dT_mm"], 1)
            pages_pv(NB - 2, 0, 1)
            pages_pv(NB - 1, 1, 0)
            pages_row(NB - 2, 0)
            pe.wait_ge(s["dp_ready"], 1)
            for g in range(3):
                last = pe.transpose(ps[:, 2, g * 64:(g + 1) * 64], zrow[:, g * P:(g + 1) * P], ident[0:64, 0:64])
            last.then_inc(s["dU_mm"], 1)
            pages_pv(NB - 1, 1, 1)
            pe.wait_ge(s["pd_ev"], 1)
            pe.wait_ge(s["m2_ready"], 1)
            spread_rows((GATE1,), 0, (1, 2), s["bc2_mm"], s["bc2_ev"])
            pages_row(NB - 1, 1)

            def window_pv(i, j, value):
                pe.wait_ge(s["pdst_ready"], i + 1)
                pe.wait_ge(dv_ready[j], value)
                for g, n in ((0, P), (1, DIL_ROWS + 1), (2, DIL_ROWS)):
                    last = pe.matmul(ps[0:NH, 6 + j, :], ast[0:n, j, g, :], DV[j][0:n, g, :],
                                     start=(g == 0), stop=(g == 2))
                last.then_inc(s["vd_used"], 1)

            def window_row(i, j, first=False):
                wait_apart(pe, s["mskd_ready"], i + 1)
                add_row(4, j, first).then_inc(s["oB_mm"], 1)

            window_pv(0, 0, 64)
            window_pv(1, 1, 64)
            window_row(0, 0, first=True)
            with pe.Fori(1, NB // 2) as i:
                window_pv(i * 2, 0, i * 64 + 64)
                window_row(i * 2 - 1, 1)
                window_pv(i * 2 + 1, 1, i * 64 + 64)
                window_row(i * 2, 0)
            pe.wait_ge(s["bc2_ev"], 2)
            for t in range(2):
                turn_tile(0, t, (0, 5, 1, 2)[2 * t:2 * t + 2], s["mg_ready"], s["mg_mm"])
            window_row(NB - 1, 1)

            pe.wait_ge(s["mg_ev"], 4)
            for k in range(WSLOTS):
                project(ADA_CH + QKV_CH, 0, k, s["out_ev"], k - 1 if k >= 2 else None, late=(k == 0))
            spread_rows((SHIFT2, SCALE2, GATE2), 2, (4, 5, 6, 7), s["bc2_mm"], s["bc2_ev"])
            pe.wait_ge(s["out_ev"], OUT_CH)
            pe.wait_ge(s["bc2_ev"], 8)
            for t in range(3):
                turn_tile(3, t, (0, 1, 2, 3, 4)[2 * t:2 * t + 2], s["h_ready"], s["hT_mm"])
            pe.wait_ge(s["hT_ev"], 10)

            pe.wait_ge(s["subk_in"], 16)
            base = ADA_CH + QKV_CH + OUT_CH

            def query_group(r, k, j, first):
                m = r * 8 + (2 * k + j)
                if j == 0:
                    w_round(base // WSLOTS + r, k)
                if not (first and 2 * k + j < 2):
                    pe.wait_ge(s["pq_ev"], m - 1)
                for c in range(KC):
                    last = pe.matmul(ps[:, j, 0:NTOK], W[k][:, c, j * P:(j + 1) * P], hT[:, c, :],
                                     start=(c == 0), stop=(c == KC - 1))
                last.then_inc(s["w_used"] if j else s["pq_mm"], 1)

            def score_group(r, k, j, first):
                m = r * 8 + (2 * k + j)
                pe.wait_ge(s["pq_ev"], m + 1)
                if not (first and 2 * k + j < 2):
                    pe.wait_ge(s["score_ev"], m - 1)
                for t in range(2):
                    last = pe.matmul(ps[:, 2 + j, t * P:(t + 1) * P], eq[:, j, t * P:(t + 1) * P],
                                     subk[:, bass.ds(m, 1), :].rearrange("p a n -> p (a n)"), start=True, stop=True)
                last.then_inc(s["score_mm"], 1)

            def pq_round(r, first):
                for k in range(WSLOTS):
                    for j in range(2):
                        query_group(r, k, j, first)
                    for j in range(2):
                        score_group(r, k, j, first)

            pq_round(0, True)
            with pe.Fori(1, 2) as r:
                pq_round(r, False)
            pe.wait_ge(s["pq_ev"], 16)
            for j in range(2):
                for h in range(NH):
                    m = 2 * h + j
                    last = pe.matmul(ps[:, 0, j * NKEY:(j + 1) * NKEY], eqz[:, m * P:(m + 1) * P],
                                     subk[:, m, :], start=(h == 0), stop=(h == NH - 1))
            last.then_inc(s["score_mm"], 1)
            for q in range(2):
                last = pe.matmul(ps[:, 6 + q, :], cst("rep8")[0:NB, :], H[0:NB, 2, q * 512:(q + 1) * 512],
                                 start=True, stop=True)
            last.then_inc(s["hr_mm"], 1)

            def experts(t, banks):
                for q in range(2):
                    pe.matmul(ps[:, banks + q, :], zeroP, H[:, t, q * 512:(q + 1) * 512], start=True, stop=False,
                              skip_group_check=True)
                with pe.Fori(0, NH) as h:
                    for k in range(TOPK):
                        pe.wait_ge(s["diag_done"], h * TOPK + (t * 128 + k + 1))
                        for q in range(2):
                            last = pe.matmul(ps[:, banks + q, :], diag[:, k % 4, :],
                                             R[:, row_slot(k), D + q * 512:D + (q + 1) * 512],
                                             start=False, stop=False, skip_group_check=True)
                        last.then_inc(s["e_used"], 1)

            zeroP = tw[:, 2048:2048 + P]
            pe.wait_ge(s["z_v"], 1)
            experts(0, 4)
            pe.wait_ge(s["hr_ev"], 1)
            experts(1, 6)

            pe.wait_ge(s["score_ev"], UNITS)
            for k in range(HALF):
                pe.wait_ge(s["diag_done"], (UNITS - 1) * TOPK + k + 1)
                for q in range(2):
                    last = pe.matmul(ps[0:NB, q, :], diag[:, k % 4, 0:NB],
                                     R[:, row_slot(k), D + q * 512:D + (q + 1) * 512],
                                     start=(k == 0), stop=(k == HALF - 1))
                last.then_inc(s["e_used"], 1)

        @block.scalar
        def _(act):
            act.wait_ge(s["c9_in"], 16)
            act.activation(cwork[1], cwork[0], ACT.Exp, scale=-1.0).then_inc(s["act"], 1)
            act.wait_ge(s["cT_mm"], 1)
            act.activation(cT[:, :, :], ps[:, 7, 0:72].rearrange("p (c n) -> p c n", c=KC), ACT.Copy
                           ).then_inc(s["cT_ev"], 1)

            def stage_sel(a, k):
                act.activation(bsel[:, k % 2, :], ident[0:ADA_CH, bass.ds(a, 1)].to_broadcast([ADA_CH, 9]), ACT.Copy
                               ).then_inc(s["sel_ready"], 1)

            def ada_ev(r, sel, k, slot, bank):
                a = (r + sel) * WSLOTS + k
                act.wait_ge(s["ada_mm"], a + 1)
                act.activation(m_rows[:, bass.ds(slot, 1), k * WC:(k + 1) * WC].rearrange("p a n -> p (a n)"),
                               ps[0:9, bank + k % 2, 0:WC], ACT.Copy).then_inc(s["ada_ev"], 1)
                stage_sel(a + 2, k)

            stage_sel(0, 0)
            stage_sel(1, 1)
            act.wait_ge(s["h_ssq"], 1)
            act.activation(stat[:, 4:7], stat[:, 0:3], ACT.Sqrt).then_inc(s["h_rt"], 1)
            with act.Fori(0, 2) as r:
                for k in range(WSLOTS):
                    ada_ev(r, 0, k, r + SHIFT1, 0)

            def spread_ev(order, n, banks, mm, ev):
                for m, slot in enumerate(q for q in order for _ in range(2)):
                    act.wait_ge(mm, n + m + 1)
                    act.activation(m_all[:, slot, (m % 2) * 512:(m % 2 + 1) * 512], ps[:, banks[m % len(banks)], :],
                                   ACT.Copy).then_inc(ev, 1)

            spread_ev((SHIFT1, SCALE1), 0, (4, 5, 6, 7), s["bc_mm"], s["bc_ev"])

            def turn_ev(n0, mm, ev):
                for n in range(5):
                    act.wait_ge(mm, n0 + n + 1)
                    if n < 4:
                        t, half = divmod(n, 2)
                        act.activation(hT[:, 4 * half:4 * half + 4, t * P:(t + 1) * P],
                                       ps[:, n, :].rearrange("p (c n) -> p c n", c=4), ACT.Copy).then_inc(ev, 1)
                    else:
                        act.activation(hT[:, :, SEQ:NTOK], ps[:, 4, 0:64].rearrange("p (c n) -> p c n", c=KC), ACT.Copy
                                       ).then_inc(ev, 1)

            turn_ev(0, s["hT_mm"], s["hT_ev"])

            def qkv_ev(r, k):
                n = r * WSLOTS + k
                act.wait_ge(s["w_used"], n + (8 + 1))
                act.activation(QKV[:, 0:2, bass.ds(n * WC, WC)],
                               ps[:, 2 * (k % 2), :].rearrange("p (t n) -> p t n", t=2), ACT.Copy)
                act.activation(QKV[0:NB, 2, bass.ds(n * WC, WC)], ps[0:NB, 2 * (k % 2) + 1, 0:WC], ACT.Copy
                               ).then_inc(s["qkv_ev"], 1)

            for k in range(WSLOTS):
                qkv_ev(0, k)

            def queries_ev(mm, ev):
                for b in range(NB):
                    act.wait_ge(mm, b + 1)
                    act.activation(QB[:, b, :], ps[:, 4 + b % 4, :], ACT.Copy).then_inc(ev, 1)

            queries_ev(s["qb_mm"], s["qb_ev"])
            with act.Fori(1, QKV_CH // WSLOTS) as r:
                for k in range(WSLOTS):
                    qkv_ev(r, k)
            def stage_pair(g, colq, colk):
                act.activation(stq, QKV[:, 0:2, bass.ds(colq + g * P, P)], ACT.Copy)
                act.activation(stk, QKV[:, 0:2, bass.ds(colk + g * P, P)], ACT.Copy).then_inc(s["st_ready"], 1)

            def turned_pair(i):
                act.wait_ge(s["t_mm"], i + 1)
                act.activation(qk, ps[:, 0, :], ACT.Copy).then_inc(s["t_ev"], 1)

            def sticks_pair(g, last=False):
                turned_pair(g)
                if last:
                    act.wait_ge(s["rot_done"], 6)
                    stage_pair(0, QB_, KB_)
                else:
                    stage_pair(g + 1, QA, KA)
                act.wait_ge(s["s_l"], g * 2 + 2)
                st = Count(s["s_t"], g * 3)
                st.inc(act.activation(aw[1], aw[0], ACT.Abs))
                st.wait(act)
                st.inc(act.activation(aw[1], aw[1], ACT.Exp, scale=-1.0))
                st.wait(act)
                st.inc(act.activation(aw[1], aw[1], ACT.Ln, bias=1.0))
                for k in range(2):
                    ada_ev(g, 2, k, g, 6)
                act.wait_ge(s["s_a"], g * 2 + 2)
                act.activation(aw[2], aw[2], ACT.Exp).then_inc(s["s_e"], 1)
                for k in range(2, 4):
                    ada_ev(g, 2, k, g, 6)

            stage_pair(0, QA, KA)
            with act.Fori(0, NH // 2 - 1) as g:
                sticks_pair(g)
            sticks_pair(NH // 2 - 1, last=True)

            def stage_b(i, j, first, src, ready, used):
                if not first:
                    act.wait_ge(used, i - 1)
                act.activation(ast[:, j, 0:src.shape[1], :], src[:, :, bass.ds(i * NH, NH)], ACT.Copy)
                act.activation(selst[:, j, :], cst("unit8")[0:NH, bass.ds(i * NB, NB)], ACT.Copy).then_inc(ready, 1)

            zsrc = Z[:, 0, :].rearrange("p (g n) -> p g n", g=NPG)

            def dilated_exp(g):
                act.wait_ge(s["d_zm"], g + 1)
                for j in range(2):
                    for n, c in enumerate((slice(0, 128), slice(128, 384))):
                        last = act.activation(aw[0][:, j, c], aw[0][:, j, c], ACT.Exp,
                                              bias=stat[:, 20 + 2 * j + n:21 + 2 * j + n], scale=SCALE)
                last.then_inc(s["d_e"], 1)

            def dilated_turned(g):
                act.wait_ge(s["d_tr"], g + 1)
                act.activation(pT, ps[:, 1:3, 0:384], ACT.Copy).then_inc(s["d_pT"], 1)

            turned_pair(4)
            stage_pair(1, QB_, KB_)
            act.wait_ge(s["z_l"], 1)
            steps = Count(s["z_abs"])
            steps.inc(act.activation(zt, z1, ACT.Abs))
            steps.wait(act)
            steps.inc(act.activation(zt, zt, ACT.Exp, scale=-1.0))
            steps.wait(act)
            steps.inc(act.activation(zt, zt, ACT.Ln, bias=1.0))
            dilated_exp(0)
            queries_ev(s["qd_mm"], s["qd_ev"])
            dilated_turned(0)
            act.wait_ge(s["z_e"], 1)
            act.activation(z1, z1, ACT.Exp).then_inc(s["zz_a"], 1)
            act.wait_ge(s["zz_a"], 1)

            def dilated_pair(g, first=False):
                a, b = g * 2 - 2, g * 2 - 1
                stage_b(a, 0, first, zsrc, s["ast_ready"], s["oA_mm"])
                turned_pair(g + 4)
                if g < NH // 2 - 1:
                    stage_pair(g + 1, QB_, KB_)
                stage_b(b, 1, first, zsrc, s["ast_ready"], s["oA_mm"])
                dilated_exp(g)
                dilated_turned(g)

            for g in range(1, NH // 2):
                dilated_pair(g, first=(g == 1))

            stage_b(NB - 2, 0, False, zsrc, s["ast_ready"], s["oA_mm"])
            act.wait_ge(s["dm_ready"], 1)
            act.activation(zrow[:, :], zrow[:, :], ACT.Exp, bias=stat[0:64, 9:10], scale=SCALE).then_inc(s["de_ready"], 1)
            stage_b(NB - 1, 1, False, zsrc, s["ast_ready"], s["oA_mm"])
            act.wait_ge(s["dU_mm"], 1)
            act.activation(pd[:, :, :], ps[:, 2, 0:192].rearrange("p (g n) -> p g n", g=3), ACT.Copy).then_inc(s["pd_ev"], 1)
            act.wait_ge(s["ff_ready"], 1)
            act.activation(stat[:, 4:8], stat[:, 10:14], ACT.Sqrt).then_inc(s["f_rt"], 1)
            spread_ev((GATE1,), 0, (1, 2), s["bc2_mm"], s["bc2_ev"])
            act.wait_ge(s["pd_ev"], 1)
            act.wait_ge(s["oA_mm"], NB)
            stage_b(0, 0, True, pd[:, :, :], s["pdst_ready"], s["oB_mm"])
            stage_b(1, 1, True, pd[:, :, :], s["pdst_ready"], s["oB_mm"])
            with act.Fori(1, NB // 2) as i:
                for j in range(2):
                    stage_b(i * 2 + j, j, False, pd[:, :, :], s["pdst_ready"], s["oB_mm"])

            act.wait_ge(s["ff_ready"], 2)
            act.activation(stat[0:NB, 8:10], stat[0:NB, 14:16], ACT.Sqrt).then_inc(s["f_rt"], 1)
            spread_ev((SHIFT2, SCALE2, GATE2), 2, (4, 5, 6, 7), s["bc2_mm"], s["bc2_ev"])
            act.wait_ge(s["h_ssq"], 2)
            act.activation(stat[:, 4:7], stat[:, 0:3], ACT.Sqrt).then_inc(s["h_rt"], 1)
            turn_ev(5, s["hT_mm"], s["hT_ev"])

            def pq_ev(r, k, first):
                for j in range(2):
                    m = r * 8 + (2 * k + j)
                    if j == 0:
                        act.wait_ge(s["pq_mm"], r * 4 + (k + 1))
                    else:
                        act.wait_ge(s["w_used"], r * 4 + (ADA_CH + QKV_CH + OUT_CH + k + 1))
                    if not (first and k == 0):
                        act.wait_ge(s["score_mm"], m - 1)
                    h = r * 4 + k
                    act.activation(eqz4[:, :, m, h * NB:(h + 1) * NB],
                                   ps[:, j, SEQ:NTOK].rearrange("p (a n) -> p a n", a=1).to_broadcast([P, 2, NB]), ACT.Copy)
                    act.activation(eq[:, j, 0:SEQ], ps[:, j, 0:SEQ], ACT.Copy).then_inc(s["pq_ev"], 1)
                for j in range(2):
                    m = r * 8 + (2 * k + j)
                    h = r * 4 + k
                    act.wait_ge(s["score_mm"], m + 1)
                    act.activation(S[:, bass.ds(h, 2, step=NH), j, :],
                                   ps[:, 2 + j, 0:256].rearrange("p (t n) -> p t n", t=2), ACT.Copy
                                   ).then_inc(s["score_ev"], 1)

            def top_exp(i):
                act.wait_ge(s["topsm"], i + 1)
                act.activation(ctop_e, ctop_d, ACT.Exp).then_inc(s["tope"], 1)

            act.wait_ge(s["z_v"], 1)
            for k in range(WSLOTS):
                pq_ev(0, k, True)
                if k == 2:
                    top_exp(0)
            for k in range(WSLOTS):
                pq_ev(1, k, False)
                if k == 1:
                    top_exp(1)
            act.wait_ge(s["score_mm"], 17)
            act.activation(S[:, UNITS - 1, :, :], ps[:, 0, 0:2 * NKEY].rearrange("p (c n) -> p c n", c=2),
                           ACT.Copy).then_inc(s["score_ev"], 1)
            act.wait_ge(s["hr_mm"], 1)
            act.activation(H[:, 2, :].rearrange("p (a n) -> p a n", a=2), ps[:, 6:8, :], ACT.Copy
                           ).then_inc(s["hr_ev"], 1)

            def weights(i, decode):
                act.wait_ge(s["top_done"], i + 1)
                if decode:
                    act.activation(gst[0:PAIRS, 0:HALF], gall[0:PAIRS, i, 0:HALF], ACT.Copy)
                    act.activation(gst[PAIRS:P, 0:HALF], gall[PAIRS:P, i, HALF:TOPK], ACT.Copy).then_inc(s["g_st"], 1)
                else:
                    act.activation(gst[:, :], gall[:, bass.ds(i, 1), :].rearrange("p a n -> p (a n)"), ACT.Copy
                                   ).then_inc(s["g_st"], 1)
                act.wait_ge(s["g_st"], i + 1)
                for k in range(0, HALF if decode else TOPK, 2):
                    act.wait_ge(s["dot_done"], i * TOPK + (k + 2))
                    act.activation(gel[:, k:k + 2], dots[:, k:k + 2], ACT.Gelu_apprx_tanh).then_inc(s["gel_done"], 1)
                    act.wait_ge(s["gel_done"], i * (TOPK // 2) + (k // 2 + 1))
                    for q in range(2):
                        last = act.activation(wgt[:, k + q:k + q + 1], gel[:, k + q:k + q + 1], ACT.Copy,
                                              scale=gst[:, k + q:k + q + 1])
                    last.then_inc(s["w_done"], 1)
                    act.wait_ge(s["w_done"], i * (TOPK // 2) + (k // 2 + 1))
                    for q in range(2):
                        yield k + q

            def final_root(t):
                act.wait_ge(s["ff_ready"], t + 3)
                act.activation(stat[0:TP[t], 17:18], stat[0:TP[t], 16:17], ACT.Sqrt).then_inc(s["f_rt"], 1)

            def head_weights(i, first=False, top=None, decode=False):
                for k in weights(i, decode):
                    if not (first and k < 4):
                        act.wait_ge(s["e_used"], i * TOPK + (k - 3))
                    if decode:
                        act.activation(diag[:, k % 4, 0:NB], cst("fold8"), ACT.Copy, scale=wgt[:, k:k + 1]).then_inc(s["diag_done"], 1)
                    else:
                        act.activation(diag[:, k % 4, :], ident, ACT.Copy, scale=wgt[:, k:k + 1]
                                       ).then_inc(s["diag_done"], 1)
                    if top is not None and k == 13:
                        top_exp(top)
                    if decode and k == 5:
                        final_root(1)

            head_weights(0, first=True, top=2)
            with act.Fori(1, NH) as h:
                head_weights(h, top=h + 2)
            final_root(0)
            with act.Fori(0, NH - 1) as h:
                head_weights(h + 8, top=h + 10)
            head_weights(2 * NH - 1)
            head_weights(2 * NH, decode=True)
            final_root(2)

        @block.vector
        def _(dve):
            ch = Count(s["dve"])

            def step(ins):
                ch.inc(ins)
                ch.wait(dve)

            dve.wait_ge(s["act"], 1)
            dve.wait_ge(s["c9_in"], 16)
            step(dve.tensor_scalar(cwork[1], cwork[1], 1.0, None, ALU.add))
            step(dve.reciprocal(cwork[1], cwork[1]))
            dve.tensor_tensor(cwork[0], cwork[0], cwork[1], ALU.mult).then_inc(s["cs_ready"], 1)
            def sums(n):
                for t in range(3):
                    last = dve.tensor_tensor_reduce(H[0:TP[t], t, :], x[0:TP[t], t, :], x[0:TP[t], t, :], 1.0, 0.0,
                                                    ALU.mult, ALU.add, stat[0:TP[t], t:t + 1])
                step(last)
                dve.tensor_scalar(stat[:, 0:3], stat[:, 0:3], 1.0 / D, EPS, ALU.mult, ALU.add).then_inc(s["h_ssq"], 1)
                dve.wait_ge(s["h_rt"], n)
                step(dve.reciprocal(stat[:, 0:3], stat[:, 4:7]))

            def modulate(scale, shift):
                for t in range(3):
                    n = TP[t]
                    a, b = (m_all[:, scale, :], m_all[:, shift, :]) if t < 2 else (m_rows[0:NB, scale, :], m_rows[0:NB, shift, :])
                    step(dve.scalar_tensor_tensor(H[0:n, t, :], x[0:n, t, :], stat[0:n, t:t + 1], a, ALU.mult, ALU.mult))
                    dve.tensor_tensor(H[0:n, t, :], H[0:n, t, :], b, ALU.add).then_inc(s["h_ready"], 1)

            dve.memset(m_all[:, 0:2, :], 0.0)
            step(dve.memset(stat[:, :], 0.0))
            dve.wait_ge(s["x_in"], 48)
            sums(1)
            dve.wait_ge(s["ada_ev"], 8)
            dve.scalar_tensor_tensor(m_rows[:, SCALE1, :], m_rows[:, SCALE1, :], 1.0, cwork[2], ALU.add, ALU.mult
                                     ).then_inc(s["m1_ready"], 1)
            dve.wait_ge(s["m1_ready"], 1)
            dve.wait_ge(s["bc_ev"], 4)
            modulate(SCALE1, SHIFT1)

            dve.wait_ge(s["qb_ev"], NB)
            def page_scores(b, chunks):
                kc = Count(s["kst"], b * CPB + chunks[0])
                for c in chunks:
                    dve.wait_ge(k_ready[c % KVS], b * 64 + 32 * (c // KVS + 1))
                    kv = KV[c % KVS]
                    q = QB[:, bass.ds(b, 1), :].to_broadcast([P, KVP, DG])
                    kc.inc(dve.tensor_tensor(kv, kv, q, ALU.mult))
                    kc.wait(dve)
                    dve.tensor_reduce(z4[:, c * KVP:(c + 1) * KVP, bass.ds(b, 1), :].rearrange("p g a h -> p g (a h)"),
                                      kv.rearrange("p g (h d) -> p g h d", h=NH), AX, ALU.add).then_inc(s["k_used"], 1)

            with dve.Fori(0, NB // 2) as b:
                page_scores(b, range(CPB))

            def both(a):
                return a.rearrange("p j (n k) -> p j n k", n=3)[:, :, bass.ds(0, 2, step=2), :]

            lat = later.rearrange("p (a b k) -> p a b k", a=1, b=1).to_broadcast([P, 2, 2, P])
            dve.wait_ge(s["small_in"], 64)
            with dve.Fori(0, NH // 2) as g:
                dve.wait_ge(s["sc_mm"], g + 1)
                for j in range(2):
                    dve.tensor_scalar(aw[0][:, j, :], ps[:, 1 + j, 0:384], SCALE, sbb[:, bass.ds(g * 2 + j, 1)],
                                      ALU.mult, ALU.add).then_inc(s["s_l"], 1)
                page_scores(g + 4, (0, 1))
                dve.wait_ge(s["s_t"], g * 3 + 3)
                dve.wait_ge(s["s_l"], g * 2 + 2)
                c = Count(s["sbs"], g)
                c.inc(dve.scalar_tensor_tensor(aw[1], aw[0], 0.0, aw[1], ALU.max, ALU.add))
                c.wait(dve)
                dve.tensor_tensor(both(aw[1]), both(aw[1]), lat, ALU.mult).then_inc(s["s_L"], 1)
                page_scores(g + 4, (2, 3))
                dve.wait_ge(s["s_mm"], g + 1)
                for j in range(2):
                    dve.tensor_tensor(aw[2][:, j, :], aw[0][:, j, :], ps[:, 3 + j, 0:384], ALU.subtract
                                      ).then_inc(s["s_a"], 1)
                page_scores(g + 4, (4, 5))
                dve.wait_ge(s["s_e"], g + 1)
                dve.tensor_tensor(both(aw[2]), both(aw[2]), lat, ALU.mult).then_inc(s["s_am"], 1)
                page_scores(g + 4, (6, 7))
                dve.wait_ge(s["o_mm"], g + 1)
                dve.tensor_copy(QKV[:, 0:2, bass.ds(QA + g * P, P)], ps[:, 5, 0:256].rearrange("p (t n) -> p t n", t=2)
                                ).then_inc(s["o_ev"], 1)

            def dilated_max(g):
                dve.wait_ge(s["sc_mm"], g + 5)
                c = Count(s["dis"], g * 3)
                for j in range(2):
                    last = dve.tensor_tensor(aw[0][:, j, :], ps[:, 1 + j, 0:384], cst("dbias"), ALU.add)
                c.inc(last)
                c.wait(dve)
                for j in range(2):
                    dve.tensor_reduce(stat[:, 24 + 2 * j:25 + 2 * j], aw[0][:, j, 0:128], AX, ALU.max)
                    last = dve.tensor_reduce(stat[:, 25 + 2 * j:26 + 2 * j], aw[0][:, j, 128:384], AX, ALU.max)
                c.inc(last)
                c.wait(dve)
                dve.tensor_scalar(stat[:, 20:24], stat[:, 24:28], -SCALE, None, ALU.mult).then_inc(s["d_zm"], 1)

            def dilated_sum(g):
                dve.wait_ge(s["d_e"], g + 1)
                for j in range(2):
                    for n, cc in enumerate((slice(0, 128), slice(128, 384))):
                        last = dve.tensor_tensor_reduce(aw[0][:, j, cc], aw[0][:, j, cc], cst("cnt")[:, cc], 1.0, 0.0,
                                                        ALU.mult, ALU.add, stat[:, 24 + 2 * j + n:25 + 2 * j + n])
                last.then_inc(s["d_p"], 1)
                dve.wait_ge(s["d_p"], g + 1)
                dve.reciprocal(stat[:, 24:28], stat[:, 24:28]).then_inc(s["dis"], 1)

            def dilated_out(g):
                dve.wait_ge(s["dis"], g * 3 + 3)
                dve.wait_ge(s["d_o"], g + 1)
                for j in range(2):
                    for t in range(2):
                        last = dve.tensor_scalar(QKV[:, t, bass.ds(QB_ + j * HD + g * P, HD)],
                                                 ps[:, 5, t * P + j * HD:t * P + (j + 1) * HD],
                                                 stat[:, 24 + 2 * j + t:25 + 2 * j + t], None, ALU.mult)
                last.then_inc(s["d_oe"], 1)

            def window_scores(g, j):
                dve.wait_ge(dk_ready[j], g * 64 + 64)
                kv = DK[j]
                kc = Count(s["dst"], g * 2 + j)
                kc.inc(dve.tensor_tensor(kv, kv, QB[:, bass.ds(g * 2 + j, 1), :].to_broadcast([P, 3, DG]), ALU.mult))
                kc.wait(dve)
                dve.tensor_reduce(zd[:, :, bass.ds(g * (2 * NH) + j * NH, NH)],
                                  kv.rearrange("p g (h d) -> p g h d", h=NH), AX, ALU.add).then_inc(s["dk_used"], 1)

            dve.wait_ge(s["k_used"], NB * CPB)
            zv = z1.rearrange("p (n h) -> p n h", h=NH)
            dve.scalar_tensor_tensor(zv, zv, SCALE, sbb[:, :].rearrange("p (a h) -> p a h", a=1).to_broadcast([P, P, NH]),
                                     ALU.mult, ALU.add).then_inc(s["z_l"], 1)
            dilated_max(0)
            dve.wait_ge(s["z_abs"], 3)
            dve.wait_ge(s["z_l"], 1)
            step(dve.scalar_tensor_tensor(zl, z1, 0.0, zt, ALU.max, ALU.add))
            step(dve.memset(zt[:, 960:1024], 0.0))
            for g in range(NPG - 2, -1, -1):
                nxt = slice((g + 1) * 64, (g + 2) * 64)
                ins = dve.tensor_tensor(zt[:, g * 64:(g + 1) * 64], zl[:, nxt], zt[:, nxt], ALU.add)
                if g:
                    step(ins)
            ins.then_inc(s["z_suf"], 1)
            dilated_sum(0)
            dve.wait_ge(s["z_s"], 1)
            dve.tensor_tensor(Z[:, 0, :].rearrange("p (a n) -> p a n", a=2), Z[:, 0, :].rearrange("p (a n) -> p a n", a=2),
                              ps[:, 3:5, :], ALU.subtract).then_inc(s["z_e"], 1)
            dilated_out(0)
            dve.wait_ge(s["qd_ev"], NB)
            for j in range(2):
                window_scores(0, j)

            def block_rows(i, j, first, mm, per, ready, used):
                dve.wait_ge(mm, i * per + per)
                if not first:
                    dve.wait_ge(used, i)
                dve.tensor_tensor(msk[:, :], ps[0:NH, 6 + j, :], cst("hmask")[0:NH, :], ALU.mult).then_inc(ready, 1)

            def page_rows(i, j, first=False):
                block_rows(i, j, first, s["v_used"], CPB, s["msk_ready"], s["oA_mm"])

            def dilated_pair(g, first=False):
                dilated_max(g)
                dilated_sum(g)
                page_rows(g * 2 - 2, 0, first)
                window_scores(g, 0)
                window_scores(g, 1)
                dilated_out(g)
                page_rows(g * 2 - 1, 1)

            dilated_pair(1, first=True)
            with dve.Fori(2, NH // 2) as g:
                dilated_pair(g)

            dve.wait_ge(s["ada_ev"], ADA_CH)
            dve.scalar_tensor_tensor(m_rows[:, SCALE2, :], m_rows[:, SCALE2, :], 1.0, nffn[:, :], ALU.add, ALU.mult
                                     ).then_inc(s["m2_ready"], 1)
            dve.wait_ge(s["dT_mm"], 1)
            step(dve.tensor_tensor(zrow[:, :], ps[0:64, 1, 0:384], cst("sbias")[0:64, :], ALU.add))
            step(dve.tensor_reduce(stat[0:64, 8:9], zrow[:, :], AX, ALU.max))
            dve.tensor_scalar(stat[0:64, 9:10], stat[0:64, 8:9], -SCALE, None, ALU.mult).then_inc(s["dm_ready"], 1)
            dve.wait_ge(s["de_ready"], 1)
            step(dve.tensor_tensor_reduce(zrow[:, :], zrow[:, :], cst("scnt")[0:64, :], 1.0, 0.0, ALU.mult, ALU.add,
                                          stat[0:64, 8:9]))
            step(dve.reciprocal(stat[0:64, 8:9], stat[0:64, 8:9]))
            dve.tensor_scalar(zrow[:, :], zrow[:, :], stat[0:64, 8:9], None, ALU.mult).then_inc(s["dp_ready"], 1)
            page_rows(NB - 2, 0)

            groups = ((0, QA), (1, QB_))

            def group_sums(t):
                n = TP[t]
                for q, col in groups:
                    o = QKV[0:n, t, col:col + DG]
                    last = dve.tensor_tensor_reduce(H[0:n, t, q * DG:(q + 1) * DG], o, o, 1.0, 0.0, ALU.mult, ALU.add,
                                                    stat[0:n, 10 + 2 * t + q:11 + 2 * t + q])
                return last

            def group_scale(t):
                n = TP[t]
                for q, col in groups:
                    last = dve.tensor_scalar(H[0:n, t, q * DG:(q + 1) * DG], QKV[0:n, t, col:col + DG],
                                             stat[0:n, 10 + 2 * t + q:11 + 2 * t + q], None, ALU.mult)
                last.then_inc(s["mg_ready"], 1)

            dve.wait_ge(s["d_oe"], NH // 2)
            group_sums(0)
            step(group_sums(1))
            dve.tensor_scalar(stat[:, 10:14], stat[:, 10:14], 1.0 / DG, EPS, ALU.mult, ALU.add).then_inc(s["ff_ready"], 1)
            page_rows(NB - 1, 1)
            dve.wait_ge(s["f_rt"], 1)
            step(dve.reciprocal(stat[:, 10:14], stat[:, 4:8]))
            group_scale(0)
            group_scale(1)

            dve.wait_ge(s["oA_mm"], NB)
            dve.tensor_copy(QKV[0:NB, 2, QA:QA + DG], ps[0:NB, 3, :])
            window_args = (s["vd_used"], 1, s["mskd_ready"], s["oB_mm"])
            block_rows(0, 0, True, *window_args)
            block_rows(1, 1, False, *window_args)
            with dve.Fori(1, NB // 2) as i:
                for j in range(2):
                    block_rows(i * 2 + j, j, False, *window_args)

            def merge_ev(n):
                dve.wait_ge(s["mg_mm"], n + 1)
                if n < 4:
                    t, half = divmod(n, 2)
                    dve.tensor_tensor(hT[:, 4 * half:4 * half + 4, t * P:(t + 1) * P],
                                      ps[:, (0, 5, 1, 2)[n], :].rearrange("p (c n) -> p c n", c=4),
                                      gcol[:, 4 * half:4 * half + 4].rearrange("p (c a) -> p c a", a=1).to_broadcast([P, 4, P]),
                                      ALU.mult).then_inc(s["mg_ev"], 1)
                else:
                    dve.tensor_tensor(hT[:, :, SEQ:NTOK], ps[:, 6, 0:64].rearrange("p (c n) -> p c n", c=KC),
                                      gcol[:, :].rearrange("p (c a) -> p c a", a=1).to_broadcast([P, KC, NB]),
                                      ALU.mult).then_inc(s["mg_ev"], 1)

            for n in range(4):
                merge_ev(n)
            dve.wait_ge(s["oB_mm"], NB)
            step(dve.tensor_copy(QKV[0:NB, 2, QB_:QB_ + DG], ps[0:NB, 4, :]))
            step(group_sums(2))
            dve.tensor_scalar(stat[0:NB, 14:16], stat[0:NB, 14:16], 1.0 / DG, EPS, ALU.mult, ALU.add).then_inc(s["ff_ready"], 1)
            dve.wait_ge(s["f_rt"], 2)
            step(dve.reciprocal(stat[0:NB, 14:16], stat[0:NB, 8:10]))
            group_scale(2)
            merge_ev(4)
            dve.wait_ge(s["kv_out"], 160)
            dve.wait_ge(s["new_out"], 32)
            dve.memset(eqz, 0.0)
            dve.memset(tw[:, 2048:2048 + P], 0.0).then_inc(s["z_v"], 1)
            dve.wait_ge(s["bc2_ev"], 2)
            for k in range(OUT_CH):
                c = slice(k * WC, (k + 1) * WC)
                dve.wait_ge(s["w_used"], ADA_CH + QKV_CH + k + 1)
                if k:
                    dve.wait_ge(s["out_ev"], k)
                g1 = m_all[:, GATE1:GATE1 + 1, c].to_broadcast([P, 2, WC])
                tmp = tw[:, 0:512].rearrange("p (t n) -> p t n", t=2)
                dve.tensor_tensor(tmp, ps[:, 2 * (k % 2), :].rearrange("p (t n) -> p t n", t=2), g1, ALU.mult)
                step(dve.tensor_tensor(tw[0:NB, 512:768], ps[0:NB, 2 * (k % 2) + 1, 0:WC], m_rows[0:NB, GATE1, c], ALU.mult))
                dve.tensor_tensor(x[:, 0:2, c], x[:, 0:2, c], tmp, ALU.add)
                dve.tensor_tensor(x[0:NB, 2, c], x[0:NB, 2, c], tw[0:NB, 512:768], ALU.add).then_inc(s["out_ev"], 1)
            dve.wait_ge(s["out_ev"], OUT_CH)
            sums(2)
            dve.wait_ge(s["bc2_ev"], 8)
            modulate(SCALE2, SHIFT2)

            def top16(tk, vals, where, row, spare):
                wait_apart(dve, tk.sem, tk.value())
                tk.inc(dve.max(vals[:, 0:8], row))
                wait_apart(dve, tk.sem, tk.value())
                dve.max_index(where[:, 0:8], vals[:, 0:8], row)
                tk.inc(dve.match_replace(spare, vals[:, 0:8], row, LOWEST))
                wait_apart(dve, tk.sem, tk.value())
                tk.inc(dve.max(vals[:, 8:16], spare))
                wait_apart(dve, tk.sem, tk.value())
                tk.inc(dve.max_index(where[:, 8:16], vals[:, 8:16], spare))

            def grid(a):
                return a.rearrange("p (k j) -> p k j", k=TOPK)

            def along(a, dim):
                if dim == 1:
                    return a.rearrange("p (k j) -> p k j", j=1).to_broadcast([P, TOPK, TOPK])
                return a.rearrange("p (k j) -> p k j", k=1).to_broadcast([P, TOPK, TOPK])

            TOPSTEPS = 22

            def choose(i, scores=UNITS):
                dve.wait_ge(s["score_ev"], scores)
                tk = Count(s["tks"], i * TOPSTEPS)
                tk.inc(dve.tensor_copy(sc, S[:, bass.ds(i, 1), :, :].rearrange("p a c n -> p (a c n)")))
                for c in range(2):
                    top16(tk, tv[c], tiu[c], sc[:, c * NKEY:(c + 1) * NKEY], rep[:, c * NKEY:(c + 1) * NKEY])
                    if c == 0:
                        yield
                tk.wait(dve)
                for c in range(2):
                    last = dve.tensor_copy(tif[c], tiu[c][:, :])
                tk.inc(dve.tensor_tensor(grid(cand), along(tv[0], 1), along(tv[1], 2), ALU.add))
                yield
                top16(tk, cv, ciu, cand, crep)
                tk.wait(dve)
                dve.tensor_scalar(ctop_d, cv, cv[:, 0:1], None, ALU.subtract).then_inc(s["topsm"], 1)
                yield
                dve.tensor_scalar(cint[:, 0, :], ciu[:, :], 4, None, ALU.logical_shift_right)
                tk.inc(dve.tensor_scalar(cint[:, 1, :], ciu[:, :], 15, None, ALU.bitwise_and))
                tk.wait(dve)
                dve.tensor_copy(row_f, cint[:, 0, :])
                tk.inc(dve.tensor_copy(col_f, cint[:, 1, :]))
                tk.wait(dve)
                for want, o in ((row_f, oh), (col_f, oh2)):
                    last = dve.tensor_tensor(grid(o), along(want, 1), along(cst("iota"), 2), ALU.is_equal)
                tk.inc(last)
                tk.wait(dve)
                for c, o in ((0, oh), (1, oh2)):
                    last = dve.tensor_tensor(grid(o), grid(o), along(tif[c], 2), ALU.mult)
                tk.inc(last)
                tk.wait(dve)
                dve.tensor_reduce(e1f, grid(oh), AX, ALU.add)
                tk.inc(dve.tensor_reduce(e2f, grid(oh2), AX, ALU.add))
                tk.wait(dve)
                tk.inc(dve.scalar_tensor_tensor(eidf, e1f, float(NKEY), e2f, ALU.mult, ALU.add))
                tk.wait(dve)
                dve.tensor_copy(idx[:, bass.ds(i, 1), :].rearrange("p a n -> p (a n)"), eidf)
                dve.wait_ge(s["tope"], i + 1)
                tk.inc(dve.tensor_reduce(tst[:, 0:1], ctop_e, AX, ALU.add))
                tk.wait(dve)
                tk.inc(dve.reciprocal(tst[:, 1:2], tst[:, 0:1]))
                tk.wait(dve)
                dve.tensor_scalar(gall[:, bass.ds(i, 1), :].rearrange("p a n -> p (a n)"), ctop_e, tst[:, 1:2], None,
                                  ALU.mult).then_inc(s["top_done"], 1)
                assert tk.n == TOPSTEPS, tk.n

            def dot_rows(i, t, rows=TOPK, beside=()):
                parts = iter(beside)
                for k in range(rows):
                    dve.wait_ge(e_ready[k % NSLOT], i * 32 + 16 * (k // NSLOT + 1))
                    u = R[:, row_slot(k), 0:D]
                    dve.tensor_tensor_reduce(u, u, H[:, t, :], 1.0, 0.0, ALU.mult, ALU.add, dots[:, k:k + 1]
                                             ).then_inc(s["dot_done"], 1)
                    if k % 4 == 3:
                        next(parts, None)

            def finish(t, bank, acc, value, gate):
                n = TP[t]
                dve.wait_ge(acc, value)
                dve.wait_ge(s["fin_in"], 16)
                a = ps[0:n, bank:bank + 2, :]
                Ht = H[0:n, t, :].rearrange("p (a n) -> p a n", a=2)
                step(dve.tensor_tensor(Ht, a, gate.rearrange("p (a n) -> p a n", a=2), ALU.mult))
                step(dve.tensor_tensor(x[0:n, t, :], x[0:n, t, :], H[0:n, t, :], ALU.add))
                step(dve.tensor_tensor_reduce(H[0:n, t, :], x[0:n, t, :], x[0:n, t, :], 1.0, 0.0, ALU.mult, ALU.add,
                                              stat[0:n, 18:19]))
                dve.tensor_scalar(stat[0:n, 16:17], stat[0:n, 18:19], 1.0 / D, EPS, ALU.mult, ALU.add
                                  ).then_inc(s["ff_ready"], 1)
                yield
                dve.wait_ge(s["f_rt"], t + 3)
                step(dve.reciprocal(stat[0:n, 19:20], stat[0:n, 17:18]))
                dve.scalar_tensor_tensor(H[0:n, t, :], x[0:n, t, :], stat[0:n, 19:20], m_all[0:n, SHIFT2, :], ALU.mult, ALU.mult
                                         ).then_inc(s["y_ready"], 1)

            def all_of(parts):
                for _ in parts:
                    pass

            for i in range(2):
                all_of(choose(i, scores=2 * i + 2))
            with dve.Fori(0, NH) as h:
                dot_rows(h, 0, beside=choose(h + 2))
            all_of(finish(0, 4, s["e_used"], NH * TOPK, m_all[:, GATE2, :]))
            with dve.Fori(0, NH - 1) as h:
                dot_rows(h + 8, 1, beside=choose(h + 10))
            dve.wait_ge(s["top_done"], UNITS)
            for half in range(2):
                p = slice(half * PAIRS, (half + 1) * PAIRS)
                last = dve.tensor_copy(idec[p, :], idx[p, UNITS - 1, half * HALF:(half + 1) * HALF])
            last.then_inc(s["idec_ready"], 1)
            dot_rows(2 * NH - 1, 1)
            dve.wait_ge(s["hr_ev"], 1)
            dot_rows(2 * NH, 2, rows=HALF, beside=finish(1, 6, s["e_used"], 2 * NH * TOPK, m_all[:, GATE2, :]))
            all_of(finish(2, 0, s["e_used"], 2 * NH * TOPK + HALF, m_rows[0:NB, GATE2, :]))


_OUTS = [("y_p", (SEQ, D), (1, SEQ, D)), ("y_s", (NB, D), (NB, 1, D)),
         ("sb_k_p", (SEQ, DG), (1, 1, SEQ, NH, HD)), ("sb_v_p", (SEQ, DG), (1, 1, SEQ, NH, HD)),
         ("dil_k_p", (SEQ, DG), (1, 1, SEQ, NH, HD)), ("dil_v_p", (SEQ, DG), (1, 1, SEQ, NH, HD)),
         ("sb_k_n", (NB, DG), (1, NB, 1, NH, HD)), ("sb_v_n", (NB, DG), (1, NB, 1, NH, HD)),
         ("dil_k_s", (NB, PAST * DG), (1, NB, PAST, NH, HD)), ("dil_v_s", (NB, PAST * DG), (1, NB, PAST, NH, HD))]


def kernel(**inputs):
    import concourse.bacc as _bacc
    from concourse.bass_utils import run_bass_kernel_spmd as _run

    a = {k: np.asarray(v) for k, v in inputs.items()}

    def chunks(w):
        return w.reshape(KC, P, -1, WC).transpose(2, 1, 0, 3).reshape(-1, P, KC * WC)

    arrays = {
        "consts": constants(),
        "c9": np.concatenate([a["c_sample"], a["c_prompt"]], 0),
        "x": np.concatenate([a["x_prompt"].reshape(SEQ, D), a["x_sample"].reshape(NB, D)], 0),
        "b_ada": a["b_ada"].reshape(ADA_CH, WC),
        "norm_mix": a["norm_mix"].reshape(1, D),
        "norm_ffn": a["norm_ffn"].reshape(1, D),
        "norm_final": a["norm_final"].reshape(1, D),
        "sb_bias": a["sb_bias"].reshape(1, NH),
        "g_out": np.concatenate([a["norm_out_sb"], a["norm_out_dil"]], -1).reshape(KC, P).T,
        "pages": a["page_table"].reshape(1, NB * NPG),
        "wts": np.concatenate([chunks(w) for w in (a["w_ada"][0][:, :2 * D], a["w_in"][0], a["w_ada"][0][:, 2 * D:],
                                                   a["w_out"][0], a["w_peer_q"][0])], 0),
        "subk": a["peer_sub_keys"].reshape(16, NKEY, P).transpose(2, 0, 1).reshape(P, 16 * NKEY),
        "sb_k": a["cache_sb_k"].reshape(-1, P, DG),
        "sb_v": a["cache_sb_v"].reshape(-1, P, DG),
        "dil_k": a["cache_dil_k"].reshape(NB, PAST * DG),
        "dil_v": a["cache_dil_v"].reshape(NB, PAST * DG),
        "uv": np.concatenate([a["peer_u"][0], a["peer_v"][0]], -1),
    }
    arrays = {k: np.ascontiguousarray(v) for k, v in arrays.items()}
    nc = _bacc.Bacc("TRN2", target_bir_lowering=False, num_devices=1)
    A = {k: nc.dram_tensor("in_" + k, v.shape, mybir.dt.from_np(v.dtype), kind="ExternalInput").ap()
         for k, v in arrays.items()}
    for name, shape, _ in _OUTS:
        A[name] = nc.dram_tensor("out_" + name, shape, F32, kind="ExternalOutput").ap()
    build(nc, A)
    r = _run(nc, [{"in_" + k: v for k, v in arrays.items()}], core_ids=[0])
    return tuple(r.results[0]["out_" + name].reshape(final) for name, _, final in _OUTS)
```
